# Optimizing a Trainium2 kernel written in Bass

```python
import math
import jax, jax.numpy as jnp
from jax import lax
import numpy as np

D_MODEL = 2048
BATCH = 1
SEQ = 512
DEPTH = 1

SSD_WIDTH = 1024
SSD_HEADDIM = 64
SSD_HEADS = SSD_WIDTH // SSD_HEADDIM
SSD_STATE = 128
SSD_GROUPS = 2
CONV_WIDTH = 4
CHUNK = 128
CONV_DIM = SSD_WIDTH + 2 * SSD_GROUPS * SSD_STATE
ATT_HEADS = 8
ATT_HEADDIM = 128
ATT_WIDTH = ATT_HEADS * ATT_HEADDIM
IDX_HEADS = 16
IDX_DIM = 64
TOPK_MAX = 256
Q_BLOCK = 128
D_MIX = SSD_WIDTH + ATT_WIDTH
D_IN = SSD_WIDTH + CONV_DIM + SSD_HEADS + 3 * ATT_WIDTH + IDX_HEADS * IDX_DIM + IDX_DIM + IDX_HEADS
N_EXPERTS = 32
N_EXPERT_GROUPS = 8
EXPERTS_PER_GROUP = N_EXPERTS // N_EXPERT_GROUPS
TOP_K = 2
D_FF = 512
DISPATCH_BLOCK = 128
PLE_DIM = 256
ALPHA = (2.0 * DEPTH) ** 0.25
BETA = (8.0 * DEPTH) ** -0.25
LN_EPS = 1e-5

kernel_name = 'hybrid_ssd_dsa_grouped_moe_deepnorm'

def _proj_splits():
    widths = [SSD_WIDTH, CONV_DIM, SSD_HEADS, ATT_WIDTH, ATT_WIDTH, ATT_WIDTH,
              IDX_HEADS * IDX_DIM, IDX_DIM, IDX_HEADS]
    return [int(v) for v in np.cumsum(widths)[:-1]]

def layer_norm(x, g, b):
    xf = x.astype(jnp.float32)
    mu = jnp.mean(xf, -1, keepdims=True)
    var = jnp.mean(jnp.square(xf - mu), -1, keepdims=True)
    return ((xf - mu) * lax.rsqrt(var + LN_EPS) * g.astype(jnp.float32) + b.astype(jnp.float32)).astype(x.dtype)

def rms_norm(x, g):
    xf = x.astype(jnp.float32)
    ms = jnp.mean(jnp.square(xf), -1, keepdims=True)
    return (xf * lax.rsqrt(ms + LN_EPS) * g.astype(jnp.float32)).astype(x.dtype)

def causal_depthwise_conv(u, w, b):
    out = lax.conv_general_dilated(u, w[:, None, :], window_strides=(1,),
                                   padding=[(CONV_WIDTH - 1, 0)],
                                   dimension_numbers=('NWC', 'WIO', 'NWC'),
                                   feature_group_count=u.shape[-1])
    return out + b

def ssd_chunked(xh, dt, a, bmat, cmat):
    bsz, seq, nh, hd = xh.shape
    nc = seq // CHUNK
    hpg = nh // SSD_GROUPS
    xdt = (xh * dt[..., None]).reshape(bsz, nc, CHUNK, nh, hd)
    a_cs = jnp.cumsum((dt * a).reshape(bsz, nc, CHUNK, nh), axis=2)
    bc = bmat.reshape(bsz, nc, CHUNK, SSD_GROUPS, SSD_STATE)
    cc = cmat.reshape(bsz, nc, CHUNK, SSD_GROUPS, SSD_STATE)
    causal = jnp.tril(jnp.ones((CHUNK, CHUNK), dtype=bool))
    seg = a_cs[:, :, :, None, :] - a_cs[:, :, None, :, :]
    decay = jnp.exp(jnp.where(causal[None, None, :, :, None], seg, -jnp.inf))
    cb = jnp.repeat(jnp.einsum('bclgn,bcsgn->bclsg', cc, bc), hpg, axis=-1)
    y_diag = jnp.einsum('bclsh,bcshp->bclhp', cb * decay, xdt)
    bh = jnp.repeat(bc, hpg, axis=3)
    ch = jnp.repeat(cc, hpg, axis=3)
    decay_to_end = jnp.exp(a_cs[:, :, -1:, :] - a_cs)
    states = jnp.einsum('bclhn,bclh,bclhp->bchpn', bh, decay_to_end, xdt)
    chunk_decay = jnp.exp(a_cs[:, :, -1, :])

    def step(carry, inp):
        st, dec = inp
        return carry * dec[..., None, None] + st, carry

    init = jnp.zeros((bsz, nh, hd, SSD_STATE), xdt.dtype)
    _, prev = lax.scan(step, init, (jnp.moveaxis(states, 1, 0), jnp.moveaxis(chunk_decay, 1, 0)))
    prev = jnp.moveaxis(prev, 0, 1)
    y_off = jnp.einsum('bclhn,bchpn,bclh->bclhp', ch, prev, jnp.exp(a_cs))
    return (y_diag + y_off).reshape(bsz, seq, nh, hd)

def dsa_attention(q, k, v, iq, ik, iw):
    bsz, seq = q.shape[0], q.shape[1]
    topk = min(TOPK_MAX, seq // 4)
    nb = seq // Q_BLOCK
    key_pos = jnp.arange(seq)
    scale = ATT_HEADDIM ** -0.5
    ikf = ik.astype(jnp.float32)

    def block(i):
        start = i * Q_BLOCK
        qb = lax.dynamic_slice_in_dim(q, start, Q_BLOCK, axis=1)
        iqb = lax.dynamic_slice_in_dim(iq, start, Q_BLOCK, axis=1).astype(jnp.float32)
        iwb = lax.dynamic_slice_in_dim(iw, start, Q_BLOCK, axis=1).astype(jnp.float32)
        q_pos = start + jnp.arange(Q_BLOCK)
        dots = jnp.einsum('bqhd,bsd->bqhs', iqb, ikf) * (IDX_DIM ** -0.5)
        score = jnp.einsum('bqh,bqhs->bqs', iwb * (IDX_HEADS ** -0.5), jax.nn.relu(dots))
        visible = key_pos[None, :] <= q_pos[:, None]
        score = jnp.where(visible[None], score, -jnp.inf)
        _, sel = lax.top_k(score, topk)
        sel_valid = sel <= q_pos[None, :, None]
        kg = jax.vmap(lambda kk, ii: kk[ii])(k, sel)
        vg = jax.vmap(lambda vv, ii: vv[ii])(v, sel)
        logits = jnp.einsum('bqhd,bqkhd->bqhk', qb, kg).astype(jnp.float32) * scale
        logits = jnp.where(sel_valid[:, :, None, :], logits, -jnp.inf)
        prob = jax.nn.softmax(logits, axis=-1).astype(v.dtype)
        return jnp.einsum('bqhk,bqkhd->bqhd', prob, vg)

    outs = lax.map(block, jnp.arange(nb))
    return jnp.moveaxis(outs, 0, 1).reshape(bsz, seq, ATT_HEADS * ATT_HEADDIM)

def hybrid_mixer(h, w_in, conv_w, conv_b, dt_bias, a_log, d_skip, ssm_norm_w,
                 idx_k_norm_g, idx_k_norm_b, w_out):
    bsz, seq, _ = h.shape
    proj = h @ w_in
    z, xbc, dt_raw, q, k, v, iq, ik, iw = jnp.split(proj, _proj_splits(), axis=-1)
    xbc = jax.nn.silu(causal_depthwise_conv(xbc, conv_w, conv_b))
    xs, bm, cm = jnp.split(xbc, [SSD_WIDTH, SSD_WIDTH + SSD_GROUPS * SSD_STATE], axis=-1)
    xh = xs.reshape(bsz, seq, SSD_HEADS, SSD_HEADDIM).astype(jnp.float32)
    bm = bm.reshape(bsz, seq, SSD_GROUPS, SSD_STATE).astype(jnp.float32)
    cm = cm.reshape(bsz, seq, SSD_GROUPS, SSD_STATE).astype(jnp.float32)
    dt = jax.nn.softplus(dt_raw.astype(jnp.float32) + dt_bias.astype(jnp.float32))
    a = -jnp.exp(a_log.astype(jnp.float32))
    y = ssd_chunked(xh, dt, a, bm, cm) + xh * d_skip.astype(jnp.float32)[:, None]
    y = y.reshape(bsz, seq, SSD_WIDTH).astype(h.dtype)
    y_ssd = rms_norm(y * jax.nn.silu(z), ssm_norm_w)
    q = q.reshape(bsz, seq, ATT_HEADS, ATT_HEADDIM)
    k = k.reshape(bsz, seq, ATT_HEADS, ATT_HEADDIM)
    v = v.reshape(bsz, seq, ATT_HEADS, ATT_HEADDIM)
    iq = iq.reshape(bsz, seq, IDX_HEADS, IDX_DIM)
    ik = layer_norm(ik, idx_k_norm_g, idx_k_norm_b)
    y_att = dsa_attention(q, k, v, iq, ik, iw)
    return jnp.concatenate([y_ssd, y_att.astype(h.dtype)], axis=-1) @ w_out

def grouped_moe(h, router_w, router_b, w_gate, w_up, w_down):
    bsz, seq, d = h.shape
    t = bsz * seq
    hf = h.reshape(t, d)
    affinity = jax.nn.sigmoid((hf @ router_w).astype(jnp.float32))
    biased = affinity + router_b.astype(jnp.float32)
    grp = biased.reshape(t, N_EXPERT_GROUPS, EXPERTS_PER_GROUP)
    grp_score = jnp.sum(lax.top_k(grp, 2)[0], axis=-1)
    best_group = jnp.argmax(grp_score, axis=-1)
    in_group = (jnp.arange(N_EXPERTS) // EXPERTS_PER_GROUP)[None, :] == best_group[:, None]
    _, expert_idx = lax.top_k(jnp.where(in_group, biased, -jnp.inf), TOP_K)
    gate = jnp.take_along_axis(affinity, expert_idx, axis=-1)
    gate = gate / jnp.sum(gate, axis=-1, keepdims=True)
    n_assign = t * TOP_K
    flat_e = expert_idx.reshape(n_assign)
    flat_tok = jnp.repeat(jnp.arange(t, dtype=jnp.int32), TOP_K)
    order = jnp.argsort(flat_e)
    sorted_e = flat_e[order]
    counts = jnp.bincount(flat_e, length=N_EXPERTS)
    padded = (counts + DISPATCH_BLOCK - 1) // DISPATCH_BLOCK * DISPATCH_BLOCK
    pad_end = jnp.cumsum(padded)
    pad_start = pad_end - padded
    start = jnp.cumsum(counts) - counts
    dest_sorted = pad_start[sorted_e] + (jnp.arange(n_assign) - start[sorted_e])
    cap = -(-n_assign // DISPATCH_BLOCK) * DISPATCH_BLOCK + N_EXPERTS * DISPATCH_BLOCK
    n_blocks = cap // DISPATCH_BLOCK
    slot_tok = jnp.full((cap,), t, dtype=jnp.int32).at[dest_sorted].set(flat_tok[order])
    block_expert = jnp.minimum(
        jnp.searchsorted(pad_end, jnp.arange(n_blocks) * DISPATCH_BLOCK, side='right'), N_EXPERTS - 1)
    hpad = jnp.concatenate([hf, jnp.zeros((1, d), hf.dtype)], axis=0)
    xb = hpad[slot_tok].reshape(n_blocks, DISPATCH_BLOCK, d)

    def run(args):
        xblk, e = args
        return (jax.nn.silu(xblk @ w_gate[e]) * (xblk @ w_up[e])) @ w_down[e]

    yb = lax.map(run, (xb, block_expert)).reshape(cap, d)
    dest = jnp.zeros((n_assign,), dtype=dest_sorted.dtype).at[order].set(dest_sorted)
    y = yb[dest].reshape(t, TOP_K, d)
    return jnp.einsum('tk,tkd->td', gate.astype(y.dtype), y).reshape(bsz, seq, d)

def setup_inputs(seed: int = 0) -> dict:
    key = jax.random.key(seed)
    ks = jax.random.split(key, 24)
    f32 = jnp.float32

    def nrm(k, shape, scale):
        return jax.random.normal(k, shape, f32) * scale

    dt0 = jnp.exp(jax.random.uniform(ks[5], (DEPTH, SSD_HEADS), f32, math.log(1e-3), math.log(1e-1)))
    return {
        'x': nrm(ks[0], (BATCH, SEQ, D_MODEL), 1.0),
        'p': nrm(ks[1], (DEPTH, BATCH, SEQ, PLE_DIM), 1.0),
        'w_in': nrm(ks[2], (DEPTH, D_MODEL, D_IN), D_MODEL ** -0.5),
        'conv_w': nrm(ks[3], (DEPTH, CONV_WIDTH, CONV_DIM), CONV_WIDTH ** -0.5),
        'conv_b': nrm(ks[4], (DEPTH, CONV_DIM), 0.02),
        'dt_bias': dt0 + jnp.log(-jnp.expm1(-dt0)),
        'a_log': jnp.log(jax.random.uniform(ks[6], (DEPTH, SSD_HEADS), f32, 1.0, 16.0)),
        'd_skip': 1.0 + nrm(ks[7], (DEPTH, SSD_HEADS), 0.1),
        'ssm_norm_w': 1.0 + nrm(ks[8], (DEPTH, SSD_WIDTH), 0.1),
        'idx_k_norm_g': 1.0 + nrm(ks[9], (DEPTH, IDX_DIM), 0.1),
        'idx_k_norm_b': nrm(ks[10], (DEPTH, IDX_DIM), 0.02),
        'w_out': nrm(ks[11], (DEPTH, D_MIX, D_MODEL), BETA * D_MIX ** -0.5),
        'ln1_g': 1.0 + nrm(ks[12], (DEPTH, D_MODEL), 0.05),
        'ln1_b': nrm(ks[13], (DEPTH, D_MODEL), 0.02),
        'router_w': nrm(ks[14], (D_MODEL, N_EXPERTS), D_MODEL ** -0.5),
        'router_b': nrm(ks[15], (N_EXPERTS,), 0.01),
        'w_gate': nrm(ks[16], (DEPTH, N_EXPERTS, D_MODEL, D_FF), D_MODEL ** -0.5),
        'w_up': nrm(ks[17], (DEPTH, N_EXPERTS, D_MODEL, D_FF), D_MODEL ** -0.5),
        'w_down': nrm(ks[18], (DEPTH, N_EXPERTS, D_FF, D_MODEL), BETA * D_FF ** -0.5),
        'ple_w': nrm(ks[19], (DEPTH, PLE_DIM, D_MODEL), BETA * PLE_DIM ** -0.5),
        'ple_gate_w': nrm(ks[20], (DEPTH, D_MODEL, D_MODEL), D_MODEL ** -0.5),
        'ln2_g': 1.0 + nrm(ks[21], (DEPTH, D_MODEL), 0.05),
        'ln2_b': nrm(ks[22], (DEPTH, D_MODEL), 0.02),
    }

def reference(x, p, w_in, conv_w, conv_b, dt_bias, a_log, d_skip, ssm_norm_w,
              idx_k_norm_g, idx_k_norm_b, w_out, ln1_g, ln1_b, router_w, router_b,
              w_gate, w_up, w_down, ple_w, ple_gate_w, ln2_g, ln2_b):
    h = x
    for i in range(DEPTH):
        mix = hybrid_mixer(h, w_in[i], conv_w[i], conv_b[i], dt_bias[i], a_log[i], d_skip[i],
                           ssm_norm_w[i], idx_k_norm_g[i], idx_k_norm_b[i], w_out[i])
        h = layer_norm(ALPHA * h + mix, ln1_g[i], ln1_b[i])
        ffn = grouped_moe(h, router_w, router_b, w_gate[i], w_up[i], w_down[i])
        ple = jax.nn.sigmoid(h @ ple_gate_w[i]) * (p[i] @ ple_w[i])
        h = layer_norm(ALPHA * h + ffn + ple, ln2_g[i], ln2_b[i])
    return h


_drawn_inputs = setup_inputs


def setup_inputs(seed=0):
    import zlib

    import numpy as np

    out = dict(_drawn_inputs(seed))
    spreads = {}
    factors = {'idx_k_norm_b': 11.687, 'ln2_b': 2.832}
    for name, (base, spread) in spreads.items():
        noise = np.random.default_rng([zlib.crc32(name.encode()), seed]).standard_normal(out[name].shape)
        drawn = base * np.exp(spread * noise) if base else spread * noise
        out[name] = __import__('jax').numpy.asarray(drawn.astype(out[name].dtype))
    for name, factor in factors.items():
        out[name] = (out[name] * factor).astype(out[name].dtype)
    return out
```

```python
import concourse.bass as bass
from concourse import mybir
from contextlib import ExitStack

FP32 = mybir.dt.float32
FP32R = mybir.dt.float32r
I32 = mybir.dt.int32
U32 = mybir.dt.uint32
ALU = mybir.AluOpType
ACT = mybir.ActivationFunctionType
AX = mybir.AxisListType


class Shared:
    pass


P = 128
SEQ, D = 512, 2048
TT = SEQ // P
DK = D // P
SSD_W, HD, HEADS, STATE, GROUPS = 1024, 64, 16, 128, 2
HPG = HEADS // GROUPS
CONV_TAPS = 4
CONV_DIM = SSD_W + 2 * GROUPS * STATE
AH, AD = 8, 128
IH, ID = 16, 64
TOPK = min(256, SEQ // 4)
N_EXP, N_GRP, PER_GRP = 32, 8, 4
D_FF = 512
PLE = 256
ALPHA = 2.0 ** 0.25
EPS = 1e-5

COL_Z = 0
COL_XBC = SSD_W
COL_DT = COL_XBC + CONV_DIM
COL_Q = COL_DT + HEADS
COL_V = COL_Q + 2 * AH * AD
COL_IQ = COL_V + AH * AD
COL_IK = COL_IQ + IH * ID
COL_IW = COL_IK + ID
SMALL = ID + IH + HEADS

PW = 512
CH = 4
KC = DK // CH
SPLIT_SLOTS = 2
NEG = -1.0e30
TAKEN = -3.0e38

IQ_PANELS, QK_PANELS, V_PANELS, ZX_PANELS = 2, 4, 2, 5
HEADS_PER_PANEL = 2
UNITS = HEADS_PER_PANEL * TT
SLOTS = UNITS + 2


def run_constants(nc, k):
    filled, shaped = (k.semaphore(n) for n in ("filled", "shaped"))
    with nc.Block() as block:
        @block.gpsimd
        def _(pool):
            pool.memset(k.ones[:], 1.0).then_inc(filled, 1)
            pool.memset(k.ident[:], 0.0).then_inc(filled, 1)
            pool.memset(k.strict[:], 1.0).then_inc(filled, 1)
            pool.memset(k.causal_bias[:], 0.0).then_inc(filled, 1)
            pool.wait_ge(filled, 4)
            pool.affine_select(out=k.ident[:], in_=k.ident[:], compare_op=ALU.not_equal, fill=1.0, base=0,
                               pattern=[[-1, P]], channel_multiplier=1).then_inc(shaped, 1)
            pool.affine_select(out=k.upto[:], in_=k.ones[:], compare_op=ALU.is_ge, fill=0.0, base=0,
                               pattern=[[1, P]], channel_multiplier=-1).then_inc(shaped, 1)
            pool.affine_select(out=k.strict[:], in_=k.strict[:], compare_op=ALU.is_gt, fill=0.0, base=0,
                               pattern=[[1, P]], channel_multiplier=-1).then_inc(shaped, 1)
            own = k.causal_bias[:, SEQ - P:SEQ]
            pool.affine_select(out=own, in_=own, compare_op=ALU.is_ge, fill=NEG, base=0,
                               pattern=[[-1, P]], channel_multiplier=1).then_inc(shaped, 1)
            pool.wait_ge(shaped, 4)


def run_projection(nc, k, x, w_in, idx_g, idx_b, scr):
    w = w_in[0]
    with ExitStack() as ctx:
        def sb(name, shape, dt=FP32):
            return ctx.enter_context(nc.sbuf_tensor(name, shape, dt))

        def sem(name):
            return k.semaphore(name)

        banks = [ctx.enter_context(nc.psum_tensor(f"bank{i}", [P, PW], FP32)) for i in range(8)]
        acc, side = banks[0:4], banks[4:8]
        xhi, xlo = sb("xhi", [P, DK, SEQ], FP32R), sb("xlo", [P, DK, SEQ], FP32R)
        raw = sb("raw", [P, CH, KC, PW])
        whi = [sb(f"whi{i}", [P, KC, PW], FP32R) for i in range(SPLIT_SLOTS)]
        wlo = [sb(f"wlo{i}", [P, KC, PW], FP32R) for i in range(SPLIT_SLOTS)]
        stage = sb("stage", [P, TT, PW])
        union = sb("union", [P, 2 * D])
        xin = union[:, 0:2 * D].rearrange("p (b n) -> p b n", b=2)
        iq = union[:, 0:IH // 2 * SEQ].rearrange("p (h n) -> p h n", h=IH // 2)
        o = HEADS_PER_PANEL * SEQ
        qh = union[:, 0:o].rearrange("p (h n) -> p h n", h=HEADS_PER_PANEL)
        kh = union[:, o:2 * o].rearrange("p (h n) -> p h n", h=HEADS_PER_PANEL)
        vh = union[:, 2 * o:3 * o].rearrange("p (s n) -> p s n", s=TT)
        oh = union[:, 3 * o:4 * o].rearrange("p (h n) -> p h n", h=HEADS_PER_PANEL)
        wsm_raw = sb("wsm_raw", [P, DK, SMALL])
        wsm_hi, wsm_lo = sb("wsm_hi", [P, DK, SMALL], FP32R), sb("wsm_lo", [P, DK, SMALL], FP32R)
        small = sb("small", [P, TT, SMALL])
        iws = sb("iws", [P, TT, IH])
        stats = sb("stats", [P, TT, 6])
        mv = sb("mv", [P, TT, 2])
        rstd = sb("rstd", [P, TT])
        ikn = sb("ikn", [P, TT, 2 * ID])
        gb = sb("gb", [P, 2])
        ikT = sb("ikT", [P, SEQ])
        relu = sb("relu", [P, 2, SEQ])
        score = [sb(f"score{q}", [P, P * (q + 1)]) for q in range(TT)]
        top8 = sb("top8", [P, 8])
        probs = sb("probs", [P, 2, SEQ])
        probsT = sb("probsT", [P, 2, SEQ])
        nmax = sb("nmax", [P, 2, 2])
        rowsum = sb("rowsum", [P, 2])

        x_here = [sem("x_here0"), sem("x_here1")]
        x_turned, x_hi, x_lo = sem("x_turned"), sem("x_hi"), sem("x_lo")
        small_here, small_hi, small_lo, small_acc = sem("small_here"), sem("small_hi"), sem("small_lo"), sem("small_acc")
        small_out, ikn_done, ik_turned, ik_ready = sem("small_out"), sem("ikn_done"), sem("ik_turned"), sem("ik_ready")
        raw_here = [sem(f"raw_here{c}") for c in range(CH)]
        hi_ready, split_ready, split_used = sem("hi_ready"), sem("split_ready"), sem("split_used")
        acc_ready, acc_taken = sem("acc_ready"), sem("acc_taken")
        stored = [sem(f"stored{t}") for t in range(TT)]
        iq_here, dots_ready, relu_ready, score_step = sem("iq_here"), sem("dots_ready"), sem("relu_ready"), sem("score_step")
        heads_here, heads_used = sem("heads_here"), sem("heads_used")
        logits_ready, logits_masked, max_ready = sem("logits_ready"), sem("logits_masked"), sem("max_ready")
        exp_ready, probs_ready, probs_turned = sem("exp_ready"), sem("probs_ready"), sem("probs_turned")
        probsT_ready, pv_ready, pv_taken, att_stored = sem("probsT_ready"), sem("pv_ready"), sem("pv_taken"), sem("att_stored")
        sum_inverted = sem("sum_inverted")
        passed_dve, passed_pool = sem("passed_dve"), sem("passed_pool")
        dve_step = sem("dve_step")

        RAW_FREE, ACC_FREE = CH, TT
        QK, IQ, V = (0, QK_PANELS), (QK_PANELS, IQ_PANELS), (QK_PANELS + IQ_PANELS, V_PANELS)
        ZX = (QK_PANELS + IQ_PANELS + V_PANELS, ZX_PANELS)
        LAST = ZX[0] + ZX[1] - 1
        N_SMALL_X = TT * (DK // 4)

        def width(q):
            return P * (q + 1)

        with nc.Block() as block:
            @block.sync
            def _(sp):
                for t in range(TT):
                    if t >= 2:
                        sp.wait_ge(x_lo, (t - 1) * (DK // 4))
                    sp.dma_start(xin[:, t % 2, :], x[0, t * P:(t + 1) * P, :]).then_inc(x_here[t % 2], 16)
                    if t == 1:
                        rows = w.rearrange("(k p) n -> p k n", p=P)
                        sp.dma_start(wsm_raw[:, :, 0:ID + IH], rows[:, :, COL_IK:COL_IK + ID + IH]).then_inc(small_here, 16)
                        sp.dma_start(wsm_raw[:, :, ID + IH:SMALL], rows[:, :, COL_DT:COL_DT + HEADS]).then_inc(small_here, 16)
                        for half in range(2):
                            sp.dma_start(gb[half * ID:(half + 1) * ID, 0:1], idx_g[0].rearrange("(n a) -> n a", a=1)).then_inc(small_here, 16)
                            sp.dma_start(gb[half * ID:(half + 1) * ID, 1:2], idx_b[0].rearrange("(n a) -> n a", a=1)).then_inc(small_here, 16)

                def panel(p, col):
                    for c in range(CH):
                        sp.wait_ge(split_ready, 4 * p + c + 1)
                        src = w[c * KC * P:(c + 1) * KC * P, :].rearrange("(k p) n -> p k n", p=P)
                        sp.dma_start(raw[:, c], src[:, :, bass.ds(col, PW)]).then_inc(raw_here[c], 16)

                with sp.Fori(0, QK[1]) as i:
                    panel(QK[0] + i, COL_Q + i * PW)
                with sp.Fori(0, IQ[1]) as i:
                    panel(IQ[0] + i, COL_IQ + i * PW)
                with sp.Fori(0, V[1]) as i:
                    panel(V[0] + i, COL_V + i * PW)
                with sp.Fori(0, ZX[1]) as i:
                    panel(ZX[0] + i, COL_Z + i * PW)

            @block.tensor
            def _(pe):
                pe.sem_inc(acc_ready, ACC_FREE)
                pe.sem_inc(probs_turned, 2)
                pe.sem_inc(pv_ready, 2)
                for u in range(N_SMALL_X):
                    t, g = u // (DK // 4), u % (DK // 4)
                    if g == 0:
                        pe.wait_ge(x_here[t % 2], 16 * (t // 2 + 1))
                    if u >= 8:
                        pe.wait_ge(x_lo, u - 7)
                    for j in range(4):
                        last = pe.transpose(banks[u % 8][:, j * P:(j + 1) * P],
                                            xin[:, t % 2, (4 * g + j) * P:(4 * g + j + 1) * P], k.ident[:])
                    last.then_inc(x_turned, 1)
                pe.wait_ge(x_lo, N_SMALL_X)
                pe.wait_ge(small_lo, 1)
                for t in range(TT):
                    for kt in range(DK):
                        for n, (a, b) in enumerate(((xhi, wsm_hi), (xhi, wsm_lo), (xlo, wsm_hi))):
                            last = pe.matmul(side[0][:, t * SMALL:(t + 1) * SMALL], a[:, kt, t * P:(t + 1) * P], b[:, kt, :],
                                             start=(kt == 0 and n == 0), stop=(kt == DK - 1 and n == 2))
                last.then_inc(small_acc, 1)

                def steps(p, turned, between=None):
                    for c in range(CH):
                        s = c % SPLIT_SLOTS
                        pe.wait_ge(split_ready, RAW_FREE + 4 * p + c + 1)
                        for t in range(TT):
                            if c == 0:
                                pe.wait_ge(acc_taken, 4 * p + t + 1)
                            cut = slice(t * P, (t + 1) * P)
                            for kk in range(KC):
                                kt = c * KC + kk
                                for n, (a, b) in enumerate(((xhi, whi[s]), (xhi, wlo[s]), (xlo, whi[s]))):
                                    first, final = c == 0 and kk == 0 and n == 0, c == CH - 1 and kk == KC - 1 and n == 2
                                    if turned:
                                        last = pe.matmul(acc[t][:], b[:, kk, cut], a[:, kt, :], start=first, stop=final)
                                    else:
                                        last = pe.matmul(acc[t][:], a[:, kt, cut], b[:, kk, :], start=first, stop=final)
                            if c == CH - 1:
                                last.then_inc(acc_ready, 1)
                            elif t == TT - 1:
                                last.then_inc(split_used, 1)
                            if between is not None and 4 * c + t < SLOTS:
                                between(4 * c + t)

                with pe.Fori(0, QK[1]) as i:
                    steps(QK[0] + i, True)

                pe.wait_ge(ikn_done, 1)
                for t in range(TT):
                    last = pe.transpose(side[1][:, t * P:(t + 1) * P], ikn[:, t, :], k.ident[:])
                last.then_inc(ik_turned, 1)

                with pe.Fori(0, IQ[1]) as i:
                    steps(IQ[0] + i, True)

                pe.wait_ge(iq_here, 16)
                pe.wait_ge(ik_ready, 1)
                for q in range(TT):
                    for h in range(IH):
                        u = q * IH + h
                        if u >= 4:
                            pe.wait_ge(relu_ready, u - 3)
                        half = slice(ID * (h % 2), ID * (h % 2) + ID)
                        pe.matmul(side[u % 4][:, 0:width(q)], iq[half, h // 2, q * P:(q + 1) * P], ikT[half, 0:width(q)],
                                  start=True, stop=True).then_inc(dots_ready, 1)

                with pe.Fori(0, V[1]) as i:
                    steps(V[0] + i, False)

                pe.wait_ge(relu_ready, TT * IH)

                def attend(it):
                    first_unit = UNITS * it

                    def between(j):
                        if j < UNITS:
                            hh, q = j // TT, j % TT
                            if j == 0:
                                pe.wait_ge(heads_here, 48 * (it + 1))
                            pe.wait_ge(logits_masked, first_unit + j + 1)
                            pe.matmul(side[j % 2][:, 0:width(q)], qh[:, hh, q * P:(q + 1) * P], kh[:, hh, 0:width(q)],
                                      start=True, stop=True).then_inc(logits_ready, 1)
                        if 1 <= j <= UNITS:
                            v, q = j - 1, (j - 1) % TT
                            pe.wait_ge(probs_ready, first_unit + v + 1)
                            pe.wait_ge(probsT_ready, first_unit + v + 1)
                            for s in range(q + 1):
                                last = pe.transpose(side[2][:, s * P:(s + 1) * P], probs[:, v % 2, s * P:(s + 1) * P], k.ident[:])
                            last.then_inc(probs_turned, 1)
                        if 2 <= j:
                            v, hh, q = j - 2, (j - 2) // TT, (j - 2) % TT
                            pe.wait_ge(probsT_ready, 1 + first_unit + v + 1)
                            pe.wait_ge(pv_taken, first_unit + v + 1)
                            for s in range(q + 1):
                                last = pe.matmul(side[3][:, 0:P], vh[:, s, hh * P:(hh + 1) * P], probsT[:, v % 2, s * P:(s + 1) * P],
                                                 start=(s == 0), stop=(s == q))
                            last.then_inc(pv_ready, 1)
                    return between

                with pe.Fori(0, ZX[1] - 1) as i:
                    steps(ZX[0] + i, True, attend(i))
                steps(LAST, True)

            @block.scalar
            def _(act):
                for u in range(N_SMALL_X):
                    t, g = u // (DK // 4), u % (DK // 4)
                    act.wait_ge(x_turned, u + 1)
                    act.activation(xhi[:, 4 * g:4 * g + 4, t * P:(t + 1) * P],
                                   banks[u % 8][:, :].rearrange("p (j n) -> p j n", j=4), ACT.Copy).then_inc(x_hi, 1)
                act.wait_ge(small_here, 16 * 6)
                act.activation(wsm_hi[:], wsm_raw[:], ACT.Copy).then_inc(small_hi, 1)

                def high(c, p):
                    act.wait_ge(raw_here[c], 16 * (p + 1))
                    act.activation(whi[c % SPLIT_SLOTS][:], raw[:, c], ACT.Copy).then_inc(hi_ready, 1)

                def high_next(c, p, more=True):
                    if c == 1:
                        act.wait_ge(acc_ready, 4 * p + TT)
                        high(1, p)
                    elif c in (2, 3):
                        act.wait_ge(split_used, 3 * p + c - 1)
                        high(c, p)
                    elif more:
                        act.wait_ge(split_used, 3 * p + 3)
                        high(0, p + 1)

                def evacuate(p):
                    for t in range(TT):
                        act.wait_ge(acc_ready, ACC_FREE + 4 * p + t + 1)
                        act.wait_ge(stored[t], 16 * (p + 1))
                        act.activation(stage[:, t, :], acc[t][:], ACT.Copy).then_inc(acc_taken, 1)

                def body(p, more=True):
                    for c in (1, 2, 3, 0):
                        high_next(c, p, more)
                    evacuate(p)

                high(0, 0)
                act.wait_ge(small_acc, 1)
                act.activation(small[:], side[0][:, 0:TT * SMALL].rearrange("p (t n) -> p t n", t=TT), ACT.Copy).then_inc(small_out, 1)
                act.wait_ge(dve_step, TT + 2)
                act.activation(rstd[:], rstd[:], ACT.Sqrt).then_inc(small_out, 1)
                with act.Fori(0, QK[1]) as i:
                    body(QK[0] + i)
                act.wait_ge(ik_turned, 1)
                act.activation(ikT[:], side[1][:], ACT.Identity, bias=gb[:, 1:2], scale=gb[:, 0:1]).then_inc(ik_ready, 1)
                with act.Fori(0, IQ[1]) as i:
                    body(IQ[0] + i)
                for u in range(TT * IH):
                    q = u // IH
                    act.wait_ge(dots_ready, u + 1)
                    if u >= 2:
                        act.wait_ge(score_step, u - 1)
                    act.activation(relu[:, u % 2, 0:width(q)], side[u % 4][:, 0:width(q)], ACT.Relu).then_inc(relu_ready, 1)
                with act.Fori(0, V[1]) as i:
                    body(V[0] + i)

                def attention_body(it, p):
                    first_unit = UNITS * it
                    for j in range(SLOTS):
                        if j in (0, 4, 8):
                            high_next(j // 4 + 1, p)
                        if j < UNITS:
                            act.wait_ge(max_ready, first_unit + j + 1)
                            act.activation(probs[:, j % 2, 0:width(j % TT)], probs[:, j % 2, 0:width(j % TT)], ACT.Exp,
                                           bias=nmax[:, j % 2, 1:2], scale=AD ** -0.5,
                                           accum_out=rowsum[:, j % 2:j % 2 + 1]).then_inc(exp_ready, 1)
                        if j >= 2:
                            v = j - 2
                            act.wait_ge(pv_ready, 2 + first_unit + v + 1)
                            act.activation(oh[:, v // TT, (v % TT) * P:(v % TT + 1) * P], side[3][:, 0:P], ACT.Copy).then_inc(pv_taken, 1)
                    high_next(0, p)
                    evacuate(p)

                with act.Fori(0, ZX[1] - 1) as i:
                    attention_body(i, ZX[0] + i)
                body(LAST, more=False)

            @block.vector
            def _(dve):
                dve.sem_inc(split_ready, RAW_FREE)
                dve.sem_inc(acc_taken, ACC_FREE)
                dve.sem_inc(logits_masked, 2)
                dve.sem_inc(probsT_ready, 1)
                dve.sem_inc(pv_taken, 1)
                for u in range(N_SMALL_X):
                    t, g = u // (DK // 4), u % (DK // 4)
                    cut = (slice(None), slice(4 * g, 4 * g + 4), slice(t * P, (t + 1) * P))
                    dve.wait_ge(x_hi, u + 1)
                    dve.tensor_tensor(xlo[cut], banks[u % 8][:, :].rearrange("p (j n) -> p j n", j=4),
                                      xhi[cut].bitcast(FP32), ALU.subtract).then_inc(x_lo, 1)
                dve.wait_ge(small_hi, 1)
                dve.tensor_tensor(wsm_lo[:], wsm_raw[:], wsm_hi[:].bitcast(FP32), ALU.subtract).then_inc(small_lo, 1)

                def low(c, p):
                    dve.wait_ge(hi_ready, 4 * p + c + 1)
                    s = c % SPLIT_SLOTS
                    dve.tensor_tensor(wlo[s][:], raw[:, c], whi[s][:].bitcast(FP32), ALU.subtract).then_inc(split_ready, 1)

                def low_next(c, p, more=True):
                    if c:
                        low(c, p)
                    elif more:
                        low(0, p + 1)

                low(0, 0)
                step = [0]

                def link(ins):
                    step[0] += 1
                    ins.then_inc(dve_step, 1)
                    dve.wait_ge(dve_step, step[0])

                dve.wait_ge(small_out, 1)
                for t in range(TT):
                    last = dve.bn_stats(stats[:, t, :], small[:, t, 0:ID])
                link(last)
                for t in range(TT):
                    link(dve.bn_aggr(mv[:, t, :], stats[:, t, :]))
                link(dve.tensor_scalar(rstd[:], mv[:, :, 1], EPS, None, ALU.add))
                link(dve.tensor_scalar(iws[:], small[:, :, ID:ID + IH], ID ** -0.5 * IH ** -0.5, None, ALU.mult))
                dve.wait_ge(small_out, 2)
                link(dve.reciprocal(rstd[:], rstd[:]))
                for t in range(TT):
                    for half in range(2):
                        last = dve.tensor_scalar(ikn[:, t, half * ID:(half + 1) * ID], small[:, t, 0:ID],
                                                 mv[:, t, 0:1], rstd[:, t:t + 1], ALU.subtract, ALU.mult)
                last.then_inc(ikn_done, 1)
                with dve.Fori(0, QK[1] + IQ[1]) as i:
                    for c in (1, 2, 3, 0):
                        low_next(c, i)
                for u in range(TT * IH):
                    q, h = u // IH, u % IH
                    dve.wait_ge(relu_ready, u + 1)
                    base = k.causal_bias[:, SEQ - width(q):SEQ] if h == 0 else score[q][:]
                    if h:
                        dve.wait_ge(score_step, u)
                    dve.scalar_tensor_tensor(out=score[q][:], in0=relu[:, u % 2, 0:width(q)], scalar=iws[:, q, h:h + 1],
                                             in1=base, op0=ALU.mult, op1=ALU.add).then_inc(score_step, 1)
                dve.wait_ge(score_step, TT * IH)

                def pick(q):
                    link(dve.max(top8[:], score[q][:]))
                    link(dve.match_replace(score[q][:], top8[:], score[q][:], TAKEN))

                rounds = [q for q in range(1, TT) for _ in range(TOPK // 8)]
                share = -(-len(rounds) // (V[1] * CH))
                for i in range(V[1]):
                    for c in (1, 2, 3, 0):
                        low_next(c, V[0] + i)
                        for q in rounds[:share]:
                            pick(q)
                        rounds = rounds[share:]
                link(dve.tensor_copy(score[0][:], k.causal_bias[:, SEQ - P:SEQ]))
                for q in range(1, TT):
                    link(dve.tensor_scalar(score[q][:], score[q][:], TAKEN, NEG, ALU.is_gt, ALU.mult))

                def attention_body(it, p):
                    first_unit = UNITS * it
                    for j in range(SLOTS):
                        if j in (0, 4, 8):
                            low_next(j // 4 + 1, p)
                        if j < UNITS:
                            q = j % TT
                            dve.wait_ge(dve_step, step[0])
                            dve.wait_ge(logits_ready, first_unit + j + 1)
                            dve.wait_ge(probs_turned, first_unit + j + 1)
                            dve.sem_inc(passed_dve, 1)
                            dve.tensor_tensor_reduce(out=probs[:, j % 2, 0:width(q)], in0=side[j % 2][:, 0:width(q)],
                                                     in1=score[q][:], scale=1.0, scalar=TAKEN, op0=ALU.add, op1=ALU.max,
                                                     accum_out=nmax[:, j % 2, 0:1]).then_inc(logits_masked, 1)
                            dve.wait_ge(logits_masked, 2 + first_unit + j + 1)
                            dve.tensor_scalar(nmax[:, j % 2, 1:2], nmax[:, j % 2, 0:1], -AD ** -0.5, None,
                                              ALU.mult).then_inc(max_ready, 1)
                        if 1 <= j <= UNITS:
                            v, q = j - 1, (j - 1) % TT
                            dve.wait_ge(probs_turned, 2 + first_unit + v + 1)
                            dve.wait_ge(pv_ready, first_unit + v + 1)
                            dve.tensor_copy(probsT[:, v % 2, 0:width(q)], side[2][:, 0:width(q)]).then_inc(probsT_ready, 1)
                        if j < UNITS:
                            dve.wait_ge(exp_ready, first_unit + j + 1)
                            dve.reciprocal(rowsum[:, j % 2:j % 2 + 1], rowsum[:, j % 2:j % 2 + 1]).then_inc(sum_inverted, 1)
                            dve.wait_ge(sum_inverted, first_unit + j + 1)
                            dve.tensor_scalar(probs[:, j % 2, 0:width(j % TT)], probs[:, j % 2, 0:width(j % TT)],
                                              rowsum[:, j % 2:j % 2 + 1], None, ALU.mult).then_inc(probs_ready, 1)
                    low_next(0, p)

                with dve.Fori(0, ZX[1] - 1) as i:
                    attention_body(i, ZX[0] + i)
                for c in (1, 2, 3, 0):
                    low_next(c, LAST, more=False)

            @block.gpsimd
            def _(pool):
                pool.wait_ge(small_out, 1)
                for t in range(TT):
                    pool.dma_start(scr.dt[t * P:(t + 1) * P, :], small[:, t, ID + IH:SMALL]).then_inc(stored[t], 16)

                def store(p, dst):
                    for t in range(TT):
                        pool.wait_ge(acc_taken, ACC_FREE + 4 * p + t + 1)
                        pool.sem_inc(passed_pool, 1)
                        pool.dma_start(dst(t), stage[:, t, :]).then_inc(stored[t], 16)

                with pool.Fori(0, QK[1]) as i:
                    store(QK[0] + i, lambda t: scr.qkT[bass.ds(i * PW + t * P, P), :])
                with pool.Fori(0, IQ[1]) as i:
                    store(IQ[0] + i, lambda t: scr.iqT[bass.ds(i * PW + t * P, P), :])
                for t in range(TT):
                    pool.wait_ge(stored[t], 16 * (1 + V[0]))
                pool.dma_start(iq, scr.iqT.rearrange("(h p) n -> p h n", p=P)).then_inc(iq_here, 16)
                with pool.Fori(0, V[1]) as i:
                    store(V[0] + i, lambda t: scr.v[t * P:(t + 1) * P, bass.ds(i * PW, PW)])
                for t in range(TT):
                    pool.wait_ge(stored[t], 16 * (1 + ZX[0]))
                pool.wait_ge(dots_ready, TT * IH)

                def load_heads(it):
                    row = it * HEADS_PER_PANEL * P
                    n = HEADS_PER_PANEL * P
                    pool.dma_start(qh, scr.qkT[bass.ds(row, n), :].rearrange("(h p) n -> p h n", p=P)).then_inc(heads_here, 16)
                    pool.dma_start(kh, scr.qkT[bass.ds(AH * AD + row, n), :].rearrange("(h p) n -> p h n", p=P)).then_inc(heads_here, 16)
                    pool.dma_start(vh, scr.v.rearrange("(s p) n -> p s n", p=P)[:, :, bass.ds(row, n)]).then_inc(heads_here, 16)

                def store_heads(it):
                    pool.wait_ge(pv_taken, 1 + UNITS * (it + 1))
                    pool.sem_inc(passed_pool, 1)
                    pool.dma_start(scr.yT[bass.ds(SSD_W + it * HEADS_PER_PANEL * P, HEADS_PER_PANEL * P), :]
                                   .rearrange("(h p) n -> p h n", p=P), oh).then_inc(att_stored, 16)

                load_heads(0)
                with pool.Fori(0, ZX[1] - 2) as i:
                    store_heads(i)
                    pool.wait_ge(att_stored, 16 * (i + 1))
                    pool.sem_inc(passed_pool, 1)
                    load_heads(i + 1)
                    store(ZX[0] + i, lambda t: scr.zxT[bass.ds(i * PW + t * P, P), :])
                store_heads(ZX[1] - 2)
                for n in (ZX[1] - 2, ZX[1] - 1):
                    store(ZX[0] + n, lambda t: scr.zxT[n * PW + t * P:n * PW + (t + 1) * P, :])
                for t in range(TT):
                    pool.wait_ge(stored[t], 16 * (1 + LAST + 1))
                pool.wait_ge(att_stored, 16 * (ZX[1] - 1))


def run_ssd(nc, k, conv_w, conv_b, dt_bias, a_log, d_skip, norm_w, scr):
    XT, CT = SSD_W // P, CONV_DIM // P
    ITER = [(c, g) for c in range(TT) for g in range(GROUPS)]
    GW = HPG * HD
    N_PAR = CONV_TAPS * CT + CT + 2 * XT
    with ExitStack() as ctx:
        def sb(name, shape, dt=FP32):
            return ctx.enter_context(nc.sbuf_tensor(name, shape, dt))

        def sem(name):
            return k.semaphore(name)

        banks = [ctx.enter_context(nc.psum_tensor(f"sbank{i}", [P, PW], FP32)) for i in range(8)]
        acs_rows, small_bank, y_bank, carry_bank, state_bank, turn_in, turn_out = \
            banks[0:2], banks[2], banks[3], banks[4], banks[5], banks[6], banks[7]
        u = sb("u", [P, CT, SEQ])
        z = sb("z", [P, XT, SEQ])
        xbc = sb("xbc", [P, CT, SEQ])
        y = sb("y", [P, XT, SEQ])
        rows = sb("rows", [N_PAR, P])
        skip2 = sb("skip2", [XT, 2])
        skip_rows = sb("skip_rows", [XT, P])
        head_rows = sb("head_rows", [1, 2 * HEADS])
        par = sb("par", [P, N_PAR])
        head = sb("head", [P, 2 * HEADS])
        H4 = [P, TT, HEADS]
        dt, pos, ea, u1, dta = sb("dtv", H4), sb("pos", H4), sb("ex", H4), sb("u1", H4), sb("dta", H4)
        acs, acs_exp, to_end, chunk_decay = sb("acs", H4), sb("acs_exp", H4), sb("to_end", H4), sb("chunk_decay", H4)
        nega = sb("nega", [P, HEADS])
        xdt, xdec = sb("xdt", [P, 2, GW]), sb("xdec", [P, 2, GW])
        b_tok = sb("b_tok", [P, 2, STATE])
        cbm = sb("cbm", [P, 2, P])
        seg = sb("seg", [P, 2, PW])
        m = sb("m", [P, 2, 2, PW])
        carry = sb("carry", [P, GROUPS, GW])
        yoff, ytok = sb("yoff", [P, 2, GW]), sb("ytok", [P, 2, GW])
        sq = sb("sq", [P, 2, SEQ])
        rinv = sb("rinv", [P, SEQ])
        zeros = sb("zeros", [P, D])

        zeros_ready, beyond_cleared = sem("zeros_ready"), sem("beyond_cleared")
        par_here, z_here, dt_here = sem("par_here"), sem("z_here"), sem("dt_here")
        u_here = [sem(f"u_here{n}") for n in range(3)]
        skip_here = sem("skip_here")
        skip_spread, par_turned, par_out = sem("skip_spread"), sem("par_turned"), sem("par_out")
        conv_step, conv_done, silu_done = sem("conv_step"), sem("conv_done"), sem("silu_done")
        dt_step, dt_exp, acs_ready = sem("dt_step"), sem("dt_exp"), sem("acs_ready")
        x_turned, cb_ready, rows_ready = sem("sx_turned"), sem("cb_ready"), sem("rows_ready")
        b_out, seg_out, seg_exp = sem("b_out"), sem("seg_out"), sem("seg_exp")
        xdt_ready, cbm_ready, m_ready, xdec_ready = sem("xdt_ready"), sem("cbm_ready"), sem("m_ready"), sem("xdec_ready")
        diag_ready, off_ready, state_ready = sem("diag_ready"), sem("off_ready"), sem("state_ready")
        off_scaled, y_ready, carry_scaled, carry_ready = sem("off_scaled"), sem("y_ready"), sem("carry_scaled"), sem("carry_ready")
        y_turned, y_skip, gated = sem("y_turned"), sem("y_skip"), sem("gated")
        squared, square_used, sums_ready, mean_out, root_out, rinv_ready = \
            sem("squared"), sem("square_used"), sem("sums_ready"), sem("mean_out"), sem("root_out"), sem("rinv_ready")
        normed, y_stored = sem("normed"), sem("y_stored")

        tap = lambda j, i: par[:, j * CT + i:j * CT + i + 1]
        bias = lambda i: par[:, CONV_TAPS * CT + i:CONV_TAPS * CT + i + 1]
        norm = lambda i: par[:, (CONV_TAPS + 1) * CT + i:(CONV_TAPS + 1) * CT + i + 1]
        skip = lambda i: par[:, (CONV_TAPS + 1) * CT + XT + i:(CONV_TAPS + 1) * CT + XT + i + 1]
        B_TILE, C_TILE = XT, XT + GROUPS
        ORDER = [B_TILE, C_TILE] + list(range(XT // 2)) + [B_TILE + 1, C_TILE + 1] + list(range(XT // 2, XT))
        FIRST_GROUP = 2 + XT // 2

        def need(i):
            return FIRST_GROUP if i == 0 else CT

        def per_head(a):
            return a.unsqueeze(2).broadcast_to((P, HPG, HD))

        def heads_of(g):
            return slice(g * HPG, (g + 1) * HPG)

        def cut(c):
            return slice(c * P, (c + 1) * P)

        with nc.Block() as block:
            @block.sync
            def _(sp):
                n = CONV_TAPS * CT
                sp.dma_start(skip2[:], d_skip[0].rearrange("(i h) -> i h", h=2)).then_inc(skip_here, 16)
                sp.dma_start(rows[0:n, :], conv_w[0].rearrange("j (i c) -> (j i) c", c=P)).then_inc(par_here, 16)
                sp.dma_start(rows[n:n + CT, :], conv_b[0].rearrange("(i c) -> i c", c=P)).then_inc(par_here, 16)
                sp.dma_start(rows[n + CT:n + CT + XT, :], norm_w[0].rearrange("(i c) -> i c", c=P)).then_inc(par_here, 16)
                sp.dma_start(head_rows[:, 0:HEADS], dt_bias).then_inc(par_here, 16)
                sp.dma_start(head_rows[:, HEADS:2 * HEADS], a_log).then_inc(par_here, 16)
                sp.dma_start(dt[:], scr.dt.rearrange("(t p) n -> p t n", p=P)).then_inc(dt_here, 16)
                src = scr.zxT.rearrange("(i p) n -> p i n", p=P)
                half = XT // 2
                sp.dma_start(u[:, B_TILE:CT, :], src[:, XT + B_TILE:XT + CT, :]).then_inc(u_here[0], 16)
                sp.dma_start(u[:, 0:half, :], src[:, XT:XT + half, :]).then_inc(u_here[1], 16)
                sp.dma_start(u[:, half:XT, :], src[:, XT + half:2 * XT, :]).then_inc(u_here[2], 16)
                sp.dma_start(z[:], src[:, 0:XT, :]).then_inc(z_here, 16)
                sp.wait_ge(skip_spread, 1)
                sp.dma_start(rows[n + CT + XT:N_PAR, :], skip_rows[:]).then_inc(par_here, 16)
                sp.wait_ge(zeros_ready, 1)
                beyond = MAX_OVER * CAP
                for r in range(0, beyond, P):
                    n = min(P, beyond - r)
                    sp.dma_start(scr.yb[N_EXP * CAP + r:N_EXP * CAP + r + n, :], zeros[0:n, :]).then_inc(beyond_cleared, 16)
                for i in range(XT):
                    sp.wait_ge(normed, i + 1)
                    sp.dma_start(scr.yT[i * P:(i + 1) * P, :], y[:, i, :]).then_inc(y_stored, 16)
                sp.wait_ge(y_stored, 16 * XT)
                sp.wait_ge(beyond_cleared, 16 * -(-beyond // P))

            @block.tensor
            def _(pe):
                pe.wait_ge(par_here, 16 * 6)
                pe.transpose(turn_in[:, 0:N_PAR], rows[:], k.ident[0:N_PAR, 0:N_PAR])
                pe.matmul(turn_out[:, 0:2 * HEADS], k.ones[0:1, :], head_rows[:], start=True, stop=True).then_inc(par_turned, 1)
                pe.wait_ge(dt_step, DT_STEPS)
                pe.matmul(y_bank[:, 0:TT * HEADS], k.upto[:], dta[:].rearrange("p t h -> p (t h)"), start=True, stop=True)
                pe.matmul(carry_bank[:, 0:TT * HEADS], k.ones[:], dta[:].rearrange("p t h -> p (t h)"),
                          start=True, stop=True).then_inc(acs_ready, 1)

                def scan_inputs(i):
                    c, g = ITER[i]
                    pe.wait_ge(silu_done, need(i))
                    if i >= 1:
                        pe.wait_ge(xdt_ready, i)
                    for j in range(4):
                        last = pe.transpose(turn_in[:, j * P:(j + 1) * P], xbc[:, 4 * g + j, cut(c)], k.ident[:])
                    last.then_inc(x_turned, 1)
                    if i >= 1:
                        pe.wait_ge(cbm_ready, i)
                        pe.wait_ge(b_out, i)
                    pe.transpose(small_bank[:, P:2 * P], xbc[:, B_TILE + g, cut(c)], k.ident[:])
                    pe.matmul(small_bank[:, 0:P], xbc[:, B_TILE + g, cut(c)], xbc[:, C_TILE + g, cut(c)],
                              start=True, stop=True).then_inc(cb_ready, 1)
                    for b in range(2):
                        if i >= 1:
                            pe.wait_ge(seg_out, 4 * (2 * (i - 1) + b + 1))
                        for j in range(4):
                            h = g * HPG + 4 * b + j
                            last = pe.matmul(acs_rows[b][:, j * P:(j + 1) * P], dta[:, c, h:h + 1].broadcast_to((P, P)),
                                             k.upto[:], start=True, stop=True)
                        last.then_inc(rows_ready, 1)

                def scan(i):
                    c, g = ITER[i]
                    pe.wait_ge(m_ready, 2 * i + 2)
                    if i >= 1:
                        pe.wait_ge(y_ready, i)
                    else:
                        pe.wait_ge(dt_exp, DT_EXPS)
                    for j in range(HPG):
                        last = pe.matmul(y_bank[:, j * HD:(j + 1) * HD], m[:, i % 2, j // 4, (j % 4) * P:(j % 4 + 1) * P],
                                         xdt[:, i % 2, j * HD:(j + 1) * HD], start=True, stop=True)
                    last.then_inc(diag_ready, 1)
                    if c:
                        pe.wait_ge(carry_ready, (c - 1) * GROUPS + g + 1)
                        pe.matmul(carry_bank[:], xbc[:, C_TILE + g, cut(c)], carry[:, g, :], start=True, stop=True).then_inc(off_ready, 1)
                    if c < TT - 1:
                        pe.wait_ge(xdec_ready, i + 1)
                        pe.wait_ge(b_out, i + 1)
                        if i >= 1:
                            pe.wait_ge(carry_ready, i)
                        pe.matmul(state_bank[:], b_tok[:, i % 2, :], xdec[:, i % 2, :], start=True, stop=True).then_inc(state_ready, 1)

                def turn_back(i):
                    pe.wait_ge(y_ready, i + 1)
                    if i >= 1:
                        pe.wait_ge(y_skip, 4 * i)
                    for j in range(4):
                        last = pe.transpose(turn_out[:, j * P:(j + 1) * P], ytok[:, i % 2, j * P:(j + 1) * P], k.ident[:])
                    last.then_inc(y_turned, 1)

                scan_inputs(0)
                for i in range(len(ITER)):
                    if i + 1 < len(ITER):
                        scan_inputs(i + 1)
                    scan(i)
                    if i:
                        turn_back(i - 1)
                turn_back(len(ITER) - 1)
                for i in range(XT):
                    pe.wait_ge(squared, i + 1)
                    pe.matmul(acs_rows[0][:], k.ones[:], sq[:, i % 2, :], start=(i == 0), stop=(i == XT - 1)).then_inc(square_used, 1)

            @block.scalar
            def _(act):
                act.wait_ge(par_turned, 1)
                act.activation(par[:], turn_in[:, 0:N_PAR], ACT.Copy).then_inc(par_out, 1)
                act.activation(head[:], turn_out[:, 0:2 * HEADS], ACT.Copy).then_inc(par_out, 1)
                act.wait_ge(par_out, 2)
                act.activation(nega[:], head[:, HEADS:2 * HEADS], ACT.Exp).then_inc(dt_exp, 1)
                act.wait_ge(dt_step, 3)
                act.activation(ea[:], ea[:], ACT.Exp, scale=-1.0).then_inc(dt_exp, 1)
                act.wait_ge(dt_step, 4)
                act.activation(acs[:], u1[:], ACT.Ln).then_inc(dt_exp, 1)
                for n, i in enumerate(ORDER[:FIRST_GROUP]):
                    act.wait_ge(conv_done, n + 1)
                    act.activation(xbc[:, i, :], xbc[:, i, :], ACT.Silu).then_inc(silu_done, 1)
                for n, i in enumerate(ORDER[FIRST_GROUP:]):
                    act.wait_ge(conv_done, FIRST_GROUP + n + 1)
                    act.activation(xbc[:, i, :], xbc[:, i, :], ACT.Silu).then_inc(silu_done, 1)
                act.wait_ge(z_here, 16)
                for i in range(XT):
                    act.activation(z[:, i, :], z[:, i, :], ACT.Silu).then_inc(silu_done, 1)
                act.wait_ge(acs_ready, 1)
                act.activation(acs[:], y_bank[:, 0:TT * HEADS].rearrange("p (t h) -> p t h", t=TT), ACT.Copy).then_inc(dt_exp, 1)
                act.activation(acs_exp[:], y_bank[:, 0:TT * HEADS].rearrange("p (t h) -> p t h", t=TT), ACT.Exp).then_inc(dt_exp, 1)
                act.activation(chunk_decay[:], carry_bank[:, 0:TT * HEADS].rearrange("p (t h) -> p t h", t=TT), ACT.Exp).then_inc(dt_exp, 1)
                act.wait_ge(dt_step, DT_STEPS + 1)
                act.activation(to_end[:], to_end[:], ACT.Exp).then_inc(dt_exp, 1)
                act.wait_ge(dt_exp, DT_EXPS)

                for i, (c, g) in enumerate(ITER):
                    for b in range(2):
                        act.wait_ge(rows_ready, 2 * i + b + 1)
                        if i >= 1:
                            act.wait_ge(m_ready, 2 * (i - 1) + b + 1)
                        for j in range(4):
                            h = g * HPG + 4 * b + j
                            act.activation(seg[:, b, j * P:(j + 1) * P], acs_rows[b][:, j * P:(j + 1) * P], ACT.Relu,
                                           bias=acs[:, c, h:h + 1], scale=-1.0).then_inc(seg_out, 1)
                        act.wait_ge(seg_out, 4 * (2 * i + b + 1))
                        act.activation(seg[:, b, :], seg[:, b, :], ACT.Exp, scale=-1.0).then_inc(seg_exp, 1)
                for i in range(XT):
                    act.wait_ge(gated, i + 1)
                    if i >= 2:
                        act.wait_ge(square_used, i - 1)
                    act.activation(sq[:, i % 2, :], y[:, i, :], ACT.Square).then_inc(squared, 1)
                act.wait_ge(mean_out, 1)
                act.activation(rinv[:], rinv[:], ACT.Sqrt).then_inc(root_out, 1)

            @block.vector
            def _(dve):
                step = [0]

                def link(ins):
                    step[0] += 1
                    ins.then_inc(dt_step, 1)
                    dve.wait_ge(dt_step, step[0])

                dve.wait_ge(skip_here, 16)
                dve.tensor_copy(skip_rows[:].rearrange("i (h n) -> i h n", h=2),
                                skip2[:].unsqueeze(2).broadcast_to((XT, 2, HD))).then_inc(skip_spread, 1)
                dve.wait_ge(par_out, 2)
                dve.wait_ge(dt_here, 16)
                every = (P, TT, HEADS)
                link(dve.tensor_tensor(dt[:], dt[:], head[:, 0:HEADS].unsqueeze(1).broadcast_to(every), ALU.add))
                link(dve.tensor_scalar(pos[:], dt[:], 0.0, None, ALU.max))
                link(dve.scalar_tensor_tensor(out=ea[:], in0=pos[:], scalar=2.0, in1=dt[:], op0=ALU.mult, op1=ALU.subtract))
                dve.wait_ge(dt_exp, 2)
                link(dve.tensor_scalar(u1[:], ea[:], 1.0, None, ALU.add))
                link(dve.tensor_scalar(dt[:], u1[:], -1.0, None, ALU.add))
                link(dve.tensor_tensor(dt[:], ea[:], dt[:], ALU.subtract))
                dve.wait_ge(dt_exp, 3)
                link(dve.reciprocal(u1[:], u1[:]))
                link(dve.tensor_tensor(dt[:], dt[:], u1[:], ALU.mult))
                link(dve.tensor_tensor(dt[:], dt[:], acs[:], ALU.add))
                link(dve.tensor_tensor(dt[:], dt[:], pos[:], ALU.add))
                link(dve.tensor_scalar(nega[:], nega[:], -1.0, None, ALU.mult))
                link(dve.tensor_tensor(dta[:], dt[:], nega[:].unsqueeze(1).broadcast_to(every), ALU.mult))
                assert step[0] == DT_STEPS

                conv = 0
                for n, i in enumerate(ORDER):
                    dve.wait_ge(u_here[0 if i >= XT else 1 if i < XT // 2 else 2], 16)
                    dve.tensor_scalar(xbc[:, i, :], u[:, i, :], tap(CONV_TAPS - 1, i), bias(i), ALU.mult, ALU.add).then_inc(conv_step, 1)
                    conv += 1
                    for back in range(1, CONV_TAPS):
                        dve.wait_ge(conv_step, conv)
                        ins = dve.scalar_tensor_tensor(out=xbc[:, i, back:], in0=u[:, i, 0:SEQ - back],
                                                       scalar=tap(CONV_TAPS - 1 - back, i), in1=xbc[:, i, back:],
                                                       op0=ALU.mult, op1=ALU.add)
                        if back < CONV_TAPS - 1:
                            ins.then_inc(conv_step, 1)
                            conv += 1
                        else:
                            ins.then_inc(conv_done, 1)

                dve.wait_ge(dt_exp, DT_EXPS - 1)
                link(dve.tensor_tensor(to_end[:], carry_bank[:, 0:TT * HEADS].rearrange("p (t h) -> p t h", t=TT), acs[:], ALU.subtract))
                dve.wait_ge(dt_exp, DT_EXPS)

                def operands(i):
                    c, g = ITER[i]
                    dve.wait_ge(x_turned, i + 1)
                    if i >= 2:
                        dve.wait_ge(diag_ready, i - 1)
                        dve.wait_ge(xdec_ready, i - 1)
                    dve.tensor_tensor(xdt[:, i % 2, :].rearrange("p (h n) -> p h n", n=HD),
                                      turn_in[:, :].rearrange("p (h n) -> p h n", n=HD),
                                      per_head(dt[:, c, heads_of(g)]), ALU.mult).then_inc(xdt_ready, 1)
                    dve.wait_ge(cb_ready, i + 1)
                    dve.tensor_tensor(cbm[:, i % 2, :], small_bank[:, 0:P], k.upto[:], ALU.mult).then_inc(cbm_ready, 1)
                    if 2 <= i and ITER[i - 2][0] < TT - 1:
                        dve.wait_ge(state_ready, i - 1)
                    dve.tensor_copy(b_tok[:, i % 2, :], small_bank[:, P:2 * P]).then_inc(b_out, 1)
                    dve.wait_ge(cbm_ready, i + 1)
                    for b in range(2):
                        dve.wait_ge(seg_exp, 2 * i + b + 1)
                        dve.tensor_tensor(m[:, i % 2, b, :].rearrange("p (h n) -> p h n", n=P),
                                          seg[:, b, :].rearrange("p (h n) -> p h n", n=P),
                                          cbm[:, i % 2, :].unsqueeze(1).broadcast_to((P, 4, P)), ALU.mult).then_inc(m_ready, 1)

                def results(i):
                    c, g = ITER[i]
                    as_heads = lambda a: a.rearrange("p (h n) -> p h n", n=HD)
                    dve.wait_ge(diag_ready, i + 1)
                    if i >= 2:
                        dve.wait_ge(y_turned, i - 1)
                    if c:
                        dve.wait_ge(off_ready, i - GROUPS + 1)
                        dve.tensor_tensor(as_heads(yoff[:, i % 2, :]), as_heads(carry_bank[:, :]),
                                          per_head(acs_exp[:, c, heads_of(g)]), ALU.mult).then_inc(off_scaled, 1)
                        dve.wait_ge(off_scaled, i - GROUPS + 1)
                        dve.tensor_tensor(ytok[:, i % 2, :], y_bank[:, :], yoff[:, i % 2, :], ALU.add).then_inc(y_ready, 1)
                    else:
                        dve.tensor_copy(ytok[:, i % 2, :], y_bank[:, :]).then_inc(y_ready, 1)
                    if c < TT - 1:
                        dve.wait_ge(state_ready, i + 1)
                        if c:
                            dve.tensor_tensor(as_heads(carry[:, g, :]), as_heads(carry[:, g, :]),
                                              per_head(chunk_decay[:, c, heads_of(g)]), ALU.mult).then_inc(carry_scaled, 1)
                            dve.wait_ge(carry_scaled, i - GROUPS + 1)
                            dve.tensor_tensor(carry[:, g, :], state_bank[:, :], carry[:, g, :], ALU.add).then_inc(carry_ready, 1)
                        else:
                            dve.tensor_copy(carry[:, g, :], state_bank[:, :]).then_inc(carry_ready, 1)

                def skips(i):
                    c, g = ITER[i]
                    dve.wait_ge(y_turned, i + 1)
                    for j in range(4):
                        t = 4 * g + j
                        dve.scalar_tensor_tensor(out=y[:, t, cut(c)], in0=xbc[:, t, cut(c)], scalar=skip(t),
                                                 in1=turn_out[:, j * P:(j + 1) * P], op0=ALU.mult, op1=ALU.add).then_inc(y_skip, 1)

                operands(0)
                for i in range(len(ITER)):
                    if i + 1 < len(ITER):
                        operands(i + 1)
                    results(i)
                    if i:
                        skips(i - 1)
                skips(len(ITER) - 1)
                dve.wait_ge(y_skip, 4 * len(ITER))
                dve.wait_ge(silu_done, CT + XT)
                for i in range(XT):
                    dve.tensor_tensor(y[:, i, :], y[:, i, :], z[:, i, :], ALU.mult).then_inc(gated, 1)
                dve.wait_ge(square_used, XT)
                dve.tensor_scalar(rinv[:], acs_rows[0][:], 1.0 / SSD_W, EPS, ALU.mult, ALU.add).then_inc(mean_out, 1)
                dve.wait_ge(root_out, 1)
                dve.reciprocal(rinv[:], rinv[:]).then_inc(rinv_ready, 1)
                dve.wait_ge(rinv_ready, 1)
                for i in range(XT):
                    dve.scalar_tensor_tensor(out=y[:, i, :], in0=y[:, i, :], scalar=norm(i), in1=rinv[:],
                                             op0=ALU.mult, op1=ALU.mult).then_inc(normed, 1)

            @block.gpsimd
            def _(pool):
                pool.memset(zeros[:], 0.0).then_inc(zeros_ready, 1)
                pool.wait_ge(dt_exp, DT_EXPS)
                for i, (c, g) in enumerate(ITER):
                    if c == TT - 1:
                        break
                    pool.wait_ge(xdt_ready, i + 1)
                    if i >= 2:
                        pool.wait_ge(state_ready, i - 1)
                    pool.tensor_tensor(xdec[:, i % 2, :].rearrange("p (h n) -> p h n", n=HD),
                                       xdt[:, i % 2, :].rearrange("p (h n) -> p h n", n=HD),
                                       per_head(to_end[:, c, heads_of(g)]), ALU.mult).then_inc(xdec_ready, 1)


DT_STEPS, DT_EXPS = 12, 7

OUT_PANELS = D // PW
CAP = 64
MAX_OVER = SEQ * 2 // CAP - 1
BLOCKS = N_EXP + MAX_OVER
LN_STAT = 6


def run_output(nc, k, x, w_out, ln_g, ln_b, router_w, router_b, scr, keep):
    w = w_out[0]
    with ExitStack() as ctx:
        def sb(name, shape, dt=FP32):
            return ctx.enter_context(nc.sbuf_tensor(name, shape, dt))

        def sem(name):
            return k.semaphore(name)

        banks = [ctx.enter_context(nc.psum_tensor(f"obank{i}", [P, PW], FP32)) for i in range(8)]
        acc, side = banks[0:4], banks[4:8]
        yhi, ylo = sb("yhi", [P, DK, SEQ], FP32R), sb("ylo", [P, DK, SEQ], FP32R)
        raw = sb("oraw", [P, CH, KC, PW])
        whi = [sb(f"owhi{i}", [P, KC, PW], FP32R) for i in range(SPLIT_SLOTS)]
        wlo = [sb(f"owlo{i}", [P, KC, PW], FP32R) for i in range(SPLIT_SLOTS)]
        h = sb("h", [P, TT, D])
        yraw = h[:, :, 0:0]
        stats = sb("ostats", [P, TT, OUT_PANELS, LN_STAT])
        mv, rstd, shift = sb("omv", [P, TT, 2]), sb("orstd", [P, TT]), sb("oshift", [P, TT])

        x_here, raw_here = sem("ox_here"), [sem(f"oraw_here{c}") for c in range(CH)]
        y_here = [sem(f"y_here{c}") for c in range(CH)]
        y_hi, y_lo = sem("y_hi"), sem("y_lo")
        hi_ready, split_ready, split_used = sem("ohi_ready"), sem("osplit_ready"), sem("osplit_used")
        acc_ready, acc_taken, stat_ready = sem("oacc_ready"), sem("oacc_taken"), sem("stat_ready")
        gb_here, gb_ready, gb_taken = sem("gb_here"), sem("gb_ready"), sem("gb_taken")
        mv_ready, var_ready, root_ready, rstd_ready, shift_ready = \
            sem("mv_ready"), sem("var_ready"), sem("root_ready"), sem("rstd_ready"), sem("shift_ready")
        normed, gained, h_ready, h_stored = sem("onormed"), sem("gained"), sem("h_ready"), sem("h_stored")
        RAW_FREE, ACC_FREE = CH, TT

        with nc.Block() as block:
            @block.sync
            def _(sp):
                src = scr.yT.rearrange("(c k p) n -> c p k n", p=P, k=KC)
                for c in range(CH):
                    sp.dma_start(raw[:, c], src[c]).then_inc(y_here[c], 16)
                for c in range(CH):
                    sp.wait_ge(y_lo, c + 1)
                    rows = w[c * KC * P:(c + 1) * KC * P, 0:PW].rearrange("(k p) n -> p k n", p=P)
                    sp.dma_start(raw[:, c], rows).then_inc(raw_here[c], 16)
                sp.dma_start(h[:], x[0].rearrange("(t p) n -> p t n", p=P)).then_inc(x_here, 16)
                sp.dma_start(keep.gain_rows[:, 0, :], ln_g).then_inc(gb_here, 16)
                sp.dma_start(keep.gain_rows[:, 1, :], ln_b).then_inc(gb_here, 16)
                with sp.Fori(1, OUT_PANELS) as p:
                    for c in range(CH):
                        sp.wait_ge(split_ready, 4 * p + c + 1)
                        rows = w[c * KC * P:(c + 1) * KC * P, :].rearrange("(k p) n -> p k n", p=P)
                        sp.dma_start(raw[:, c], rows[:, :, bass.ds(p * PW, PW)]).then_inc(raw_here[c], 16)
                for t in range(TT):
                    sp.wait_ge(h_ready, t + 1)
                    sp.dma_start(scr.h1[t * P:(t + 1) * P, :], h[:, t, :]).then_inc(h_stored, 16)
                sp.wait_ge(h_stored, 16 * TT)

            @block.tensor
            def _(pe):
                pe.sem_inc(acc_ready, ACC_FREE)
                pe.wait_ge(y_lo, CH)
                with pe.Fori(0, OUT_PANELS) as p:
                    for c in range(CH):
                        s = c % SPLIT_SLOTS
                        pe.wait_ge(split_ready, RAW_FREE + 4 * p + c + 1)
                        for t in range(TT):
                            if c == 0:
                                pe.wait_ge(acc_taken, 4 * p + t + 1)
                            for kk in range(KC):
                                kt = c * KC + kk
                                for n, (a, b) in enumerate(((yhi, whi[s]), (yhi, wlo[s]), (ylo, whi[s]))):
                                    last = pe.matmul(acc[t][:], a[:, kt, t * P:(t + 1) * P], b[:, kk, :],
                                                     start=(c == 0 and kk == 0 and n == 0),
                                                     stop=(c == CH - 1 and kk == KC - 1 and n == 2))
                            if c == CH - 1:
                                last.then_inc(acc_ready, 1)
                            elif t == TT - 1:
                                last.then_inc(split_used, 1)
                pe.wait_ge(gb_here, 32)
                for n in range(2):
                    if n:
                        pe.wait_ge(gb_taken, TT)
                    for j in range(TT):
                        last = pe.matmul(side[j][:], k.ones[0:1, :], keep.gain_rows[:, n, j * PW:(j + 1) * PW], start=True, stop=True)
                    last.then_inc(gb_ready, 1)

            @block.scalar
            def _(act):
                for c in range(CH):
                    act.wait_ge(y_here[c], 16)
                    act.activation(yhi[:, c * KC:(c + 1) * KC, :], raw[:, c], ACT.Copy).then_inc(y_hi, 1)

                def high(c, p):
                    act.wait_ge(raw_here[c], 16 * (p + 1))
                    act.activation(whi[c % SPLIT_SLOTS][:], raw[:, c], ACT.Copy).then_inc(hi_ready, 1)

                def high_next(c, p, more=True):
                    if c == 1:
                        act.wait_ge(acc_ready, 4 * p + TT)
                        high(1, p)
                    elif c in (2, 3):
                        act.wait_ge(split_used, 3 * p + c - 1)
                        high(c, p)
                    elif more:
                        act.wait_ge(split_used, 3 * p + 3)
                        high(0, p + 1)

                high(0, 0)
                with act.Fori(0, OUT_PANELS - 1) as p:
                    for c in (1, 2, 3, 0):
                        high_next(c, p)
                for c in (1, 2, 3, 0):
                    high_next(c, OUT_PANELS - 1, more=False)
                for n in range(2):
                    act.wait_ge(gb_ready, n + 1)
                    for j in range(TT):
                        act.activation(keep.gain[:, n, j * PW:(j + 1) * PW], side[j][:], ACT.Copy).then_inc(gb_taken, 1)
                act.wait_ge(var_ready, 1)
                act.activation(rstd[:], rstd[:], ACT.Sqrt).then_inc(root_ready, 1)
                for t in range(TT):
                    act.wait_ge(shift_ready, 1)
                    act.activation(h[:, t, :], h[:, t, :], ACT.Identity, bias=shift[:, t:t + 1], scale=rstd[:, t:t + 1]).then_inc(normed, 1)

            @block.vector
            def _(dve):
                dve.sem_inc(split_ready, RAW_FREE)
                dve.sem_inc(acc_taken, ACC_FREE)
                for c in range(CH):
                    cut = (slice(None), slice(c * KC, (c + 1) * KC))
                    dve.wait_ge(y_hi, c + 1)
                    dve.tensor_tensor(ylo[cut], raw[:, c], yhi[cut].bitcast(FP32), ALU.subtract).then_inc(y_lo, 1)

                def low(c, p):
                    dve.wait_ge(hi_ready, 4 * p + c + 1)
                    s = c % SPLIT_SLOTS
                    dve.tensor_tensor(wlo[s][:], raw[:, c], whi[s][:].bitcast(FP32), ALU.subtract).then_inc(split_ready, 1)

                def evacuate(p):
                    for t in range(TT):
                        here = h[:, t, bass.ds(p * PW, PW)]
                        dve.wait_ge(acc_ready, ACC_FREE + 4 * p + t + 1)
                        dve.scalar_tensor_tensor(out=here, in0=here, scalar=ALPHA, in1=acc[t][:],
                                                 op0=ALU.mult, op1=ALU.add).then_inc(acc_taken, 1)
                        dve.wait_ge(acc_taken, ACC_FREE + 4 * p + t + 1)
                        dve.bn_stats(stats[:, t, bass.ds(p, 1), :] if not isinstance(p, int) else stats[:, t, p:p + 1, :],
                                     here).then_inc(stat_ready, 1)

                low(0, 0)
                dve.wait_ge(x_here, 16)
                with dve.Fori(0, OUT_PANELS - 1) as p:
                    for c in range(1, CH):
                        low(c, p)
                    low(0, p + 1)
                    evacuate(p)
                for c in range(1, CH):
                    low(c, OUT_PANELS - 1)
                evacuate(OUT_PANELS - 1)
                dve.wait_ge(stat_ready, 4 * OUT_PANELS)
                for t in range(TT):
                    dve.bn_aggr(mv[:, t, :], stats[:, t, :, :].rearrange("p a b -> p (a b)")).then_inc(mv_ready, 1)
                dve.wait_ge(mv_ready, TT)
                dve.tensor_scalar(rstd[:], mv[:, :, 1], EPS, None, ALU.add).then_inc(var_ready, 1)
                dve.wait_ge(root_ready, 1)
                dve.reciprocal(rstd[:], rstd[:]).then_inc(rstd_ready, 1)
                dve.wait_ge(rstd_ready, 1)
                dve.scalar_tensor_tensor(out=shift[:], in0=mv[:, :, 0], scalar=-1.0, in1=rstd[:],
                                         op0=ALU.mult, op1=ALU.mult).then_inc(shift_ready, 1)
                dve.wait_ge(gb_taken, 2 * TT)
                for t in range(TT):
                    dve.wait_ge(normed, t + 1)
                    dve.tensor_tensor(h[:, t, :], h[:, t, :], keep.gain[:, 0, :], ALU.mult).then_inc(gained, 1)
                    dve.wait_ge(gained, t + 1)
                    dve.tensor_tensor(h[:, t, :], h[:, t, :], keep.gain[:, 1, :], ALU.add).then_inc(h_ready, 1)


def run_router(nc, k, router_w, router_b, scr, keep):
    with ExitStack() as ctx:
        def sb(name, shape, dt=FP32):
            return ctx.enter_context(nc.sbuf_tensor(name, shape, dt))

        def sem(name):
            return k.semaphore(name)

        banks = [ctx.enter_context(nc.psum_tensor(f"rbank{i}", [P, PW], FP32)) for i in range(8)]
        turn, (logit_bank, rank_bank, count_bank, misc_bank) = banks[0:4], banks[4:8]
        h = sb("rh", [P, TT, D])
        rw = sb("router_sb", [P, DK, N_EXP])
        rb_row = sb("rb_row", [1, N_EXP])
        T8, T32, T1 = [P, TT, N_GRP], [P, TT, N_EXP], [P, TT]
        aff, biased, masked, eq, wgt, sel, dest, over = (sb(n, T32) for n in
                                                         ("aff", "biased", "masked", "eq", "wgt", "sel", "dest", "over"))
        hot = [sb("hot0", T32), sb("hot1", T32)]
        hi1, lo1, hi2, lo2, gs, g_eq, in_grp, pen = (sb(n, T8) for n in ("hi1", "lo1", "hi2", "lo2", "gs", "g_eq", "in_grp", "pen"))
        best, key = sb("best", T1), sb("key", T1)
        gate_sum = sb("gate_sum", T1)
        rank_g, rank_e = sb("rank_g", [P, N_GRP]), sb("rank_e", [P, N_EXP])
        base = sb("base", [P, N_EXP])
        slot_f = sb("slot_f", [P, 2, TT])
        slot_i = keep.slot_i
        token_f = sb("token_f", [P, TT])
        cnt = sb("cnt", [N_EXP, 1])
        blocks = sb("blocks", [N_EXP, 1])
        start, jump = sb("start", [P, N_EXP]), sb("jump", [P, N_EXP])
        ends, numbers = sb("ends", [1, N_EXP]), sb("numbers", [1, MAX_OVER])
        below, owner = sb("below", [1, MAX_OVER, N_EXP]), sb("owner", [1, MAX_OVER])
        zero_table = sb("zero_table", [BLOCKS, CAP])
        table = sb("table", [BLOCKS, CAP])

        h_here, rw_here = [sem(f"rh_here{t}") for t in range(TT)], sem("rw_here")
        h_turned, h_out, logits_ready, aff_ready = sem("h_turned"), sem("h_out"), sem("rlogits_ready"), sem("aff_ready")
        filled, step = sem("rfilled"), sem("rstep")
        sel_ready, counts_ready, blocks_ready, starts_ready = sem("sel_ready"), sem("counts_ready"), sem("blocks_ready"), sem("starts_ready")
        slots_ready, table_zero, scattered, table_here = sem("slots_ready"), sem("table_zero"), sem("scattered"), sem("table_here")
        table_turned, tokens_ready = sem("table_turned"), sem("tokens_ready")
        UNITS_H = TT * (DK // 4)

        with nc.Block() as block:
            @block.sync
            def _(sp):
                for t in range(TT):
                    sp.dma_start(h[:, t, :], scr.h1[t * P:(t + 1) * P, :]).then_inc(h_here[t], 16)
                    if t == 0:
                        sp.dma_start(rw[:], router_w.rearrange("(k p) n -> p k n", p=P)).then_inc(rw_here, 16)
                        sp.dma_start(rb_row[:], router_b.rearrange("(a n) -> a n", a=1)).then_inc(rw_here, 16)

            @block.tensor
            def _(pe):
                for u in range(UNITS_H):
                    t, g = u // (DK // 4), u % (DK // 4)
                    pe.wait_ge(h_here[t], 16)
                    if u >= 4:
                        pe.wait_ge(h_out, u - 3)
                    for j in range(4):
                        last = pe.transpose(turn[u % 4][:, j * P:(j + 1) * P], h[:, t, (4 * g + j) * P:(4 * g + j + 1) * P], k.ident[:])
                    last.then_inc(h_turned, 1)
                pe.wait_ge(rw_here, 32)
                pe.matmul(misc_bank[:, 0:N_EXP], k.ones[0:1, :], rb_row[:], start=True, stop=True)
                pe.wait_ge(h_out, UNITS_H)
                for t in range(TT):
                    for kt in range(DK):
                        last = pe.matmul(logit_bank[:, t * N_EXP:(t + 1) * N_EXP], keep.hT[:, kt, t * P:(t + 1) * P], rw[:, kt, :],
                                         start=(kt == 0), stop=(kt == DK - 1))
                last.then_inc(logits_ready, 1)
                pe.wait_ge(sel_ready, 1)
                for t in range(TT):
                    for s in range(t + 1):
                        pe.matmul(rank_bank[:, t * N_EXP:(t + 1) * N_EXP], (k.strict if s == t else k.ones)[:], sel[:, s, :],
                                  start=(s == 0), stop=(s == t))
                for t in range(TT):
                    last = pe.matmul(count_bank[0:N_EXP, 0:1], sel[:, t, :], k.ones[:, 0:1], start=(t == 0), stop=(t == TT - 1))
                last.then_inc(counts_ready, 1)
                pe.wait_ge(blocks_ready, 1)
                own = blocks[:, 0:1].broadcast_to((N_EXP, P))
                pe.matmul(misc_bank[:, 0:N_EXP], own, k.strict[0:N_EXP, 0:N_EXP], start=True, stop=True)
                pe.matmul(misc_bank[0:1, N_EXP:2 * N_EXP], blocks[:, 0:1], k.upto[0:N_EXP, 0:N_EXP], start=True, stop=True).then_inc(starts_ready, 1)
                pe.wait_ge(table_here, 16)
                pe.transpose(turn[0][0:CAP, 0:BLOCKS], table[:], k.ident[0:BLOCKS, 0:BLOCKS]).then_inc(table_turned, 1)

            @block.scalar
            def _(act):
                for u in range(UNITS_H):
                    t, g = u // (DK // 4), u % (DK // 4)
                    act.wait_ge(h_turned, u + 1)
                    act.activation(keep.hT[:, 4 * g:4 * g + 4, t * P:(t + 1) * P],
                                   turn[u % 4][:, :].rearrange("p (j n) -> p j n", j=4), ACT.Copy).then_inc(h_out, 1)
                act.wait_ge(logits_ready, 1)
                act.activation(aff[:], logit_bank[:, 0:TT * N_EXP].rearrange("p (t n) -> p t n", t=TT), ACT.Sigmoid).then_inc(aff_ready, 1)

            @block.vector
            def _(dve):
                count = [0]

                def link(ins):
                    count[0] += 1
                    ins.then_inc(step, 1)
                    dve.wait_ge(step, count[0])

                def tt(out, a, b, op):
                    link(dve.tensor_tensor(out, a, b, op))

                def last_max(values, weights, out, n):
                    every = (P, TT, n)
                    link(dve.tensor_reduce(best[:], values, AX.X, ALU.max))
                    tt(out, values, best[:].unsqueeze(2).broadcast_to(every), ALU.is_equal)
                    tt(out, out, weights.unsqueeze(1).broadcast_to(every), ALU.mult)
                    link(dve.tensor_reduce(key[:], out, AX.X, ALU.max))
                    tt(out, out, key[:].unsqueeze(2).broadcast_to(every), ALU.is_equal)

                dve.wait_ge(aff_ready, 1)
                dve.wait_ge(filled, 7)
                tt(biased[:], aff[:], misc_bank[:, 0:N_EXP].unsqueeze(1).broadcast_to((P, TT, N_EXP)), ALU.add)
                a, b, c, d = (biased[:].rearrange("p t (g n) -> p t g n", n=PER_GRP)[:, :, :, j] for j in range(PER_GRP))
                tt(hi1[:], a, b, ALU.max)
                tt(lo1[:], a, b, ALU.min)
                tt(hi2[:], c, d, ALU.max)
                tt(lo2[:], c, d, ALU.min)
                tt(gs[:], hi1[:], hi2[:], ALU.max)
                tt(hi1[:], hi1[:], hi2[:], ALU.min)
                tt(lo1[:], lo1[:], lo2[:], ALU.max)
                tt(hi1[:], hi1[:], lo1[:], ALU.max)
                tt(gs[:], gs[:], hi1[:], ALU.add)
                last_max(gs[:], rank_g[:], in_grp[:], N_GRP)
                link(dve.tensor_scalar(pen[:], in_grp[:], -1.0, -NEG, ALU.add, ALU.mult))
                four = lambda v: v.rearrange("p t g -> p (t g)").unsqueeze(2).broadcast_to((P, TT * N_GRP, PER_GRP))
                by_four = lambda v: v.rearrange("p t (g n) -> p (t g) n", n=PER_GRP)
                tt(by_four(masked[:]), by_four(biased[:]), four(in_grp[:]), ALU.mult)
                tt(by_four(masked[:]), by_four(masked[:]), four(pen[:]), ALU.add)
                for n in range(2):
                    last_max(masked[:], rank_e[:], hot[n][:], N_EXP)
                    if n == 0:
                        link(dve.scalar_tensor_tensor(out=masked[:], in0=hot[0][:], scalar=2 * NEG, in1=masked[:],
                                                      op0=ALU.mult, op1=ALU.add))
                    tt(eq[:], aff[:], hot[n][:], ALU.mult)
                    link(dve.tensor_reduce(keep.gate[:, n, :], eq[:], AX.X, ALU.add))
                dve.tensor_tensor(sel[:], hot[0][:], hot[1][:], ALU.add).then_inc(sel_ready, 1)
                tt(gate_sum[:], keep.gate[:, 0, :], keep.gate[:, 1, :], ALU.add)
                link(dve.reciprocal(gate_sum[:], gate_sum[:]))
                tt(keep.gate[:], keep.gate[:], gate_sum[:].unsqueeze(1).broadcast_to((P, 2, TT)), ALU.mult)
                dve.wait_ge(counts_ready, 1)
                link(dve.tensor_copy(cnt[:], count_bank[0:N_EXP, 0:1]))
                link(dve.tensor_scalar(blocks[:], cnt[:], float(CAP), None, ALU.is_gt))
                for j in range(2, SEQ // CAP):
                    link(dve.scalar_tensor_tensor(out=blocks[:], in0=cnt[:], scalar=float(j * CAP), in1=blocks[:],
                                                  op0=ALU.is_gt, op1=ALU.add))
                dve.sem_inc(blocks_ready, 1)
                dve.wait_ge(starts_ready, 1)
                link(dve.tensor_scalar(start[:], misc_bank[:, 0:N_EXP], float(CAP), float(CAP * (N_EXP - 1)), ALU.mult, ALU.add))
                tt(jump[:], start[:], base[:], ALU.subtract)
                link(dve.tensor_copy(ends[:], misc_bank[0:1, N_EXP:2 * N_EXP]))
                rank = rank_bank[:, 0:TT * N_EXP].rearrange("p (t n) -> p t n", t=TT)
                every = (P, TT, N_EXP)
                link(dve.tensor_scalar(over[:], rank, float(CAP), None, ALU.is_ge))
                tt(over[:], over[:], jump[:].unsqueeze(1).broadcast_to(every), ALU.mult)
                tt(over[:], over[:], base[:].unsqueeze(1).broadcast_to(every), ALU.add)
                tt(dest[:], rank, over[:], ALU.add)
                for n in range(2):
                    tt(eq[:], dest[:], hot[n][:], ALU.mult)
                    link(dve.tensor_reduce(slot_f[:, n, :], eq[:], AX.X, ALU.add))
                dve.tensor_copy(slot_i[:], slot_f[:]).then_inc(slots_ready, 1)
                tt(below[:], ends[:].unsqueeze(1).broadcast_to((1, MAX_OVER, N_EXP)),
                   numbers[:].unsqueeze(2).broadcast_to((1, MAX_OVER, N_EXP)), ALU.is_le)
                link(dve.tensor_reduce(owner[:], below[:], AX.X, ALU.add))
                link(dve.tensor_scalar(owner[:], owner[:], float(N_EXP - 1), None, ALU.min))
                link(dve.tensor_copy(keep.over_info[:, 1:1 + MAX_OVER], owner[:]))
                link(dve.tensor_copy(keep.over_info[:, 0:1], ends[:, N_EXP - 1:N_EXP]))
                dve.wait_ge(table_turned, 1)
                dve.tensor_copy(keep.slot_token[:], turn[0][0:CAP, 0:BLOCKS]).then_inc(tokens_ready, 1)

            @block.gpsimd
            def _(pool):
                pool.memset(zero_table[:], 0.0).then_inc(filled, 1)
                iota = lambda out, pattern, base, mult: pool.iota(out, pattern, base=base, channel_multiplier=mult,
                                                                 allow_small_or_imprecise_dtypes=True).then_inc(filled, 1)
                iota(rank_g[:], [[-1, N_GRP]], N_GRP, 0)
                iota(rank_e[:], [[-1, N_EXP]], N_EXP, 0)
                iota(base[:], [[CAP, N_EXP]], 0, 0)
                iota(token_f[:], [[P, TT]], 0, 1)
                iota(numbers[:], [[1, MAX_OVER]], 0, 0)
                pool.memset(keep.over_info[:], 0).then_inc(filled, 1)
                pool.wait_ge(filled, 7)
                pool.dma_start(scr.table.rearrange("(b s) o -> b (s o)", s=CAP), zero_table[:]).then_inc(table_zero, 16)
                pool.wait_ge(table_zero, 16)
                pool.wait_ge(slots_ready, 1)
                for n in range(2):
                    for t in range(TT):
                        pool.indirect_dma_start(out=scr.table, out_offset=bass.IndirectOffsetOnAxis(ap=slot_i[:, n, t:t + 1], axis=0),
                                                in_=token_f[:, t:t + 1], in_offset=None).then_inc(scattered, 16)
                pool.wait_ge(scattered, 16 * 2 * TT)
                pool.dma_start(table[:], scr.table.rearrange("(b s) o -> b (s o)", s=CAP)).then_inc(table_here, 16)

GU_CHUNKS, DN_CHUNKS = 4, 2
KG = DK // GU_CHUNKS
FT = D_FF // P
DN_W = D // DN_CHUNKS
PAIRS = N_EXP // 2
UW = D // PAIRS
KP = PLE // P
HALF_X = DK // 2


def run_moe(nc, k, p, w_gate, w_up, w_down, ple_w, ple_gate_w, scr, keep):
    wg, wu, wd = w_gate[0], w_up[0], w_down[0]
    with ExitStack() as ctx:
        def sb(name, shape, dt=FP32):
            return ctx.enter_context(nc.sbuf_tensor(name, shape, dt))

        def sem(name):
            return k.semaphore(name)

        banks = [ctx.enter_context(nc.psum_tensor(f"mbank{i}", [P, PW], FP32)) for i in range(8)]
        turn, hid, turned_hid, down, gate_bank, emb_bank = banks[0:2], banks[2], banks[3], banks[4:6], banks[6], banks[7]
        gu = [sb(f"gu{j}", [P, 2, KG, D_FF]) for j in range(GU_CHUNKS)]
        dn = [sb(f"dn{j}", [P, FT, DN_W]) for j in range(DN_CHUNKS)]
        pg = sb("pg", [P, DK, UW])
        pw = sb("pw", [P, KP, UW])
        pT = sb("pT", [P, KP, SEQ])
        p_in = sb("p_in", [P, TT, PLE])
        h_cols = sb("h_cols", [P, TT, UW])
        sig_emb = sb("sig_emb", [P, TT, UW])
        xg = [sb(f"xg{i}", [CAP, D]) for i in range(2)]
        xT = [sb(f"xT{i}", [P, DK, CAP]) for i in range(2)]
        act_sig = [sb(f"act_sig{i}", [P, FT, CAP]) for i in range(2)]
        hid_sb = [sb(f"hid_sb{i}", [P, FT, CAP]) for i in range(2)]
        both_sb = sb("both_sb", [P, D_FF])
        y_out = [sb(f"y_out{i}", [P, 2, PW]) for i in range(2)]
        token = [sb(f"token{i}", [CAP, 1], I32) for i in range(2)]

        gu_here = [sem(f"gu_here{j}") for j in range(GU_CHUNKS)]
        dn_here = [sem(f"dn_here{j}") for j in range(DN_CHUNKS)]
        gu_used = sem("gu_used")
        p_here, p_turned, p_out = sem("p_here"), sem("p_turned"), sem("p_out")
        emb_here, emb_used, emb_mid, gate_ready, emb_ready = sem("emb_here"), sem("emb_used"), sem("emb_mid"), sem("gate_ready"), sem("emb_ready")
        emb_sig, emb_step, emb_done, emb_stored = sem("emb_sig"), sem("emb_step"), sem("emb_done"), sem("emb_stored")
        token_ready = sem("token_ready")
        x_here = [sem(f"mx_here{i}") for i in range(2)]
        x_turned, x_out = sem("mx_turned"), sem("mx_out")
        hid_ready, sig_ready, half_ready, act_ready = sem("hid_ready"), sem("sig_ready"), sem("half_ready"), sem("act_ready")
        down_ready, y_out_ready = sem("down_ready"), sem("y_out_ready")
        y_stored = [sem(f"my_stored{i}") for i in range(2)]

        def gu_source(e, j):
            rows = slice(j * KG * P, (j + 1) * KG * P)
            return [v[e, rows, :].rearrange("(k p) n -> p k n", p=P) for v in (wg, wu)]

        def dn_source(e, j):
            return wd[e, :, j * DN_W:(j + 1) * DN_W].rearrange("(f p) n -> p f n", p=P)

        def turn_x(pe, i, done, free=None):
            for half in range(2):
                if free is not None:
                    pe.wait_ge(x_out, free + half)
                pe.sem_inc(mpassed_pe, 1)
                for j in range(HALF_X):
                    kt = half * HALF_X + j
                    last = pe.transpose(turn[half][:, j * CAP:(j + 1) * CAP], xg[i][:, kt * P:(kt + 1) * P], k.ident[0:CAP, 0:CAP])
                last.then_inc(done, 1)

        def hidden(pe, i, j):
            for kk in range(KG):
                kt = j * KG + kk
                for side in range(2):
                    last = pe.matmul(hid[side * CAP:(side + 1) * CAP, :], xT[i][:, kt, :], gu[j][:, side, kk, :],
                                     start=(kt == 0), stop=(kt == DK - 1))
            return last

        def turn_hidden(pe):
            for f in range(FT):
                last = pe.transpose(turned_hid[:, f * P:(f + 1) * P], both_sb[:, f * P:(f + 1) * P], k.ident[:])
            return last

        def down_product(pe, i, b):
            for f in range(FT):
                for half in range(2):
                    last = pe.matmul(down[b][half * CAP:(half + 1) * CAP, :], hid_sb[i][:, f, :],
                                     dn[b][:, f, half * PW:(half + 1) * PW], start=(f == 0), stop=(f == FT - 1))
            return last

        def token_copy(dve, i, block, done):
            dve.tensor_copy(token[i][:], keep.slot_token[:, bass.ds(block, 1)] if not isinstance(block, int)
                            else keep.slot_token[:, block:block + 1]).then_inc(done, 1)

        def x_from_psum(act, i, half, done):
            act.activation(xT[i][:, half * HALF_X:(half + 1) * HALF_X, :],
                           turn[half][:, :].rearrange("p (k n) -> p k n", n=CAP), ACT.Copy).then_inc(done, 1)

        turned = turned_hid[:, :].rearrange("p (f n) -> p f n", n=P)
        gate_turned, up_turned = turned[:, :, 0:CAP], turned[:, :, CAP:2 * CAP]
        hid_out, hid_turned, ov_hid_out, ov_hid_turned = (sem(n) for n in ("hid_out", "hid_turned", "ov_hid_out", "ov_hid_turned"))
        ov_here, ov_token, ov_x, ov_turned, ov_x_out = (sem(n) for n in ("ov_here", "ov_token", "ov_x", "ov_turned", "ov_x_out"))
        ov_hidden, ov_sig, ov_half, ov_act = (sem(n) for n in ("ov_hidden", "ov_sig", "ov_half", "ov_act"))
        ov_down, ov_y_out, ov_stored = (sem(n) for n in ("ov_down", "ov_y_out", "ov_stored"))
        mpassed_pe, mpassed_pool = sem("mpassed_pe"), sem("mpassed_pool")
        OV_DMAS = 2 * GU_CHUNKS + DN_CHUNKS

        def blocks_beyond(eng):
            return eng.value_load(keep.over_info[0:1, 0:1], min_val=0, max_val=MAX_OVER)

        with nc.Block() as block:
            @block.sync
            def _(sp):
                sp.dma_start(p_in[:], p[0, 0].rearrange("(t p) n -> p t n", p=P)).then_inc(p_here, 16)

                def gate_and_up(e):
                    for j in range(GU_CHUNKS):
                        sp.wait_ge(gu_used, GU_CHUNKS * e + j + 1)
                        for side, src in enumerate(gu_source(e, j)):
                            sp.dma_start(gu[j][:, side], src).then_inc(gu_here[j], 16)

                def down_weights(e):
                    for j in range(DN_CHUNKS):
                        sp.wait_ge(down_ready, DN_CHUNKS * e + j + 1)
                        sp.dma_start(dn[j][:], dn_source(e, j)).then_inc(dn_here[j], 16)

                def embedding(n):
                    sp.wait_ge(emb_used, n + 1)
                    cols = bass.ds(n * UW, UW)
                    sp.dma_start(pg[:], ple_gate_w[0].rearrange("(k p) n -> p k n", p=P)[:, :, cols]).then_inc(emb_here, 16)
                    sp.dma_start(pw[:], ple_w[0].rearrange("(k p) n -> p k n", p=P)[:, :, cols]).then_inc(emb_here, 16)

                with sp.Fori(0, PAIRS) as n:
                    gate_and_up(2 * n)
                    embedding(n)
                    down_weights(2 * n)
                    gate_and_up(2 * n + 1)
                    down_weights(2 * n + 1)

                over = blocks_beyond(sp)
                with sp.If(over > 0):
                    with sp.Fori(0, over) as b:
                        sp.wait_ge(ov_down, DN_CHUNKS * b + 1)
                        e = sp.value_load(keep.over_info[0:1, bass.ds(b + 1, 1)], min_val=0, max_val=N_EXP - 1)
                        for j in range(GU_CHUNKS):
                            for side, v in enumerate((w_gate, w_up)):
                                sp.dma_start(gu[j][:, side], v[0, bass.ds(e, 1), j * KG * P:(j + 1) * KG * P, :]
                                             .rearrange("a (k p) n -> p (a k) n", p=P)).then_inc(ov_here, 16)
                        for j in range(DN_CHUNKS):
                            sp.dma_start(dn[j][:], w_down[0, bass.ds(e, 1), :, j * DN_W:(j + 1) * DN_W]
                                         .rearrange("a (f p) n -> p (a f) n", p=P)).then_inc(ov_here, 16)

            @block.tensor
            def _(pe):
                pe.sem_inc(gu_used, GU_CHUNKS)
                pe.sem_inc(down_ready, DN_CHUNKS)
                pe.sem_inc(emb_used, 1)
                pe.wait_ge(p_here, 16)
                for t in range(TT):
                    for j in range(KP):
                        b = banks[6 + j]
                        last = pe.transpose(b[:, t * P:(t + 1) * P], p_in[:, t, j * P:(j + 1) * P], k.ident[:])
                last.then_inc(p_turned, 1)
                pe.wait_ge(p_out, KP)
                pe.wait_ge(x_here[0], 16)
                turn_x(pe, 0, x_turned)

                def embedding(n, half):
                    if half == 0:
                        pe.wait_ge(emb_here, 32 * (n + 1))
                        pe.wait_ge(emb_done, n + 1)
                    for t in range(half * TT // 2, (half + 1) * TT // 2):
                        for kt in range(DK):
                            last = pe.matmul(gate_bank[:, t * UW:(t + 1) * UW], keep.hT[:, kt, t * P:(t + 1) * P], pg[:, kt, :],
                                             start=(kt == 0), stop=(kt == DK - 1))
                    if half:
                        last.then_inc(gate_ready, 1)
                        for t in range(TT):
                            for kt in range(KP):
                                last = pe.matmul(emb_bank[:, t * UW:(t + 1) * UW], pT[:, kt, t * P:(t + 1) * P], pw[:, kt, :],
                                                 start=(kt == 0), stop=(kt == KP - 1))
                        last.then_inc(emb_used, 1)

                with pe.Fori(0, PAIRS) as n:
                    for i in range(2):
                        e = 2 * n + i
                        for j in range(GU_CHUNKS):
                            pe.wait_ge(gu_here[j], 32 * (e + 1))
                            if j == 0:
                                pe.wait_ge(x_out, 2 * (e + 1))
                                pe.wait_ge(hid_out, e + 1)
                            last = hidden(pe, i, j)
                            last.then_inc(gu_used, 1)
                        pe.wait_ge(hid_out, 1 + e + 1)
                        pe.wait_ge(act_ready, e + 1)
                        turn_hidden(pe).then_inc(hid_turned, 1)
                        embedding(n, i)
                        pe.wait_ge(x_here[1 - i], 16 * (n + 1 + i))
                        turn_x(pe, 1 - i, x_turned, free=2 * e + 1)
                        pe.wait_ge(act_ready, 1 + e + 1)
                        for b in range(DN_CHUNKS):
                            pe.wait_ge(dn_here[b], 16 * (e + 1))
                            pe.wait_ge(y_out_ready, 2 * e + b + 1)
                            down_product(pe, i, b).then_inc(down_ready, 1)

                pe.wait_ge(down_ready, DN_CHUNKS * (N_EXP + 1))
                pe.wait_ge(y_out_ready, DN_CHUNKS * (N_EXP + 1))
                pe.wait_ge(x_out, 2 * (N_EXP + 1))
                pe.sem_inc(ov_down, 1)
                over = blocks_beyond(pe)
                with pe.If(over > 0):
                    with pe.Fori(0, over) as b:
                        pe.wait_ge(ov_x, 16 * (b + 1))
                        turn_x(pe, 0, ov_turned)
                        pe.wait_ge(ov_here, 16 * OV_DMAS * (b + 1))
                        pe.wait_ge(ov_x_out, 2 * (b + 1))
                        for j in range(GU_CHUNKS):
                            last = hidden(pe, 0, j)
                        last.then_inc(ov_hidden, 1)
                        pe.wait_ge(ov_hid_out, b + 1)
                        turn_hidden(pe).then_inc(ov_hid_turned, 1)
                        pe.wait_ge(ov_act, b + 1)
                        for c in range(DN_CHUNKS):
                            pe.wait_ge(ov_y_out, DN_CHUNKS * b + c + 1)
                            down_product(pe, 0, c).then_inc(ov_down, 1)

            @block.scalar
            def _(act):
                act.sem_inc(y_out_ready, DN_CHUNKS)
                act.sem_inc(hid_out, 1)
                act.sem_inc(ov_y_out, DN_CHUNKS)
                act.wait_ge(p_turned, 1)
                for j in range(KP):
                    act.activation(pT[:, j, :], banks[6 + j][:], ACT.Copy).then_inc(p_out, 1)
                for half in range(2):
                    act.wait_ge(x_turned, half + 1)
                    act.activation(xT[0][:, half * HALF_X:(half + 1) * HALF_X, :],
                                   turn[half][:, :].rearrange("p (k n) -> p k n", n=CAP), ACT.Copy).then_inc(x_out, 1)
                with act.Fori(0, PAIRS) as n:
                    for i in range(2):
                        e = 2 * n + i
                        act.wait_ge(gu_used, GU_CHUNKS * (e + 2))
                        act.activation(both_sb[:], hid[:], ACT.Copy).then_inc(hid_out, 1)
                        act.wait_ge(hid_turned, e + 1)
                        act.activation(act_sig[i][:], gate_turned, ACT.Sigmoid).then_inc(sig_ready, 1)
                        if i:
                            act.wait_ge(gate_ready, n + 1)
                            act.activation(sig_emb[:], gate_bank[:, :].rearrange("p (t n) -> p t n", n=UW), ACT.Sigmoid).then_inc(emb_sig, 1)
                        for half in range(2):
                            act.wait_ge(x_turned, 2 * (e + 1) + half + 1)
                            act.activation(xT[1 - i][:, half * HALF_X:(half + 1) * HALF_X, :],
                                           turn[half][:, :].rearrange("p (k n) -> p k n", n=CAP), ACT.Copy).then_inc(x_out, 1)
                        for b in range(DN_CHUNKS):
                            act.wait_ge(down_ready, DN_CHUNKS * (e + 1) + b + 1)
                            act.activation(y_out[i][:, b, :], down[b][:], ACT.Copy).then_inc(y_out_ready, 1)
                over = blocks_beyond(act)
                with act.If(over > 0):
                    with act.Fori(0, over) as b:
                        for half in range(2):
                            act.wait_ge(ov_turned, 2 * b + half + 1)
                            x_from_psum(act, 0, half, ov_x_out)
                        act.wait_ge(ov_hidden, b + 1)
                        act.activation(both_sb[:], hid[:], ACT.Copy).then_inc(ov_hid_out, 1)
                        act.wait_ge(ov_hid_turned, b + 1)
                        act.activation(act_sig[0][:], gate_turned, ACT.Sigmoid).then_inc(ov_sig, 1)
                        for c in range(DN_CHUNKS):
                            act.wait_ge(ov_down, 1 + DN_CHUNKS * b + c + 1)
                            act.activation(y_out[0][:, c, :], down[c][:], ACT.Copy).then_inc(ov_y_out, 1)

            @block.vector
            def _(dve):
                dve.sem_inc(act_ready, 1)
                dve.sem_inc(emb_done, 1)
                token_copy(dve, 0, 0, token_ready)
                with dve.Fori(0, PAIRS) as n:
                    for i in range(2):
                        e = 2 * n + i
                        dve.wait_ge(x_turned, 2 * (e + 1))
                        token_copy(dve, 1 - i, e + 1, token_ready)
                        dve.wait_ge(sig_ready, e + 1)
                        dve.tensor_tensor(act_sig[i][:], gate_turned, act_sig[i][:], ALU.mult).then_inc(half_ready, 1)
                        dve.wait_ge(half_ready, e + 1)
                        dve.tensor_tensor(hid_sb[i][:], up_turned, act_sig[i][:], ALU.mult).then_inc(act_ready, 1)
                        if i:
                            dve.wait_ge(emb_sig, n + 1)
                            dve.wait_ge(emb_used, 1 + n + 1)
                            emb = emb_bank[:, :].rearrange("p (t n) -> p t n", n=UW)
                            dve.tensor_tensor(sig_emb[:], emb, sig_emb[:], ALU.mult).then_inc(emb_step, 1)
                            dve.wait_ge(emb_step, n + 1)
                            dve.wait_ge(emb_mid, 16 * (n + 1))
                            dve.scalar_tensor_tensor(out=h_cols[:], in0=h_cols[:], scalar=ALPHA, in1=sig_emb[:],
                                                     op0=ALU.mult, op1=ALU.add).then_inc(emb_done, 1)
                over = blocks_beyond(dve)
                with dve.If(over > 0):
                    with dve.Fori(0, over) as b:
                        dve.wait_ge(ov_down, DN_CHUNKS * b + 1)
                        token_copy(dve, 0, b + N_EXP, ov_token)
                        dve.wait_ge(ov_sig, b + 1)
                        dve.tensor_tensor(act_sig[0][:], gate_turned, act_sig[0][:], ALU.mult).then_inc(ov_half, 1)
                        dve.wait_ge(ov_half, b + 1)
                        dve.tensor_tensor(hid_sb[0][:], up_turned, act_sig[0][:], ALU.mult).then_inc(ov_act, 1)

            @block.gpsimd
            def _(pool):
                def gather(i, done):
                    pool.sem_inc(mpassed_pool, 1)
                    pool.indirect_dma_start(out=xg[i][:], out_offset=None, in_=scr.h1,
                                            in_offset=bass.IndirectOffsetOnAxis(ap=token[i][:, 0:1], axis=0)).then_inc(done, 16)

                def store(i, block, done):
                    pool.sem_inc(mpassed_pool, 1)
                    rows = scr.yb[bass.ds(block * CAP, CAP), :].rearrange("r (b h n) -> h r b n", h=2, n=PW)
                    for half in range(2):
                        pool.dma_start(rows[half], y_out[i][half * CAP:(half + 1) * CAP]).then_inc(done, 16)

                pool.wait_ge(token_ready, 1)
                gather(0, x_here[0])
                with pool.Fori(0, PAIRS) as n:
                    cols = bass.ds(n * UW, UW)
                    pool.dma_start(h_cols[:], scr.h1.rearrange("(t p) n -> p t n", p=P)[:, :, cols]).then_inc(emb_mid, 16)
                    for i in range(2):
                        e = 2 * n + i
                        pool.wait_ge(token_ready, 1 + e + 1)
                        pool.wait_ge(x_turned, 2 * (e + 1))
                        gather(1 - i, x_here[1 - i])
                        pool.wait_ge(y_out_ready, DN_CHUNKS * (e + 2))
                        store(i, e, y_stored[i])
                        pool.wait_ge(y_stored[i], 32 * (n + 1))
                    pool.wait_ge(emb_done, 1 + n + 1)
                    pool.sem_inc(mpassed_pool, 1)
                    pool.dma_start(scr.res.rearrange("(t p) n -> p t n", p=P)[:, :, cols], h_cols[:]).then_inc(emb_stored, 16)
                    pool.wait_ge(emb_stored, 16 * (n + 1))
                over = blocks_beyond(pool)
                with pool.If(over > 0):
                    with pool.Fori(0, over) as b:
                        pool.wait_ge(ov_token, b + 1)
                        gather(0, ov_x)
                        pool.wait_ge(ov_y_out, DN_CHUNKS * (b + 2))
                        store(0, b + N_EXP, ov_stored)
                        pool.wait_ge(ov_stored, 32 * (b + 1))


def run_result(nc, k, ln_g, ln_b, scr, keep, out):
    with ExitStack() as ctx:
        def sb(name, shape, dt=FP32):
            return ctx.enter_context(nc.sbuf_tensor(name, shape, dt))

        def sem(name):
            return k.semaphore(name)

        banks = [ctx.enter_context(nc.psum_tensor(f"fbank{i}", [P, PW], FP32)) for i in range(8)]
        rows = sb("fgain_rows", [1, 2, D])
        gain = sb("fgain", [P, 2, D])
        res = sb("fres", [P, TT, D])
        y = [sb(f"fy{n}", [P, 2, D]) for n in range(2)]
        stats = sb("fstats", [P, TT, D // PW, 6])
        mv, rstd, shift = sb("fmv", [P, TT, 2]), sb("frstd", [P, TT]), sb("fshift", [P, TT])
        rows_here, gain_ready, gain_out = sem("frows_here"), sem("fgain_ready"), sem("fgain_out")
        res_here = [sem(f"res_here{t}") for t in range(TT)]
        y_here = [sem(f"fy_here{t}") for t in range(TT)]
        first_added, summed, stat_ready, mv_ready, var_ready = (sem(n) for n in ("first_added", "summed", "fstat_ready", "fmv_ready", "fvar_ready"))
        root_ready, rstd_ready, shift_ready, normed, gained, finished, out_stored = \
            (sem(n) for n in ("froot_ready", "frstd_ready", "fshift_ready", "fnormed", "fgained", "finished", "out_stored"))
        with nc.Block() as block:
            @block.sync
            def _(sp):
                sp.dma_start(rows[:, 0, :], ln_g).then_inc(rows_here, 16)
                sp.dma_start(rows[:, 1, :], ln_b).then_inc(rows_here, 16)
                for t in range(TT):
                    sp.dma_start(res[:, t, :], scr.res[t * P:(t + 1) * P, :]).then_inc(res_here[t], 16)
                for t in range(TT):
                    sp.wait_ge(finished, t + 1)
                    sp.dma_start(out[0, t * P:(t + 1) * P, :], res[:, t, :]).then_inc(out_stored, 16)
                sp.wait_ge(out_stored, 16 * TT)

            @block.tensor
            def _(pe):
                pe.wait_ge(rows_here, 32)
                for j in range(8):
                    last = pe.matmul(banks[j][:], k.ones[0:1, :], rows[:, j // 4, (j % 4) * PW:(j % 4 + 1) * PW], start=True, stop=True)
                last.then_inc(gain_ready, 1)

            @block.gpsimd
            def _(pool):
                for t in range(TT):
                    if t >= 2:
                        pool.wait_ge(summed, t - 1)
                    for n in range(2):
                        pool.indirect_dma_start(out=y[n][:, t % 2, :], out_offset=None, in_=scr.yb,
                                                in_offset=bass.IndirectOffsetOnAxis(ap=keep.slot_i[:, n, t:t + 1], axis=0)).then_inc(y_here[t], 16)
                for t in range(TT):
                    pool.wait_ge(gained, t + 1)
                    pool.tensor_tensor(res[:, t, :], res[:, t, :], gain[:, 1, :], ALU.add).then_inc(finished, 1)

            @block.scalar
            def _(act):
                act.wait_ge(gain_ready, 1)
                for j in range(8):
                    act.activation(gain[:, j // 4, (j % 4) * PW:(j % 4 + 1) * PW], banks[j][:], ACT.Copy).then_inc(gain_out, 1)
                for t in range(TT):
                    act.wait_ge(var_ready, t + 1)
                    act.activation(rstd[:, t:t + 1], rstd[:, t:t + 1], ACT.Sqrt).then_inc(root_ready, 1)
                    act.wait_ge(shift_ready, t + 1)
                    act.activation(res[:, t, :], res[:, t, :], ACT.Identity, bias=shift[:, t:t + 1], scale=rstd[:, t:t + 1]).then_inc(normed, 1)

            @block.vector
            def _(dve):
                def normalised(t):
                    dve.wait_ge(gain_out, 8)
                    dve.wait_ge(normed, t + 1)
                    dve.tensor_tensor(res[:, t, :], res[:, t, :], gain[:, 0, :], ALU.mult).then_inc(gained, 1)

                for t in range(TT):
                    dve.wait_ge(res_here[t], 16)
                    dve.wait_ge(y_here[t], 32)
                    dve.scalar_tensor_tensor(out=res[:, t, :], in0=y[0][:, t % 2, :], scalar=keep.gate[:, 0, t:t + 1], in1=res[:, t, :],
                                             op0=ALU.mult, op1=ALU.add).then_inc(first_added, 1)
                    dve.wait_ge(first_added, t + 1)
                    dve.scalar_tensor_tensor(out=res[:, t, :], in0=y[1][:, t % 2, :], scalar=keep.gate[:, 1, t:t + 1], in1=res[:, t, :],
                                             op0=ALU.mult, op1=ALU.add).then_inc(summed, 1)
                    dve.wait_ge(summed, t + 1)
                    for j in range(D // PW):
                        dve.bn_stats(stats[:, t, j, :], res[:, t, j * PW:(j + 1) * PW]).then_inc(stat_ready, 1)
                    dve.wait_ge(stat_ready, (D // PW) * (t + 1))
                    dve.bn_aggr(mv[:, t, :], stats[:, t, :, :].rearrange("p a b -> p (a b)")).then_inc(mv_ready, 1)
                    dve.wait_ge(mv_ready, t + 1)
                    dve.tensor_scalar(rstd[:, t:t + 1], mv[:, t, 1:2], EPS, None, ALU.add).then_inc(var_ready, 1)
                    dve.wait_ge(root_ready, t + 1)
                    dve.reciprocal(rstd[:, t:t + 1], rstd[:, t:t + 1]).then_inc(rstd_ready, 1)
                    dve.wait_ge(rstd_ready, t + 1)
                    dve.scalar_tensor_tensor(out=shift[:, t:t + 1], in0=mv[:, t, 0:1], scalar=-1.0, in1=rstd[:, t:t + 1],
                                             op0=ALU.mult, op1=ALU.mult).then_inc(shift_ready, 1)
                    if t:
                        normalised(t - 1)
                normalised(TT - 1)


def decoder_layer(nc, x, p, w_in, conv_w, conv_b, dt_bias, a_log, d_skip, ssm_norm_w, idx_k_norm_g, idx_k_norm_b, w_out,
                  ln1_g, ln1_b, router_w, router_b, w_gate, w_up, w_down, ple_w, ple_gate_w, ln2_g, ln2_b, out):
    scr, k, keep = Shared(), Shared(), Shared()

    def scratch(name, shape):
        return nc.dram_tensor(f"scratch_{name}", shape, FP32).ap()

    scr.qkT, scr.iqT, scr.v = scratch("qkT", [2 * AH * AD, SEQ]), scratch("iqT", [IH * ID, SEQ]), scratch("v", [SEQ, AH * AD])
    scr.zxT, scr.dt, scr.yT = scratch("zxT", [COL_DT, SEQ]), scratch("dt", [SEQ, HEADS]), scratch("yT", [D, SEQ])
    scr.h1, scr.res = scratch("h1", [SEQ, D]), scratch("res", [SEQ, D])
    scr.table, scr.yb = scratch("table", [BLOCKS * CAP, 1]), scratch("yb", [BLOCKS * CAP, D])
    with ExitStack() as ctx:
        def sb(name, shape, dt=FP32):
            return ctx.enter_context(nc.sbuf_tensor(name, shape, dt))

        taken = []

        def semaphore(name):
            taken.append(nc.alloc_semaphore(name=name))
            return taken[-1]

        def clear_semaphores():
            nc.clear_and_free_semaphores(taken)
            nc.all_engine_barrier()
            taken.clear()

        k.semaphore = semaphore
        k.ones, k.ident, k.strict, k.upto = sb("ones", [P, P]), sb("ident", [P, P]), sb("strict", [P, P]), sb("upto", [P, P])
        keep.gate, keep.slot_i = sb("gate", [P, 2, TT]), sb("slot_i", [P, 2, TT], I32)
        keep.over_info, keep.slot_token = sb("over_info", [1, 1 + MAX_OVER], I32), sb("slot_token", [CAP, BLOCKS], I32)
        with ExitStack() as own:
            k.causal_bias = own.enter_context(nc.sbuf_tensor("causal_bias", [P, SEQ], FP32))
            run_constants(nc, k)
            run_projection(nc, k, x, w_in, idx_k_norm_g, idx_k_norm_b, scr)
        run_ssd(nc, k, conv_w, conv_b, dt_bias, a_log, d_skip, ssm_norm_w, scr)
        clear_semaphores()
        with ExitStack() as own:
            keep.gain = own.enter_context(nc.sbuf_tensor("gain", [P, 2, D], FP32))
            keep.gain_rows = own.enter_context(nc.sbuf_tensor("gain_rows", [1, 2, D], FP32))
            run_output(nc, k, x, w_out, ln1_g, ln1_b, router_w, router_b, scr, keep)
        keep.hT = sb("hT", [P, DK, SEQ])
        run_router(nc, k, router_w, router_b, scr, keep)
        run_moe(nc, k, p, w_gate, w_up, w_down, ple_w, ple_gate_w, scr, keep)
        clear_semaphores()
        run_result(nc, k, ln2_g, ln2_b, scr, keep, out)


INPUTS = ["x", "p", "w_in", "conv_w", "conv_b", "dt_bias", "a_log", "d_skip", "ssm_norm_w", "idx_k_norm_g", "idx_k_norm_b",
          "w_out", "ln1_g", "ln1_b", "router_w", "router_b", "w_gate", "w_up", "w_down", "ple_w", "ple_gate_w", "ln2_g", "ln2_b"]


def kernel(**inputs):
    import numpy as np
    import concourse.bacc as bacc
    from concourse.bass_utils import run_bass_kernel_spmd

    nc = bacc.Bacc("TRN2", target_bir_lowering=False, num_devices=1)
    arrays, args = {}, []
    for name in INPUTS:
        a = np.ascontiguousarray(inputs[name])
        arrays[f"in_{name}"] = a
        args.append(nc.dram_tensor(f"in_{name}", a.shape, mybir.dt.from_np(a.dtype), kind="ExternalInput").ap())
    args.append(nc.dram_tensor("result", (1, SEQ, D), FP32, kind="ExternalOutput").ap())
    decoder_layer(nc, *args)
    r = run_bass_kernel_spmd(nc, [arrays], core_ids=[0])
    return r.results[0]["result"]
```

```python
import concourse.bass as bass
from concourse import mybir
from contextlib import ExitStack

FP32 = mybir.dt.float32
FP32R = mybir.dt.float32r
I32 = mybir.dt.int32
U32 = mybir.dt.uint32
ALU = mybir.AluOpType
ACT = mybir.ActivationFunctionType
AX = mybir.AxisListType


class Shared:
    pass


P = 128
SEQ, D = 512, 2048
TT = SEQ // P
DK = D // P
SSD_W, HD, HEADS, STATE, GROUPS = 1024, 64, 16, 128, 2
HPG = HEADS // GROUPS
CONV_TAPS = 4
CONV_DIM = SSD_W + 2 * GROUPS * STATE
AH, AD = 8, 128
IH, ID = 16, 64
TOPK = min(256, SEQ // 4)
N_EXP, N_GRP, PER_GRP = 32, 8, 4
D_FF = 512
PLE = 256
ALPHA = 2.0 ** 0.25
EPS = 1e-5

XT, CT = SSD_W // P, CONV_DIM // P
N_PAR = (CONV_TAPS + 1) * CT + 2 * XT

COL_Z = 0
COL_XBC = SSD_W
COL_DT = COL_XBC + CONV_DIM
COL_Q = COL_DT + HEADS
COL_V = COL_Q + 2 * AH * AD
COL_IQ = COL_V + AH * AD
COL_IK = COL_IQ + IH * ID
COL_IW = COL_IK + ID
SMALL = ID + IH + HEADS

PW = 512
CH = 4
KC = DK // CH
SPLIT_SLOTS = 2
NEG = -1.0e30
TAKEN = -3.0e38

IQ_PANELS, QK_PANELS, V_PANELS, ZX_PANELS = 2, 4, 2, 5
IH_PASS = IH // QK_PANELS
DOTS_FROM = 5
HEADS_PER_PANEL = 2
UNITS = HEADS_PER_PANEL * TT
SLOTS = UNITS + 2


def run_constants(nc, k):
    filled, shaped = (k.semaphore(n) for n in ("filled", "shaped"))
    with nc.Block() as block:
        @block.gpsimd
        def _(pool):
            pool.memset(k.ones[:], 1.0).then_inc(filled, 1)
            pool.memset(k.ident[:], 0.0).then_inc(filled, 1)
            pool.memset(k.strict[:], 1.0).then_inc(filled, 1)
            pool.memset(k.causal_bias[:], 0.0).then_inc(filled, 1)
            pool.wait_ge(filled, 4)
            pool.affine_select(out=k.ident[:], in_=k.ident[:], compare_op=ALU.not_equal, fill=1.0, base=0,
                               pattern=[[-1, P]], channel_multiplier=1).then_inc(shaped, 1)
            pool.affine_select(out=k.upto[:], in_=k.ones[:], compare_op=ALU.is_ge, fill=0.0, base=0,
                               pattern=[[1, P]], channel_multiplier=-1).then_inc(shaped, 1)
            pool.affine_select(out=k.strict[:], in_=k.strict[:], compare_op=ALU.is_gt, fill=0.0, base=0,
                               pattern=[[1, P]], channel_multiplier=-1).then_inc(shaped, 1)
            own = k.causal_bias[:, SEQ - P:SEQ]
            pool.affine_select(out=own, in_=own, compare_op=ALU.is_ge, fill=NEG, base=0,
                               pattern=[[-1, P]], channel_multiplier=1).then_inc(shaped, 1)
            pool.wait_ge(shaped, 4)


def run_projection(nc, k, x, w_in, idx_g, idx_b, conv_w, conv_b, dt_bias, a_log, d_skip, norm_w, scr):
    w = w_in[0]
    with ExitStack() as ctx:
        def sb(name, shape, dt=FP32):
            return ctx.enter_context(nc.sbuf_tensor(name, shape, dt))

        def sem(name):
            return k.semaphore(name)

        banks = [ctx.enter_context(nc.psum_tensor(f"bank{i}", [P, PW], FP32)) for i in range(8)]
        acc, side = banks[0:4], banks[4:8]
        xhi, xlo = sb("xhi", [P, DK, SEQ], FP32R), sb("xlo", [P, DK, SEQ], FP32R)
        raw = sb("raw", [P, CH, KC, PW])
        whi = [sb(f"whi{i}", [P, KC, PW], FP32R) for i in range(SPLIT_SLOTS)]
        wlo = [sb(f"wlo{i}", [P, KC, PW], FP32R) for i in range(SPLIT_SLOTS)]
        stage = sb("stage", [P, TT, PW])
        conved = sb("conved", [P, TT, PW])
        smallT = conved[0:SMALL, 0, :]
        par_rows, head_rows = sb("par_rows", [N_PAR, P]), sb("head_rows", [1, 2 * HEADS])
        skip2, skip_rows = sb("skip2", [XT, 2]), sb("skip_rows", [XT, P])
        taps = sb("taps", [P, CONV_TAPS + 1, TT])
        union = sb("union", [P, 2 * D])
        xin = [union[:, t * D:(t + 1) * D] for t in range(2)] + [raw[:, c].rearrange("p k n -> p (k n)") for c in (2, 3)]
        iq = union[:, 0:IH_PASS // 2 * SEQ].rearrange("p (h n) -> p h n", h=IH_PASS // 2)
        o = HEADS_PER_PANEL * SEQ
        qh = union[:, 0:o].rearrange("p (h n) -> p h n", h=HEADS_PER_PANEL)
        kh = union[:, o:2 * o].rearrange("p (h n) -> p h n", h=HEADS_PER_PANEL)
        vh = union[:, 2 * o:3 * o].rearrange("p (s n) -> p s n", s=TT)
        oh = union[:, 3 * o:4 * o].rearrange("p (h n) -> p h n", h=HEADS_PER_PANEL)
        wsm_raw = sb("wsm_raw", [P, DK, SMALL])
        wsm_hi, wsm_lo = sb("wsm_hi", [P, DK, SMALL], FP32R), sb("wsm_lo", [P, DK, SMALL], FP32R)
        small = sb("small", [P, TT, SMALL])
        iws, iws_pass = sb("iws", [P, TT, IH]), sb("iws_pass", [P, TT, IH_PASS])
        stats = sb("stats", [P, TT, 6])
        mv = sb("mv", [P, TT, 2])
        rstd = sb("rstd", [P, TT])
        ikn = sb("ikn", [P, TT, 2 * ID])
        gb = sb("gb", [P, 2])
        ikT = sb("ikT", [P, SEQ])
        relu = sb("relu", [P, 2, SEQ])
        score = [sb(f"score{q}", [P, P * (q + 1)]) for q in range(TT)]
        top8 = sb("top8", [P, 8])
        probs = sb("probs", [P, 2, SEQ])
        probsT = sb("probsT", [P, 2, SEQ])
        nmax = sb("nmax", [P, 2, 2])
        rowsum = sb("rowsum", [P, 2])

        x_here = [sem(f"x_here{t}") for t in range(TT)]
        x_turned, x_hi, x_lo = sem("x_turned"), sem("x_hi"), sem("x_lo")
        small_here, small_hi, small_lo, small_acc = sem("small_here"), sem("small_hi"), sem("small_lo"), sem("small_acc")
        small_turned, small_flat = sem("small_turned"), sem("small_flat")
        small_out, ikn_done, ik_turned, ik_ready = sem("small_out"), sem("ikn_done"), sem("ik_turned"), sem("ik_ready")
        raw_here = [sem(f"raw_here{c}") for c in range(CH)]
        hi_ready, split_ready, split_used = sem("hi_ready"), sem("split_ready"), sem("split_used")
        acc_ready, acc_taken = sem("acc_ready"), sem("acc_taken")
        stored = [sem(f"stored{t}") for t in range(TT)]
        iq_here, dots_ready, relu_ready, score_step = sem("iq_here"), sem("dots_ready"), sem("relu_ready"), sem("score_step")
        heads_here, heads_used = sem("heads_here"), sem("heads_used")
        logits_ready, logits_masked, max_ready = sem("logits_ready"), sem("logits_masked"), sem("max_ready")
        exp_ready, probs_ready, probs_turned = sem("exp_ready"), sem("probs_ready"), sem("probs_turned")
        probsT_ready, pv_ready, pv_taken, att_stored = sem("probsT_ready"), sem("pv_ready"), sem("pv_taken"), sem("att_stored")
        sum_inverted = sem("sum_inverted")
        passed_dve, passed_pool, passed_pe = sem("passed_dve"), sem("passed_pool"), sem("passed_pe")
        pass_weights = sem("pass_weights")
        par_here, par_turned, par_out = sem("par_here"), sem("par_turned"), sem("par_out")
        skip_here, skip_spread = sem("skip_here"), sem("skip_spread")
        taps_ready, conv_step, silu_done, conv_stored, passed_act = \
            (sem(n) for n in ("taps_ready", "conv_step", "silu_done", "conv_stored", "passed_act"))
        dve_step = sem("dve_step")

        RAW_FREE, ACC_FREE = CH, TT
        IQ, QK, V = (0, IQ_PANELS), (IQ_PANELS, QK_PANELS), (QK_PANELS + IQ_PANELS, V_PANELS)
        ZX = (QK_PANELS + IQ_PANELS + V_PANELS, ZX_PANELS)
        LAST = ZX[0] + ZX[1] - 1
        CONV_PANELS = CONV_DIM // PW
        CONV_OPS = CONV_TAPS * TT
        N_PAR_DMAS = 2 * (CONV_TAPS + 1) + 4
        N_SMALL_X = TT * (DK // 4)

        DOTS = IH_PASS * TT
        slot_of = [DOTS_FROM + n * (CH * TT - DOTS_FROM) // DOTS for n in range(DOTS)]
        units_in = [[n for n in range(DOTS) if slot_of[n] == j] for j in range(CH * TT)]

        def width(q):
            return P * (q + 1)

        def conv_count(t):
            return 2 * CONV_TAPS * (t // 2 + 1) - 1 + t % 2

        with nc.Block() as block:
            @block.sync
            def _(sp):
                for t in range(TT):
                    sp.dma_start(xin[t], x[0, t * P:(t + 1) * P, :]).then_inc(x_here[t], 16)
                    if t == TT - 1:
                        rows = w.rearrange("(k p) n -> p k n", p=P)
                        sp.dma_start(wsm_raw[:, :, 0:ID + IH], rows[:, :, COL_IK:COL_IK + ID + IH]).then_inc(small_here, 16)
                        sp.dma_start(wsm_raw[:, :, ID + IH:SMALL], rows[:, :, COL_DT:COL_DT + HEADS]).then_inc(small_here, 16)
                        for half in range(2):
                            sp.dma_start(gb[half * ID:(half + 1) * ID, 0:1], idx_g[0].rearrange("(n a) -> n a", a=1)).then_inc(small_here, 16)
                            sp.dma_start(gb[half * ID:(half + 1) * ID, 1:2], idx_b[0].rearrange("(n a) -> n a", a=1)).then_inc(small_here, 16)

                def panel(p, col, behind_x=False):
                    for c in range(CH):
                        if behind_x and c >= 2:
                            sp.wait_ge(x_turned, (c + 1) * (DK // 4))
                        sp.wait_ge(split_ready, 4 * p + c + 1)
                        src = w[c * KC * P:(c + 1) * KC * P, :].rearrange("(k p) n -> p k n", p=P)
                        sp.dma_start(raw[:, c], src[:, :, bass.ds(col, PW)]).then_inc(raw_here[c], 16)

                sp.dma_start(skip2[:], d_skip[0].rearrange("(i h) -> i h", h=2)).then_inc(skip_here, 16)
                panel(0, COL_IQ, behind_x=True)
                bc = CT - XT
                for j in range(CONV_TAPS + 1):
                    of = conv_w[0, j] if j < CONV_TAPS else conv_b[0]
                    sp.dma_start(par_rows[j * CT:j * CT + bc, :], of[SSD_W:CONV_DIM].rearrange("(i c) -> i c", c=P)).then_inc(par_here, 16)
                    sp.dma_start(par_rows[j * CT + bc:(j + 1) * CT, :], of[0:SSD_W].rearrange("(i c) -> i c", c=P)).then_inc(par_here, 16)
                n = (CONV_TAPS + 1) * CT
                sp.dma_start(par_rows[n:n + XT, :], norm_w[0].rearrange("(i c) -> i c", c=P)).then_inc(par_here, 16)
                sp.wait_ge(skip_spread, 1)
                sp.dma_start(par_rows[n + XT:N_PAR, :], skip_rows[:]).then_inc(par_here, 16)
                sp.dma_start(head_rows[:, 0:HEADS], dt_bias).then_inc(par_here, 16)
                sp.dma_start(head_rows[:, HEADS:2 * HEADS], a_log).then_inc(par_here, 16)
                with sp.Fori(1, IQ[1]) as i:
                    panel(IQ[0] + i, COL_IQ + i * PW)
                with sp.Fori(0, QK[1]) as i:
                    panel(QK[0] + i, COL_Q + i * PW)
                with sp.Fori(0, V[1]) as i:
                    panel(V[0] + i, COL_V + i * PW)
                panel(ZX[0], COL_XBC + SSD_W)
                with sp.Fori(1, CONV_PANELS) as i:
                    panel(ZX[0] + i, COL_XBC + (i - 1) * PW)
                with sp.Fori(CONV_PANELS, ZX[1]) as i:
                    panel(ZX[0] + i, COL_Z + (i - CONV_PANELS) * PW)

            @block.tensor
            def _(pe):
                pe.sem_inc(acc_ready, ACC_FREE)
                pe.sem_inc(probs_turned, 2)
                pe.sem_inc(pv_ready, 2)
                pe.sem_inc(relu_ready, 4)
                for u in range(N_SMALL_X):
                    t, g = u // (DK // 4), u % (DK // 4)
                    if g == 0:
                        pe.wait_ge(x_here[t], 16)
                    if u >= 8:
                        pe.wait_ge(x_lo, u - 7)
                    for j in range(4):
                        last = pe.transpose(banks[u % 8][:, j * P:(j + 1) * P],
                                            xin[t][:, (4 * g + j) * P:(4 * g + j + 1) * P], k.ident[:])
                    last.then_inc(x_turned, 1)
                pe.wait_ge(x_lo, N_SMALL_X)
                pe.wait_ge(small_lo, 1)
                for kt in range(DK):
                    for n, (a, b) in enumerate(((xhi, wsm_hi), (xhi, wsm_lo), (xlo, wsm_hi))):
                        last = pe.matmul(side[0][0:SMALL, :], b[:, kt, :], a[:, kt, :],
                                         start=(kt == 0 and n == 0), stop=(kt == DK - 1 and n == 2))
                last.then_inc(small_turned, 1)
                pe.wait_ge(small_flat, 1)
                for t in range(TT):
                    last = pe.transpose(side[1][:, t * SMALL:(t + 1) * SMALL], smallT[:, t * P:(t + 1) * P], k.ident[0:SMALL, 0:SMALL])
                last.then_inc(small_acc, 1)

                def steps(p, turned, between=None):
                    for c in range(CH):
                        s = c % SPLIT_SLOTS
                        pe.wait_ge(split_ready, RAW_FREE + 4 * p + c + 1)
                        for t in range(TT):
                            if c == 0:
                                pe.wait_ge(acc_taken, 4 * p + t + 1)
                            cut = slice(t * P, (t + 1) * P)
                            for kk in range(KC):
                                kt = c * KC + kk
                                for n, (a, b) in enumerate(((xhi, whi[s]), (xhi, wlo[s]), (xlo, whi[s]))):
                                    first, final = c == 0 and kk == 0 and n == 0, c == CH - 1 and kk == KC - 1 and n == 2
                                    if turned:
                                        last = pe.matmul(acc[t][:], b[:, kk, cut], a[:, kt, :], start=first, stop=final)
                                    else:
                                        last = pe.matmul(acc[t][:], a[:, kt, cut], b[:, kk, :], start=first, stop=final)
                            if c == CH - 1:
                                last.then_inc(acc_ready, 1)
                            elif t == TT - 1:
                                last.then_inc(split_used, 1)
                            if between is not None:
                                between(4 * c + t)

                with pe.Fori(0, IQ[1]) as i:
                    steps(IQ[0] + i, True)

                pe.wait_ge(ikn_done, 1)
                for t in range(TT):
                    last = pe.transpose(side[1][:, t * P:(t + 1) * P], ikn[:, t, :], k.ident[:])
                last.then_inc(ik_turned, 1)
                pe.wait_ge(par_here, 16 * N_PAR_DMAS)
                pe.transpose(side[2][:, 0:N_PAR], par_rows[:], k.ident[0:N_PAR, 0:N_PAR])
                pe.matmul(side[3][:, 0:2 * HEADS], k.ones[0:1, :], head_rows[:], start=True, stop=True).then_inc(par_turned, 1)
                pe.wait_ge(par_out, 2)

                pe.wait_ge(ik_ready, 1)

                def indexer(i):
                    def between(j):
                        for n in units_in[j]:
                            hh, q = n // TT, n % TT
                            if n == 0:
                                pe.wait_ge(iq_here, 16 * (i + 1))
                            pe.wait_ge(relu_ready, DOTS * i + n + 1)
                            pe.sem_inc(passed_pe, 1)
                            half = slice(ID * (hh % 2), ID * (hh % 2) + ID)
                            pe.matmul(side[n % 4][:, 0:width(q)], iq[half, hh // 2, q * P:(q + 1) * P], ikT[half, 0:width(q)],
                                      start=True, stop=True).then_inc(dots_ready, 1)
                    return between

                with pe.Fori(0, QK[1]) as i:
                    steps(QK[0] + i, True, indexer(i))

                with pe.Fori(0, V[1]) as i:
                    steps(V[0] + i, False)

                pe.wait_ge(relu_ready, 4 + TT * IH)

                def attend(it):
                    first_unit = UNITS * it

                    def between(j):
                        if j >= SLOTS:
                            return
                        if j < UNITS:
                            hh, q = j // TT, j % TT
                            if j == 0:
                                pe.wait_ge(heads_here, 48 * (it + 1))
                            pe.wait_ge(logits_masked, first_unit + j + 1)
                            pe.matmul(side[j % 2][:, 0:width(q)], qh[:, hh, q * P:(q + 1) * P], kh[:, hh, 0:width(q)],
                                      start=True, stop=True).then_inc(logits_ready, 1)
                        if 1 <= j <= UNITS:
                            v, q = j - 1, (j - 1) % TT
                            pe.wait_ge(probs_ready, first_unit + v + 1)
                            pe.wait_ge(probsT_ready, first_unit + v + 1)
                            for s in range(q + 1):
                                last = pe.transpose(side[2][:, s * P:(s + 1) * P], probs[:, v % 2, s * P:(s + 1) * P], k.ident[:])
                            last.then_inc(probs_turned, 1)
                        if 2 <= j:
                            v, hh, q = j - 2, (j - 2) // TT, (j - 2) % TT
                            pe.wait_ge(probsT_ready, 1 + first_unit + v + 1)
                            pe.wait_ge(pv_taken, first_unit + v + 1)
                            for s in range(q + 1):
                                last = pe.matmul(side[3][:, 0:P], vh[:, s, hh * P:(hh + 1) * P], probsT[:, v % 2, s * P:(s + 1) * P],
                                                 start=(s == 0), stop=(s == q))
                            last.then_inc(pv_ready, 1)
                    return between

                with pe.Fori(0, ZX[1] - 1) as i:
                    steps(ZX[0] + i, True, attend(i))
                steps(LAST, True)

            @block.scalar
            def _(act):
                act.sem_inc(conv_stored, 16)
                for u in range(N_SMALL_X):
                    t, g = u // (DK // 4), u % (DK // 4)
                    act.wait_ge(x_turned, u + 1)
                    act.activation(xhi[:, 4 * g:4 * g + 4, t * P:(t + 1) * P],
                                   banks[u % 8][:, :].rearrange("p (j n) -> p j n", j=4), ACT.Copy).then_inc(x_hi, 1)
                    if u == N_SMALL_X - 1:
                        act.wait_ge(small_here, 16 * 6)
                        act.activation(wsm_hi[:], wsm_raw[:], ACT.Copy).then_inc(small_hi, 1)

                def high(c, p):
                    act.wait_ge(raw_here[c], 16 * (p + 1))
                    act.activation(whi[c % SPLIT_SLOTS][:], raw[:, c], ACT.Copy).then_inc(hi_ready, 1)

                def high_next(c, p, more=True):
                    if c == 1:
                        act.wait_ge(acc_ready, 4 * p + TT)
                        high(1, p)
                    elif c in (2, 3):
                        act.wait_ge(split_used, 3 * p + c - 1)
                        high(c, p)
                    elif more:
                        act.wait_ge(split_used, 3 * p + 3)
                        high(0, p + 1)

                def evacuate(p, behind=None, convolved=None, tiles=range(TT)):
                    for t in tiles:
                        act.wait_ge(acc_ready, ACC_FREE + 4 * p + t + 1)
                        if convolved is None:
                            act.wait_ge(stored[t], 16 * (p + 1 if behind is None else behind))
                        elif t == 0:
                            act.wait_ge(conv_step, CONV_OPS * convolved)
                        act.activation(stage[:, t, :], acc[t][:], ACT.Copy).then_inc(acc_taken, 1)

                def body(p, more=True, behind=None):
                    for c in (1, 2, 3, 0):
                        high_next(c, p, more)
                    evacuate(p, behind)

                high(0, 0)
                act.wait_ge(small_turned, 1)
                act.activation(smallT[:], side[0][0:SMALL, :], ACT.Copy).then_inc(small_flat, 1)
                act.wait_ge(small_acc, 1)
                act.activation(small[:], side[1][:, 0:TT * SMALL].rearrange("p (t n) -> p t n", t=TT), ACT.Copy).then_inc(small_out, 1)
                act.wait_ge(dve_step, TT + 2)
                act.activation(rstd[:], rstd[:], ACT.Sqrt).then_inc(small_out, 1)
                with act.Fori(0, IQ[1]) as i:
                    body(IQ[0] + i)
                act.wait_ge(ik_turned, 1)
                act.activation(ikT[:], side[1][:], ACT.Identity, bias=gb[:, 1:2], scale=gb[:, 0:1]).then_inc(ik_ready, 1)
                act.wait_ge(par_turned, 1)
                act.activation(k.par[:], side[2][:, 0:N_PAR], ACT.Copy).then_inc(par_out, 1)
                act.activation(k.head[:], side[3][:, 0:2 * HEADS], ACT.Copy).then_inc(par_out, 1)
                with act.Fori(0, QK[1]) as i:
                    for j in range(CH * TT):
                        if j % 4 == 0:
                            high_next((j // 4 + 1) % CH, QK[0] + i)
                        elif j > (CH - 1) * TT:
                            evacuate(QK[0] + i, tiles=[j - 1 - (CH - 1) * TT])
                        for n in units_in[j]:
                            q = n % TT
                            act.wait_ge(dots_ready, DOTS * i + n + 1)
                            act.wait_ge(score_step, TT + DOTS * i + n - 1)
                            act.activation(relu[:, n % 2, 0:width(q)], side[n % 4][:, 0:width(q)], ACT.Relu).then_inc(relu_ready, 1)
                    evacuate(QK[0] + i, tiles=[TT - 1])
                with act.Fori(0, V[1]) as i:
                    body(V[0] + i)

                def attention_body(it, p):
                    first_unit = UNITS * it
                    for j in range(SLOTS):
                        if j in (0, 4, 8):
                            high_next(j // 4 + 1, p)
                        if j < UNITS:
                            act.wait_ge(max_ready, first_unit + j + 1)
                            act.activation(probs[:, j % 2, 0:width(j % TT)], probs[:, j % 2, 0:width(j % TT)], ACT.Exp,
                                           bias=nmax[:, j % 2, 1:2], scale=AD ** -0.5,
                                           accum_out=rowsum[:, j % 2:j % 2 + 1]).then_inc(exp_ready, 1)
                        if j >= 2:
                            v = j - 2
                            act.wait_ge(pv_ready, 2 + first_unit + v + 1)
                            act.activation(oh[:, v // TT, (v % TT) * P:(v % TT + 1) * P], side[3][:, 0:P], ACT.Copy).then_inc(pv_taken, 1)
                    high_next(0, p)

                attention_body(0, ZX[0])
                evacuate(ZX[0])
                with act.Fori(1, ZX[1] - 1) as i:
                    attention_body(i, ZX[0] + i)
                    for t in range(TT):
                        act.wait_ge(conv_step, CONV_OPS * (i - 1) + conv_count(t))
                        act.activation(conved[:, t, :], conved[:, t, :], ACT.Silu).then_inc(silu_done, 1)
                    evacuate(ZX[0] + i, convolved=i)
                    act.wait_ge(silu_done, TT * i)
                    act.sem_inc(passed_act, 1)
                    act.dma_start(scr.xbcT[bass.ds((i - 1) * PW, PW), :].rearrange("(t p) n -> p t n", p=P), conved[:]).then_inc(conv_stored, 16)
                body(LAST, more=False, behind=1 + ZX[0] + 1)
                act.wait_ge(conv_stored, 16 * (1 + CONV_PANELS))

            @block.vector
            def _(dve):
                dve.sem_inc(split_ready, RAW_FREE)
                dve.sem_inc(acc_taken, ACC_FREE)
                dve.sem_inc(logits_masked, 2)
                dve.sem_inc(probsT_ready, 1)
                dve.sem_inc(pv_taken, 1)
                for u in range(N_SMALL_X):
                    t, g = u // (DK // 4), u % (DK // 4)
                    cut = (slice(None), slice(4 * g, 4 * g + 4), slice(t * P, (t + 1) * P))
                    dve.wait_ge(x_hi, u + 1)
                    dve.tensor_tensor(xlo[cut], banks[u % 8][:, :].rearrange("p (j n) -> p j n", j=4),
                                      xhi[cut].bitcast(FP32), ALU.subtract).then_inc(x_lo, 1)
                    if u == N_SMALL_X - 1:
                        dve.wait_ge(small_hi, 1)
                        dve.tensor_tensor(wsm_lo[:], wsm_raw[:], wsm_hi[:].bitcast(FP32), ALU.subtract).then_inc(small_lo, 1)

                def low(c, p):
                    dve.wait_ge(hi_ready, 4 * p + c + 1)
                    s = c % SPLIT_SLOTS
                    dve.tensor_tensor(wlo[s][:], raw[:, c], whi[s][:].bitcast(FP32), ALU.subtract).then_inc(split_ready, 1)

                def low_next(c, p, more=True):
                    if c:
                        low(c, p)
                    elif more:
                        low(0, p + 1)

                low(0, 0)
                dve.wait_ge(skip_here, 16)
                dve.tensor_copy(skip_rows[:].rearrange("i (h n) -> i h n", h=2),
                                skip2[:].unsqueeze(2).broadcast_to((XT, 2, HD))).then_inc(skip_spread, 1)
                step = [0]

                def link(ins):
                    step[0] += 1
                    ins.then_inc(dve_step, 1)
                    dve.wait_ge(dve_step, step[0])

                dve.wait_ge(small_out, 1)
                for t in range(TT):
                    last = dve.bn_stats(stats[:, t, :], small[:, t, 0:ID])
                link(last)
                for t in range(TT):
                    link(dve.bn_aggr(mv[:, t, :], stats[:, t, :]))
                link(dve.tensor_scalar(rstd[:], mv[:, :, 1], EPS, None, ALU.add))
                link(dve.tensor_scalar(iws[:], small[:, :, ID:ID + IH], ID ** -0.5 * IH ** -0.5, None, ALU.mult))
                dve.wait_ge(small_out, 2)
                link(dve.reciprocal(rstd[:], rstd[:]))
                for t in range(TT):
                    for half in range(2):
                        last = dve.tensor_scalar(ikn[:, t, half * ID:(half + 1) * ID], small[:, t, 0:ID],
                                                 mv[:, t, 0:1], rstd[:, t:t + 1], ALU.subtract, ALU.mult)
                last.then_inc(ikn_done, 1)
                with dve.Fori(0, IQ[1]) as i:
                    for c in (1, 2, 3, 0):
                        low_next(c, i)
                for q in range(TT):
                    dve.tensor_copy(score[q][:], k.causal_bias[:, SEQ - width(q):SEQ]).then_inc(score_step, 1)
                with dve.Fori(0, QK[1]) as i:
                    dve.wait_ge(score_step, TT + DOTS * i)
                    dve.tensor_copy(iws_pass[:], iws[:, :, bass.ds(i * IH_PASS, IH_PASS)]).then_inc(pass_weights, 1)
                    for j in range(CH * TT):
                        if j % 4 == 0:
                            low_next((j // 4 + 1) % CH, QK[0] + i)
                        for n in units_in[j]:
                            hh, q = n // TT, n % TT
                            if n == 0:
                                dve.wait_ge(pass_weights, i + 1)
                            dve.wait_ge(relu_ready, 4 + DOTS * i + n + 1)
                            dve.wait_ge(score_step, DOTS * i + n + 1)
                            dve.scalar_tensor_tensor(out=score[q][:], in0=relu[:, n % 2, 0:width(q)], scalar=iws_pass[:, q, hh:hh + 1],
                                                     in1=score[q][:], op0=ALU.mult, op1=ALU.add).then_inc(score_step, 1)
                dve.wait_ge(score_step, TT + TT * IH)

                def pick(q):
                    link(dve.max(top8[:], score[q][:]))
                    link(dve.match_replace(score[q][:], top8[:], score[q][:], TAKEN))

                rounds = [q for q in range(1, TT) for _ in range(TOPK // 8)]
                share = -(-len(rounds) // (V[1] * CH))
                for i in range(V[1]):
                    for c in (1, 2, 3, 0):
                        low_next(c, V[0] + i)
                        for q in rounds[:share]:
                            pick(q)
                        rounds = rounds[share:]
                link(dve.tensor_copy(score[0][:], k.causal_bias[:, SEQ - P:SEQ]))
                for q in range(1, TT):
                    link(dve.tensor_scalar(score[q][:], score[q][:], TAKEN, NEG, ALU.is_gt, ALU.mult))

                def attention_body(it, p):
                    first_unit = UNITS * it
                    for j in range(SLOTS):
                        if j in (0, 4, 8):
                            low_next(j // 4 + 1, p)
                        if j < UNITS:
                            q = j % TT
                            dve.wait_ge(dve_step, step[0])
                            dve.wait_ge(logits_ready, first_unit + j + 1)
                            dve.wait_ge(probs_turned, first_unit + j + 1)
                            dve.sem_inc(passed_dve, 1)
                            dve.tensor_tensor_reduce(out=probs[:, j % 2, 0:width(q)], in0=side[j % 2][:, 0:width(q)],
                                                     in1=score[q][:], scale=1.0, scalar=TAKEN, op0=ALU.add, op1=ALU.max,
                                                     accum_out=nmax[:, j % 2, 0:1]).then_inc(logits_masked, 1)
                            dve.wait_ge(logits_masked, 2 + first_unit + j + 1)
                            dve.tensor_scalar(nmax[:, j % 2, 1:2], nmax[:, j % 2, 0:1], -AD ** -0.5, None,
                                              ALU.mult).then_inc(max_ready, 1)
                        if 1 <= j <= UNITS:
                            v, q = j - 1, (j - 1) % TT
                            dve.wait_ge(probs_turned, 2 + first_unit + v + 1)
                            dve.wait_ge(pv_ready, first_unit + v + 1)
                            dve.tensor_copy(probsT[:, v % 2, 0:width(q)], side[2][:, 0:width(q)]).then_inc(probsT_ready, 1)
                        if j < UNITS:
                            dve.wait_ge(exp_ready, first_unit + j + 1)
                            dve.reciprocal(rowsum[:, j % 2:j % 2 + 1], rowsum[:, j % 2:j % 2 + 1]).then_inc(sum_inverted, 1)
                            dve.wait_ge(sum_inverted, first_unit + j + 1)
                            dve.tensor_scalar(probs[:, j % 2, 0:width(j % TT)], probs[:, j % 2, 0:width(j % TT)],
                                              rowsum[:, j % 2:j % 2 + 1], None, ALU.mult).then_inc(probs_ready, 1)

                def convolve(i, r):
                    for n in range(2 * CONV_TAPS):
                        t, back = 2 * r + n % 2, n // 2
                        count = CONV_OPS * (i - 1) + 2 * CONV_TAPS * r + n
                        tap = taps[:, CONV_TAPS - 1 - back, t:t + 1]
                        if back == 0:
                            dve.tensor_scalar(conved[:, t, :], stage[:, t, :], tap, taps[:, CONV_TAPS, t:t + 1],
                                              ALU.mult, ALU.add).then_inc(conv_step, 1)
                        else:
                            dve.wait_ge(conv_step, count - 1)
                            dve.scalar_tensor_tensor(out=conved[:, t, back:], in0=stage[:, t, 0:SEQ - back], scalar=tap,
                                                     in1=conved[:, t, back:], op0=ALU.mult, op1=ALU.add).then_inc(conv_step, 1)

                attention_body(0, ZX[0])
                low_next(0, ZX[0])
                with dve.Fori(1, ZX[1] - 1) as i:
                    attention_body(i, ZX[0] + i)
                    dve.wait_ge(acc_taken, ACC_FREE + TT * (ZX[0] + i))
                    dve.wait_ge(conv_stored, 16 * i)
                    of = k.par[:, 0:(CONV_TAPS + 1) * CT].rearrange("p (j c) -> p j c", c=CT)
                    dve.tensor_copy(taps[:], of[:, :, bass.ds((i - 1) * TT, TT)]).then_inc(taps_ready, 1)
                    dve.wait_ge(taps_ready, i)
                    convolve(i, 0)
                    low_next(0, ZX[0] + i)
                    convolve(i, 1)
                for c in (1, 2, 3, 0):
                    low_next(c, LAST, more=False)

            @block.gpsimd
            def _(pool):
                pool.wait_ge(small_out, 1)
                for t in range(TT):
                    pool.dma_start(scr.dt[t * P:(t + 1) * P, :], small[:, t, ID + IH:SMALL]).then_inc(stored[t], 16)

                def store(p, dst):
                    for t in range(TT):
                        pool.wait_ge(acc_taken, ACC_FREE + 4 * p + t + 1)
                        pool.sem_inc(passed_pool, 1)
                        pool.dma_start(dst(t), stage[:, t, :]).then_inc(stored[t], 16)

                def load_iq(i):
                    n = IH_PASS * ID
                    pool.dma_start(iq, scr.iqT[bass.ds(i * n, n), :].rearrange("(h p) n -> p h n", p=P)).then_inc(iq_here, 16)

                store_qk = lambda i: store(QK[0] + i, lambda t: scr.qkT[bass.ds(i * PW + t * P, P), :])
                with pool.Fori(0, IQ[1]) as i:
                    store(IQ[0] + i, lambda t: scr.iqT[bass.ds(i * PW + t * P, P), :])
                for t in range(TT):
                    pool.wait_ge(stored[t], 16 * (1 + QK[0]))
                load_iq(0)
                with pool.Fori(0, QK[1] - 1) as i:
                    pool.wait_ge(dots_ready, DOTS * (i + 1))
                    pool.sem_inc(passed_pool, 1)
                    load_iq(i + 1)
                    store_qk(i)
                store_qk(QK[1] - 1)
                def load_heads(it):
                    row = it * HEADS_PER_PANEL * P
                    n = HEADS_PER_PANEL * P
                    pool.dma_start(qh, scr.qkT[bass.ds(row, n), :].rearrange("(h p) n -> p h n", p=P)).then_inc(heads_here, 16)
                    pool.dma_start(kh, scr.qkT[bass.ds(AH * AD + row, n), :].rearrange("(h p) n -> p h n", p=P)).then_inc(heads_here, 16)
                    pool.dma_start(vh, scr.v.rearrange("(s p) n -> p s n", p=P)[:, :, bass.ds(row, n)]).then_inc(heads_here, 16)

                def store_heads(it):
                    pool.wait_ge(pv_taken, 1 + UNITS * (it + 1))
                    pool.sem_inc(passed_pool, 1)
                    pool.dma_start(scr.attT[bass.ds(it * HEADS_PER_PANEL * P, HEADS_PER_PANEL * P), :]
                                   .rearrange("(h p) n -> p h n", p=P), oh).then_inc(att_stored, 16)

                pool.wait_ge(dots_ready, TT * IH)
                for i in range(V[1]):
                    store(V[0] + i, lambda t: scr.v[t * P:(t + 1) * P, i * PW:(i + 1) * PW])
                    for t in range(TT):
                        pool.wait_ge(stored[t], 16 * (1 + V[0] + i + 1))
                    if i == 0:
                        load_heads(0)
                with pool.Fori(0, ZX[1] - 2) as i:
                    store_heads(i)
                    pool.wait_ge(att_stored, 16 * (i + 1))
                    pool.sem_inc(passed_pool, 1)
                    load_heads(i + 1)
                store_heads(ZX[1] - 2)
                for n in range(ZX_PANELS - CONV_PANELS):
                    store(ZX[0] + CONV_PANELS + n, lambda t: scr.zT[n * PW + t * P:n * PW + (t + 1) * P, :])
                for t in range(TT):
                    pool.wait_ge(stored[t], 16 * (1 + LAST + 1 - CONV_PANELS))
                pool.wait_ge(att_stored, 16 * (ZX[1] - 1))


def run_ssd(nc, k, p, w_out, ln_g, ln_b, scr, keep):
    ITER = [(c, g) for c in range(TT) for g in range(GROUPS)]
    GW = HPG * HD
    with ExitStack() as ctx:
        def sb(name, shape, dt=FP32):
            return ctx.enter_context(nc.sbuf_tensor(name, shape, dt))

        def sem(name):
            return k.semaphore(name)

        banks = [ctx.enter_context(nc.psum_tensor(f"sbank{i}", [P, PW], FP32)) for i in range(8)]
        acs_rows, small_bank, y_bank, carry_bank, state_bank, turn_in, turn_out = \
            banks[0:2], banks[2], banks[3], banks[4], banks[5], banks[6], banks[7]
        z = sb("z", [P, XT, SEQ])
        xbc = sb("xbc", [P, CT, SEQ])
        mixed = keep.h[:].rearrange("p t n -> p (t n)").rearrange("p (i n) -> p i n", n=SEQ)
        y, y_att = mixed[:, 0:XT, :], mixed[:, XT:DK, :]
        head = k.head
        H4 = [P, TT, HEADS]
        dt, pos, ea, u1, dta = sb("dtv", H4), sb("pos", H4), sb("ex", H4), sb("u1", H4), sb("dta", H4)
        acs, acs_exp, to_end, chunk_decay = sb("acs", H4), sb("acs_exp", H4), sb("to_end", H4), sb("chunk_decay", H4)
        nega = sb("nega", [P, HEADS])
        xdt, xdec = sb("xdt", [P, 2, GW]), sb("xdec", [P, 2, GW])
        b_tok = sb("b_tok", [P, 2, STATE])
        cbm = sb("cbm", [P, 2, P])
        seg = sb("seg", [P, 2, PW])
        m = sb("m", [P, 2, 2, PW])
        carry = sb("carry", [P, GROUPS, GW])
        yoff, ytok = sb("yoff", [P, 2, GW]), sb("ytok", [P, 2, GW])
        sq = sb("sq", [P, 2, SEQ])
        rinv = sb("rinv", [P, SEQ])
        zeros = sb("zeros", [P, D])

        zeros_ready, beyond_cleared = sem("zeros_ready"), sem("beyond_cleared")
        z_here, dt_here, z_silu = sem("z_here"), sem("dt_here"), sem("z_silu")
        xbc_here = [sem(f"xbc_here{n}") for n in range(3)]
        dt_step, dt_exp, acs_ready = sem("dt_step"), sem("dt_exp"), sem("acs_ready")
        x_turned, cb_ready, rows_ready = sem("sx_turned"), sem("cb_ready"), sem("rows_ready")
        b_out, seg_out, seg_exp = sem("b_out"), sem("seg_out"), sem("seg_exp")
        xdt_ready, cbm_ready, m_ready, xdec_ready = sem("xdt_ready"), sem("cbm_ready"), sem("m_ready"), sem("xdec_ready")
        diag_ready, off_ready, state_ready = sem("diag_ready"), sem("off_ready"), sem("state_ready")
        off_scaled, y_ready, carry_scaled, carry_ready = sem("off_scaled"), sem("y_ready"), sem("carry_scaled"), sem("carry_ready")
        y_turned, y_skip, gated = sem("y_turned"), sem("y_skip"), sem("gated")
        squared, square_used, sums_ready, mean_out, root_out, rinv_ready = \
            sem("squared"), sem("square_used"), sem("sums_ready"), sem("mean_out"), sem("root_out"), sem("rinv_ready")
        next_here = sem("next_here")
        gain = keep.gain
        p_in, turned_rows = sb("p_in", [P, TT, PLE]), sb("turned_rows", [2 * DK, P])
        gb_here, gb_ready, gb_taken = sem("gb_here"), sem("gb_ready"), sem("gb_taken")
        p_here, p_turned, p_out = sem("p_here"), sem("p_turned"), sem("p_out")
        p_banks, gain_banks = [acs_rows[1], carry_bank], [turn_in, state_bank, y_bank, turn_out]

        norm = lambda i: k.par[:, (CONV_TAPS + 1) * CT + i:(CONV_TAPS + 1) * CT + i + 1]
        skip = lambda i: k.par[:, (CONV_TAPS + 1) * CT + XT + i:(CONV_TAPS + 1) * CT + XT + i + 1]
        B_TILE, C_TILE = XT, XT + GROUPS
        def per_head(a):
            return a.unsqueeze(2).broadcast_to((P, HPG, HD))

        def heads_of(g):
            return slice(g * HPG, (g + 1) * HPG)

        def cut(c):
            return slice(c * P, (c + 1) * P)

        with nc.Block() as block:
            @block.sync
            def _(sp):
                sp.dma_start(dt[:], scr.dt.rearrange("(t p) n -> p t n", p=P)).then_inc(dt_here, 16)
                src = scr.xbcT.rearrange("(i p) n -> p i n", p=P)
                bc, half = CT - XT, XT // 2
                sp.dma_start(xbc[:, XT:CT, :], src[:, 0:bc, :]).then_inc(xbc_here[0], 16)
                sp.dma_start(gain[0:1, 0, :], ln_g).then_inc(gb_here, 16)
                sp.dma_start(gain[0:1, 1, :], ln_b).then_inc(gb_here, 16)
                for n, v in enumerate((ln_g, ln_b)):
                    sp.dma_start(turned_rows[n * DK:(n + 1) * DK, :], v[0].rearrange("(k c) -> k c", c=P)).then_inc(p_here, 16)
                sp.dma_start(p_in[:], p[0, 0].rearrange("(t p) n -> p t n", p=P)).then_inc(p_here, 16)
                for n in range(2):
                    sp.dma_start(xbc[:, n * half:(n + 1) * half, :], src[:, bc + n * half:bc + (n + 1) * half, :]).then_inc(xbc_here[1 + n], 16)
                sp.dma_start(z[:], scr.zT.rearrange("(i p) n -> p i n", p=P)).then_inc(z_here, 16)
                sp.dma_start(y_att, scr.attT.rearrange("(i p) n -> p i n", p=P)).then_inc(next_here, 16)
                for c in range(CH):
                    rows = w_out[0, c * KC * P:(c + 1) * KC * P, 0:PW].rearrange("(k p) n -> p k n", p=P)
                    sp.dma_start(keep.raw[:, c], rows).then_inc(next_here, 16)
                sp.wait_ge(zeros_ready, 1)
                beyond = MAX_OVER * CAP
                for r in range(0, beyond, P):
                    n = min(P, beyond - r)
                    sp.dma_start(scr.yb[N_EXP * CAP + r:N_EXP * CAP + r + n, :], zeros[0:n, :]).then_inc(beyond_cleared, 16)
                sp.wait_ge(next_here, 16 * (1 + CH))
                sp.wait_ge(beyond_cleared, 16 * -(-beyond // P))

            @block.tensor
            def _(pe):
                pe.wait_ge(dt_step, DT_STEPS)
                pe.matmul(y_bank[:, 0:TT * HEADS], k.upto[:], dta[:].rearrange("p t h -> p (t h)"), start=True, stop=True)
                pe.matmul(carry_bank[:, 0:TT * HEADS], k.ones[:], dta[:].rearrange("p t h -> p (t h)"),
                          start=True, stop=True).then_inc(acs_ready, 1)

                def scan_inputs(i):
                    c, g = ITER[i]
                    if i <= 1:
                        pe.wait_ge(xbc_here[1 + i], 16)
                    if i == 0:
                        pe.wait_ge(xbc_here[0], 16)
                    if i >= 1:
                        pe.wait_ge(xdt_ready, i)
                    for j in range(4):
                        last = pe.transpose(turn_in[:, j * P:(j + 1) * P], xbc[:, 4 * g + j, cut(c)], k.ident[:])
                    last.then_inc(x_turned, 1)
                    if i >= 1:
                        pe.wait_ge(cbm_ready, i)
                        pe.wait_ge(b_out, i)
                    pe.transpose(small_bank[:, P:2 * P], xbc[:, B_TILE + g, cut(c)], k.ident[:])
                    pe.matmul(small_bank[:, 0:P], xbc[:, B_TILE + g, cut(c)], xbc[:, C_TILE + g, cut(c)],
                              start=True, stop=True).then_inc(cb_ready, 1)
                    for b in range(2):
                        if i >= 1:
                            pe.wait_ge(seg_out, 4 * (2 * (i - 1) + b + 1))
                        for j in range(4):
                            h = g * HPG + 4 * b + j
                            last = pe.matmul(acs_rows[b][:, j * P:(j + 1) * P], dta[:, c, h:h + 1].broadcast_to((P, P)),
                                             k.upto[:], start=True, stop=True)
                        last.then_inc(rows_ready, 1)

                def scan(i):
                    c, g = ITER[i]
                    pe.wait_ge(m_ready, 2 * i + 2)
                    if i >= 1:
                        pe.wait_ge(y_ready, i)
                    else:
                        pe.wait_ge(dt_exp, DT_EXPS)
                    for j in range(HPG):
                        last = pe.matmul(y_bank[:, j * HD:(j + 1) * HD], m[:, i % 2, j // 4, (j % 4) * P:(j % 4 + 1) * P],
                                         xdt[:, i % 2, j * HD:(j + 1) * HD], start=True, stop=True)
                    last.then_inc(diag_ready, 1)
                    if c:
                        pe.wait_ge(carry_ready, (c - 1) * GROUPS + g + 1)
                        pe.matmul(carry_bank[:], xbc[:, C_TILE + g, cut(c)], carry[:, g, :], start=True, stop=True).then_inc(off_ready, 1)
                    if c < TT - 1:
                        pe.wait_ge(xdec_ready, i + 1)
                        pe.wait_ge(b_out, i + 1)
                        if i >= 1:
                            pe.wait_ge(carry_ready, i)
                        pe.matmul(state_bank[:], b_tok[:, i % 2, :], xdec[:, i % 2, :], start=True, stop=True).then_inc(state_ready, 1)

                def turn_back(i):
                    pe.wait_ge(y_ready, i + 1)
                    if i >= 1:
                        pe.wait_ge(y_skip, 4 * i)
                    for j in range(4):
                        last = pe.transpose(turn_out[:, j * P:(j + 1) * P], ytok[:, i % 2, j * P:(j + 1) * P], k.ident[:])
                    last.then_inc(y_turned, 1)

                scan_inputs(0)
                for i in range(len(ITER)):
                    if i + 1 < len(ITER):
                        scan_inputs(i + 1)
                    scan(i)
                    if i:
                        turn_back(i - 1)
                turn_back(len(ITER) - 1)

                def broadcast(n):
                    for j, bank in enumerate(gain_banks):
                        if n == 0 and j == len(gain_banks) - 1:
                            pe.wait_ge(y_skip, 4 * len(ITER))
                        last = pe.matmul(bank[:], k.ones[0:1, :], gain[0:1, n, j * PW:(j + 1) * PW], start=True, stop=True)
                    last.then_inc(gb_ready, 1)

                pe.wait_ge(p_here, 48)
                pe.wait_ge(seg_out, HPG * len(ITER))
                for j, bank in enumerate(p_banks):
                    for t in range(TT):
                        pe.transpose(bank[:, t * P:(t + 1) * P], p_in[:, t, j * P:(j + 1) * P], k.ident[:])
                pe.transpose(small_bank[:, 0:2 * DK], turned_rows[:], k.ident[0:2 * DK, 0:2 * DK]).then_inc(p_turned, 1)
                pe.wait_ge(gb_here, 32)
                broadcast(0)
                for i in range(XT):
                    pe.wait_ge(squared, i + 1)
                    pe.matmul(acs_rows[0][:], k.ones[:], sq[:, i % 2, :], start=(i == 0), stop=(i == XT - 1)).then_inc(square_used, 1)
                pe.wait_ge(gb_taken, TT)
                broadcast(1)

            @block.scalar
            def _(act):
                act.activation(nega[:], head[:, HEADS:2 * HEADS], ACT.Exp).then_inc(dt_exp, 1)
                act.wait_ge(dt_step, 3)
                act.activation(ea[:], ea[:], ACT.Exp, scale=-1.0).then_inc(dt_exp, 1)
                act.wait_ge(dt_step, 4)
                act.activation(acs[:], u1[:], ACT.Ln).then_inc(dt_exp, 1)
                act.wait_ge(acs_ready, 1)
                act.activation(acs[:], y_bank[:, 0:TT * HEADS].rearrange("p (t h) -> p t h", t=TT), ACT.Copy).then_inc(dt_exp, 1)
                act.activation(acs_exp[:], y_bank[:, 0:TT * HEADS].rearrange("p (t h) -> p t h", t=TT), ACT.Exp).then_inc(dt_exp, 1)
                act.activation(chunk_decay[:], carry_bank[:, 0:TT * HEADS].rearrange("p (t h) -> p t h", t=TT), ACT.Exp).then_inc(dt_exp, 1)
                act.wait_ge(dt_step, DT_STEPS + 1)
                act.activation(to_end[:], to_end[:], ACT.Exp).then_inc(dt_exp, 1)
                act.wait_ge(dt_exp, DT_EXPS)

                for i, (c, g) in enumerate(ITER):
                    for b in range(2):
                        act.wait_ge(rows_ready, 2 * i + b + 1)
                        if i >= 1:
                            act.wait_ge(m_ready, 2 * (i - 1) + b + 1)
                        for j in range(4):
                            h = g * HPG + 4 * b + j
                            act.activation(seg[:, b, j * P:(j + 1) * P], acs_rows[b][:, j * P:(j + 1) * P], ACT.Relu,
                                           bias=acs[:, c, h:h + 1], scale=-1.0).then_inc(seg_out, 1)
                        act.wait_ge(seg_out, 4 * (2 * i + b + 1))
                        act.activation(seg[:, b, :], seg[:, b, :], ACT.Exp, scale=-1.0).then_inc(seg_exp, 1)
                act.wait_ge(z_here, 16)
                for i in range(XT):
                    act.activation(z[:, i, :], z[:, i, :], ACT.Silu).then_inc(z_silu, 1)

                def gain_from_psum(n):
                    act.wait_ge(gb_ready, n + 1)
                    for j, bank in enumerate(gain_banks):
                        act.activation(gain[:, n, j * PW:(j + 1) * PW], bank[:], ACT.Copy).then_inc(gb_taken, 1)

                act.wait_ge(p_turned, 1)
                for j, bank in enumerate(p_banks):
                    act.activation(keep.pT[:, j, :], bank[:], ACT.Copy).then_inc(p_out, 1)
                act.activation(keep.turned_gain[:], small_bank[:, 0:2 * DK], ACT.Copy).then_inc(p_out, 1)
                for i in range(XT):
                    act.wait_ge(gated, i + 1)
                    if i >= 2:
                        act.wait_ge(square_used, i - 1)
                    act.activation(sq[:, i % 2, :], y[:, i, :], ACT.Square).then_inc(squared, 1)
                gain_from_psum(0)
                act.wait_ge(mean_out, 1)
                act.activation(rinv[:], rinv[:], ACT.Sqrt).then_inc(root_out, 1)
                gain_from_psum(1)

            @block.vector
            def _(dve):
                step = [0]

                def link(ins):
                    step[0] += 1
                    ins.then_inc(dt_step, 1)
                    dve.wait_ge(dt_step, step[0])

                dve.wait_ge(dt_here, 16)
                every = (P, TT, HEADS)
                link(dve.tensor_tensor(dt[:], dt[:], head[:, 0:HEADS].unsqueeze(1).broadcast_to(every), ALU.add))
                link(dve.tensor_scalar(pos[:], dt[:], 0.0, None, ALU.max))
                link(dve.scalar_tensor_tensor(out=ea[:], in0=pos[:], scalar=2.0, in1=dt[:], op0=ALU.mult, op1=ALU.subtract))
                dve.wait_ge(dt_exp, 2)
                link(dve.tensor_scalar(u1[:], ea[:], 1.0, None, ALU.add))
                link(dve.tensor_scalar(dt[:], u1[:], -1.0, None, ALU.add))
                link(dve.tensor_tensor(dt[:], ea[:], dt[:], ALU.subtract))
                dve.wait_ge(dt_exp, 3)
                link(dve.reciprocal(u1[:], u1[:]))
                link(dve.tensor_tensor(dt[:], dt[:], u1[:], ALU.mult))
                link(dve.tensor_tensor(dt[:], dt[:], acs[:], ALU.add))
                link(dve.tensor_tensor(dt[:], dt[:], pos[:], ALU.add))
                link(dve.tensor_scalar(nega[:], nega[:], -1.0, None, ALU.mult))
                link(dve.tensor_tensor(dta[:], dt[:], nega[:].unsqueeze(1).broadcast_to(every), ALU.mult))
                assert step[0] == DT_STEPS

                dve.wait_ge(dt_exp, DT_EXPS - 1)
                link(dve.tensor_tensor(to_end[:], carry_bank[:, 0:TT * HEADS].rearrange("p (t h) -> p t h", t=TT), acs[:], ALU.subtract))
                dve.wait_ge(dt_exp, DT_EXPS)

                def operands(i):
                    c, g = ITER[i]
                    dve.wait_ge(x_turned, i + 1)
                    if i >= 2:
                        dve.wait_ge(diag_ready, i - 1)
                        dve.wait_ge(xdec_ready, i - 1)
                    dve.tensor_tensor(xdt[:, i % 2, :].rearrange("p (h n) -> p h n", n=HD),
                                      turn_in[:, :].rearrange("p (h n) -> p h n", n=HD),
                                      per_head(dt[:, c, heads_of(g)]), ALU.mult).then_inc(xdt_ready, 1)
                    dve.wait_ge(cb_ready, i + 1)
                    dve.tensor_tensor(cbm[:, i % 2, :], small_bank[:, 0:P], k.upto[:], ALU.mult).then_inc(cbm_ready, 1)
                    if 2 <= i and ITER[i - 2][0] < TT - 1:
                        dve.wait_ge(state_ready, i - 1)
                    dve.tensor_copy(b_tok[:, i % 2, :], small_bank[:, P:2 * P]).then_inc(b_out, 1)
                    dve.wait_ge(cbm_ready, i + 1)
                    for b in range(2):
                        dve.wait_ge(seg_exp, 2 * i + b + 1)
                        dve.tensor_tensor(m[:, i % 2, b, :].rearrange("p (h n) -> p h n", n=P),
                                          seg[:, b, :].rearrange("p (h n) -> p h n", n=P),
                                          cbm[:, i % 2, :].unsqueeze(1).broadcast_to((P, 4, P)), ALU.mult).then_inc(m_ready, 1)

                def results(i):
                    c, g = ITER[i]
                    as_heads = lambda a: a.rearrange("p (h n) -> p h n", n=HD)
                    dve.wait_ge(diag_ready, i + 1)
                    if i >= 2:
                        dve.wait_ge(y_turned, i - 1)
                    if c:
                        dve.wait_ge(off_ready, i - GROUPS + 1)
                        dve.tensor_tensor(as_heads(yoff[:, i % 2, :]), as_heads(carry_bank[:, :]),
                                          per_head(acs_exp[:, c, heads_of(g)]), ALU.mult).then_inc(off_scaled, 1)
                        dve.wait_ge(off_scaled, i - GROUPS + 1)
                        dve.tensor_tensor(ytok[:, i % 2, :], y_bank[:, :], yoff[:, i % 2, :], ALU.add).then_inc(y_ready, 1)
                    else:
                        dve.tensor_copy(ytok[:, i % 2, :], y_bank[:, :]).then_inc(y_ready, 1)
                    if c < TT - 1:
                        dve.wait_ge(state_ready, i + 1)
                        if c:
                            dve.tensor_tensor(as_heads(carry[:, g, :]), as_heads(carry[:, g, :]),
                                              per_head(chunk_decay[:, c, heads_of(g)]), ALU.mult).then_inc(carry_scaled, 1)
                            dve.wait_ge(carry_scaled, i - GROUPS + 1)
                            dve.tensor_tensor(carry[:, g, :], state_bank[:, :], carry[:, g, :], ALU.add).then_inc(carry_ready, 1)
                        else:
                            dve.tensor_copy(carry[:, g, :], state_bank[:, :]).then_inc(carry_ready, 1)

                def skips(i):
                    c, g = ITER[i]
                    dve.wait_ge(y_turned, i + 1)
                    for j in range(4):
                        t = 4 * g + j
                        dve.scalar_tensor_tensor(out=y[:, t, cut(c)], in0=xbc[:, t, cut(c)], scalar=skip(t),
                                                 in1=turn_out[:, j * P:(j + 1) * P], op0=ALU.mult, op1=ALU.add).then_inc(y_skip, 1)

                operands(0)
                for i in range(len(ITER)):
                    if i + 1 < len(ITER):
                        operands(i + 1)
                    results(i)
                    if i:
                        skips(i - 1)
                skips(len(ITER) - 1)
                dve.wait_ge(y_skip, 4 * len(ITER))
                for i in range(XT):
                    dve.wait_ge(z_silu, i + 1)
                    dve.tensor_tensor(y[:, i, :], y[:, i, :], z[:, i, :], ALU.mult).then_inc(gated, 1)
                dve.wait_ge(square_used, XT)
                dve.tensor_scalar(rinv[:], acs_rows[0][:], 1.0 / SSD_W, EPS, ALU.mult, ALU.add).then_inc(mean_out, 1)
                dve.wait_ge(root_out, 1)
                dve.reciprocal(rinv[:], rinv[:]).then_inc(rinv_ready, 1)
                dve.wait_ge(rinv_ready, 1)
                for i in range(XT):
                    dve.scalar_tensor_tensor(out=y[:, i, :], in0=y[:, i, :], scalar=norm(i), in1=rinv[:],
                                             op0=ALU.mult, op1=ALU.mult)

            @block.gpsimd
            def _(pool):
                pool.memset(zeros[:], 0.0).then_inc(zeros_ready, 1)
                pool.wait_ge(dt_exp, DT_EXPS)
                for i, (c, g) in enumerate(ITER):
                    if c == TT - 1:
                        break
                    pool.wait_ge(xdt_ready, i + 1)
                    if i >= 2:
                        pool.wait_ge(state_ready, i - 1)
                    pool.tensor_tensor(xdec[:, i % 2, :].rearrange("p (h n) -> p h n", n=HD),
                                       xdt[:, i % 2, :].rearrange("p (h n) -> p h n", n=HD),
                                       per_head(to_end[:, c, heads_of(g)]), ALU.mult).then_inc(xdec_ready, 1)


DT_STEPS, DT_EXPS = 12, 7

OUT_PANELS = D // PW
CAP = 64
MAX_OVER = SEQ * 2 // CAP - 1
BLOCKS = N_EXP + MAX_OVER
LN_STAT = 6


GU_CHUNKS, DN_CHUNKS = 4, 2
KG = DK // GU_CHUNKS
FT = D_FF // P
DN_W = D // DN_CHUNKS
PAIRS = N_EXP // 2
UW = D // PAIRS
KP = PLE // P
HALF_X = DK // 2


QUARTERS = P // N_EXP


def run_output(nc, k, x, w_out, router_w, router_b, w_gate, w_up, w_down, scr, keep):
    w = w_out[0]
    with ExitStack() as ctx:
        def sb(name, shape, dt=FP32):
            return ctx.enter_context(nc.sbuf_tensor(name, shape, dt))

        def sem(name):
            return k.semaphore(name)

        banks = [ctx.enter_context(nc.psum_tensor(f"obank{i}", [P, PW], FP32)) for i in range(8)]
        acc, side = banks[0:4], banks[4:8]
        turn, (logit_bank, rank_bank, count_bank, misc_bank) = side, acc
        part_bank = rank_bank
        yhi, ylo, whi, wlo, raw = keep.yhi, keep.ylo, keep.whi, keep.wlo, keep.raw
        h = keep.h
        yraw = [h[:, c, :].rearrange("p (k n) -> p k n", n=SEQ) for c in range(CH)]
        gain, turned_gain = keep.gain, keep.turned_gain
        stats = sb("ostats", [P, TT, OUT_PANELS, LN_STAT])
        mv, rstd, shift = sb("omv", [P, TT, 2]), sb("orstd", [P, TT]), sb("oshift", [P, TT])

        x_here, raw_here = sem("ox_here"), [sem(f"oraw_here{c}") for c in range(CH)]
        y_hi, y_lo = sem("y_hi"), sem("y_lo")
        hi_ready, split_ready, split_used = sem("ohi_ready"), sem("osplit_ready"), sem("osplit_used")
        acc_ready, acc_taken, stat_ready = sem("oacc_ready"), sem("oacc_taken"), sem("stat_ready")
        mv_ready, var_ready, root_ready, rstd_ready, shift_ready = \
            sem("mv_ready"), sem("var_ready"), sem("root_ready"), sem("rstd_ready"), sem("shift_ready")
        normed, gained, h_stored = sem("onormed"), sem("gained"), sem("h_stored")
        h_ready = [sem(f"h_ready{t}") for t in range(TT)]
        RAW_FREE, ACC_FREE = CH, TT

        rw = sb("router_sb", [P, DK, N_EXP])
        rb_row = sb("rb_row", [1, N_EXP])
        T8, T32, T1 = [P, TT, N_GRP], [P, TT, N_EXP], [P, TT]
        aff, biased, masked, eq, wgt, sel, dest, over = (sb(n, T32) for n in
                                                         ("aff", "biased", "masked", "eq", "wgt", "sel", "dest", "over"))
        hot = [sb("hot0", T32), sb("hot1", T32)]
        hi1, lo1, hi2, lo2, gs, g_eq, in_grp, pen = (sb(n, T8) for n in ("hi1", "lo1", "hi2", "lo2", "gs", "g_eq", "in_grp", "pen"))
        best, key = sb("best", T1), sb("key", T1)
        gate_sum = sb("gate_sum", T1)
        rank_g, rank_e = sb("rank_g", [P, N_GRP]), sb("rank_e", [P, N_EXP])
        base = sb("base", [P, N_EXP])
        slot_f = sb("slot_f", [P, 2, TT])
        slot_i = keep.slot_i
        token_f = sb("token_f", [P, 2, TT])
        edges, places = sb("edges", [P, BLOCKS + 1]), sb("places", [P, CAP])
        reached, in_block = sb("reached", [P, 2 * TT, BLOCKS + 1]), sb("in_block", [P, 2 * TT, BLOCKS])
        n_reached, place, in_place = sb("n_reached", [P, 2 * TT]), sb("place", [P, 2 * TT]), sb("in_place", [P, 2 * TT, CAP])
        cnt = sb("cnt", [N_EXP, 1])
        blocks = sb("blocks", [N_EXP, 1])
        start, jump = sb("start", [P, N_EXP]), sb("jump", [P, N_EXP])
        ends, numbers = sb("ends", [1, N_EXP]), sb("numbers", [1, MAX_OVER])
        below, owner = sb("below", [1, MAX_OVER, N_EXP]), sb("owner", [1, MAX_OVER])
        parts, folded = sb("parts", [P, SEQ]), sb("folded", [P, N_EXP])

        rw_here = sem("rw_here")
        parts_ready, parts_out, folded_ready = sem("parts_ready"), sem("parts_out"), sem("folded_ready")
        h_out = [sem("h_out_act"), sem("h_out_dve")]
        h_turned, logits_ready, aff_ready = sem("h_turned"), sem("rlogits_ready"), sem("aff_ready")
        filled, step = sem("rfilled"), sem("rstep")
        sel_ready, counts_ready, blocks_ready, starts_ready = sem("sel_ready"), sem("counts_ready"), sem("blocks_ready"), sem("starts_ready")
        placed, table_ready, tokens_ready = sem("placed"), sem("table_ready"), sem("tokens_ready")
        UNITS_H = TT * (DK // 4)

        def units_of(t, n):
            return [u for u in range(t * (DK // 4), (t + 1) * (DK // 4)) if u % 2 == n]

        def out_of_psum(u, j):
            t, kt = u // (DK // 4), 4 * (u % (DK // 4)) + j
            return (keep.hT[:, kt, t * P:(t + 1) * P], turn[u % 4][:, j * P:(j + 1) * P], turned_gain[:, kt:kt + 1],
                    turned_gain[:, DK + kt:DK + kt + 1])

        with nc.Block() as block:
            @block.sync
            def _(sp):
                for t in range(TT):
                    sp.wait_ge(y_lo, t + 1)
                    sp.dma_start(h[:, t, :], x[0, t * P:(t + 1) * P, :]).then_inc(x_here, 16)
                sp.dma_start(rw[:], router_w.rearrange("(k p) n -> p k n", p=P)).then_inc(rw_here, 16)
                sp.dma_start(rb_row[:], router_b.rearrange("(a n) -> a n", a=1)).then_inc(rw_here, 16)
                with sp.Fori(1, OUT_PANELS) as p:
                    for c in range(CH):
                        sp.wait_ge(split_ready, 4 * p + c + 1)
                        rows = w[c * KC * P:(c + 1) * KC * P, :].rearrange("(k p) n -> p k n", p=P)
                        sp.dma_start(raw[:, c], rows[:, :, bass.ds(p * PW, PW)]).then_inc(raw_here[c], 16)
                for j in range(DN_CHUNKS):
                    sp.wait_ge(split_ready, RAW_FREE + 4 * (OUT_PANELS - 1) + 2 * j + 2)
                    sp.dma_start(keep.dn[j][:], w_down[0, 0, :, j * DN_W:(j + 1) * DN_W].rearrange("(f p) n -> p f n", p=P)) \
                        .then_inc(keep.dn_here[j], 16)
                sp.wait_ge(acc_ready, ACC_FREE + TT * OUT_PANELS)
                for j in range(GU_CHUNKS):
                    for side_, v in enumerate((w_gate, w_up)):
                        sp.dma_start(keep.gu[j][:, side_], v[0, 0, j * KG * P:(j + 1) * KG * P, :].rearrange("(k p) n -> p k n", p=P)) \
                            .then_inc(keep.gu_here[j], 16)
                for t in range(TT):
                    sp.wait_ge(h_ready[t], 1)
                    sp.dma_start(scr.h1[t * P:(t + 1) * P, :], h[:, t, :]).then_inc(h_stored, 16)
                sp.wait_ge(h_stored, 16 * TT)

            @block.tensor
            def _(pe):
                pe.sem_inc(acc_ready, ACC_FREE)
                with pe.Fori(0, OUT_PANELS) as p:
                    for c in range(CH):
                        s = c % SPLIT_SLOTS
                        pe.wait_ge(y_lo, c + 1)
                        pe.wait_ge(split_ready, RAW_FREE + 4 * p + c + 1)
                        for t in range(TT):
                            if c == 0:
                                pe.wait_ge(acc_taken, 4 * p + t + 1)
                            for kk in range(KC):
                                kt = c * KC + kk
                                high, low = yhi[:, kt, t * P:(t + 1) * P], ylo[:, kt, t * P:(t + 1) * P]
                                for n, (a, b) in enumerate(((high, whi[s]), (high, wlo[s]), (low, whi[s]))):
                                    last = pe.matmul(acc[t][:], a, b[:, kk, :],
                                                     start=(c == 0 and kk == 0 and n == 0),
                                                     stop=(c == CH - 1 and kk == KC - 1 and n == 2))
                            if c == CH - 1:
                                last.then_inc(acc_ready, 1)
                            elif t == TT - 1:
                                last.then_inc(split_used, 1)
                for u in range(UNITS_H):
                    t, g = u // (DK // 4), u % (DK // 4)
                    pe.wait_ge(normed, t + 1)
                    if u >= 4:
                        pe.wait_ge(h_out[u % 2], (u - 4) // 2 + 1)
                    for j in range(4):
                        last = pe.transpose(turn[u % 4][:, j * P:(j + 1) * P], h[:, t, (4 * g + j) * P:(4 * g + j + 1) * P], k.ident[:])
                    last.then_inc(h_turned, 1)
                pe.wait_ge(rw_here, 32)
                pe.matmul(misc_bank[:, 0:N_EXP], k.ones[0:1, :], rb_row[:], start=True, stop=True)
                for n in range(2):
                    pe.wait_ge(h_out[n], UNITS_H // 2)
                for kt in range(DK):
                    q = kt % QUARTERS
                    last = pe.matmul(part_bank[q * N_EXP:(q + 1) * N_EXP, :], rw[:, kt, :], keep.hT[:, kt, :],
                                     start=(kt < QUARTERS), stop=(kt >= DK - QUARTERS))
                last.then_inc(parts_ready, 1)
                pe.wait_ge(parts_out, 1)
                pe.wait_ge(folded_ready, 1)
                for t in range(TT):
                    last = pe.matmul(logit_bank[:, t * N_EXP:(t + 1) * N_EXP], parts[:, t * P:(t + 1) * P], folded[:],
                                     start=True, stop=True)
                last.then_inc(logits_ready, 1)
                pe.wait_ge(sel_ready, 1)
                for t in range(TT):
                    for s in range(t + 1):
                        pe.matmul(rank_bank[:, t * N_EXP:(t + 1) * N_EXP], (k.strict if s == t else k.ones)[:], sel[:, s, :],
                                  start=(s == 0), stop=(s == t))
                for t in range(TT):
                    last = pe.matmul(count_bank[0:N_EXP, 0:1], sel[:, t, :], k.ones[:, 0:1], start=(t == 0), stop=(t == TT - 1))
                last.then_inc(counts_ready, 1)
                pe.wait_ge(blocks_ready, 1)
                own = blocks[:, 0:1].broadcast_to((N_EXP, P))
                pe.matmul(misc_bank[:, 0:N_EXP], own, k.strict[0:N_EXP, 0:N_EXP], start=True, stop=True)
                pe.matmul(misc_bank[0:1, N_EXP:2 * N_EXP], blocks[:, 0:1], k.upto[0:N_EXP, 0:N_EXP], start=True, stop=True).then_inc(starts_ready, 1)
                pe.wait_ge(placed, 1)
                for r in range(2 * TT):
                    last = pe.matmul(turn[0][0:CAP, 0:BLOCKS], in_place[:, r, :], in_block[:, r, :], start=(r == 0), stop=(r == 2 * TT - 1))
                last.then_inc(table_ready, 1)

            @block.scalar
            def _(act):
                for c in range(CH):
                    act.sem_inc(raw_here[c], 16)

                def high(c, p):
                    act.wait_ge(raw_here[c], 16 * (p + 1))
                    act.activation(whi[c % SPLIT_SLOTS][:], raw[:, c], ACT.Copy).then_inc(hi_ready, 1)

                def high_next(c, p, more=True):
                    if c == 1:
                        act.wait_ge(acc_ready, 4 * p + TT)
                        high(1, p)
                    elif c in (2, 3):
                        act.wait_ge(split_used, 3 * p + c - 1)
                        high(c, p)
                    elif more:
                        act.wait_ge(split_used, 3 * p + 3)
                        high(0, p + 1)

                for c in range(CH):
                    act.activation(yhi[:, c * KC:(c + 1) * KC, :], yraw[c], ACT.Copy).then_inc(y_hi, 1)
                    if c == 0:
                        high(0, 0)
                with act.Fori(0, OUT_PANELS - 1) as p:
                    for c in (1, 2, 3, 0):
                        high_next(c, p)
                for c in (1, 2, 3, 0):
                    high_next(c, OUT_PANELS - 1, more=False)

                def turned(t):
                    for u in units_of(t, 0):
                        act.wait_ge(h_turned, u + 1)
                        for j in range(4):
                            place, source, g, b = out_of_psum(u, j)
                            last = act.activation(place, source, ACT.Identity, bias=b, scale=g)
                        last.then_inc(h_out[0], 1)

                for t in range(TT):
                    act.wait_ge(var_ready, t + 1)
                    act.activation(rstd[:, t:t + 1], rstd[:, t:t + 1], ACT.Sqrt).then_inc(root_ready, 1)
                    act.wait_ge(shift_ready, t + 1)
                    act.activation(h[:, t, :], h[:, t, :], ACT.Identity, bias=shift[:, t:t + 1], scale=rstd[:, t:t + 1]).then_inc(normed, 1)
                    if t:
                        turned(t - 1)
                turned(TT - 1)
                act.wait_ge(parts_ready, 1)
                act.activation(parts[:], part_bank[:], ACT.Copy).then_inc(parts_out, 1)
                act.wait_ge(logits_ready, 1)
                act.activation(aff[:], logit_bank[:, 0:TT * N_EXP].rearrange("p (t n) -> p t n", t=TT), ACT.Sigmoid).then_inc(aff_ready, 1)

            @block.vector
            def _(dve):
                dve.sem_inc(split_ready, RAW_FREE)
                dve.sem_inc(acc_taken, ACC_FREE)
                def low(c, p):
                    dve.wait_ge(hi_ready, 4 * p + c + 1)
                    s = c % SPLIT_SLOTS
                    dve.tensor_tensor(wlo[s][:], raw[:, c], whi[s][:].bitcast(FP32), ALU.subtract).then_inc(split_ready, 1)

                def evacuate(p, tiles=range(TT)):
                    for t in tiles:
                        here = h[:, t, bass.ds(p * PW, PW)]
                        dve.wait_ge(acc_ready, ACC_FREE + 4 * p + t + 1)
                        dve.scalar_tensor_tensor(out=here, in0=here, scalar=ALPHA, in1=acc[t][:],
                                                 op0=ALU.mult, op1=ALU.add).then_inc(acc_taken, 1)
                        dve.wait_ge(acc_taken, ACC_FREE + 4 * p + t + 1)
                        dve.bn_stats(stats[:, t, bass.ds(p, 1), :] if not isinstance(p, int) else stats[:, t, p:p + 1, :],
                                     here).then_inc(stat_ready, 1)

                dve.wait_ge(filled, 8)
                dve.tensor_reduce(folded[:], k.ident[:].rearrange("p (q n) -> p n q", q=QUARTERS), AX.X, ALU.add).then_inc(folded_ready, 1)
                for c in range(CH):
                    cut = (slice(None), slice(c * KC, (c + 1) * KC))
                    dve.wait_ge(y_hi, c + 1)
                    dve.tensor_tensor(ylo[cut], yraw[c], yhi[cut].bitcast(FP32), ALU.subtract).then_inc(y_lo, 1)
                    if c == 0:
                        low(0, 0)
                with dve.Fori(0, OUT_PANELS - 1) as p:
                    for c in range(1, CH):
                        low(c, p)
                    low(0, p + 1)
                    dve.wait_ge(x_here, 16 * TT)
                    evacuate(p)
                for c in range(1, CH):
                    low(c, OUT_PANELS - 1)

                def turned(t):
                    for u in units_of(t, 1):
                        dve.wait_ge(h_turned, u + 1)
                        for j in range(4):
                            place, source, g, b = out_of_psum(u, j)
                            last = dve.tensor_scalar(place, source, g, b, ALU.mult, ALU.add)
                        last.then_inc(h_out[1], 1)

                for t in range(TT):
                    evacuate(OUT_PANELS - 1, [t])
                    dve.wait_ge(stat_ready, TT * (OUT_PANELS - 1) + t + 1)
                    dve.bn_aggr(mv[:, t, :], stats[:, t, :, :].rearrange("p a b -> p (a b)")).then_inc(mv_ready, 1)
                    dve.wait_ge(mv_ready, t + 1)
                    dve.tensor_scalar(rstd[:, t:t + 1], mv[:, t, 1:2], EPS, None, ALU.add).then_inc(var_ready, 1)
                    dve.wait_ge(root_ready, t + 1)
                    dve.reciprocal(rstd[:, t:t + 1], rstd[:, t:t + 1]).then_inc(rstd_ready, 1)
                    dve.wait_ge(rstd_ready, t + 1)
                    dve.scalar_tensor_tensor(out=shift[:, t:t + 1], in0=mv[:, t, 0:1], scalar=-1.0, in1=rstd[:, t:t + 1],
                                             op0=ALU.mult, op1=ALU.mult).then_inc(shift_ready, 1)
                    if t:
                        turned(t - 1)
                turned(TT - 1)

                count = [0]

                def link(ins):
                    count[0] += 1
                    ins.then_inc(step, 1)
                    dve.wait_ge(step, count[0])

                def tt(out, a, b, op):
                    link(dve.tensor_tensor(out, a, b, op))

                def last_max(values, weights, out, n):
                    every = (P, TT, n)
                    link(dve.tensor_reduce(best[:], values, AX.X, ALU.max))
                    tt(out, values, best[:].unsqueeze(2).broadcast_to(every), ALU.is_equal)
                    tt(out, out, weights.unsqueeze(1).broadcast_to(every), ALU.mult)
                    link(dve.tensor_reduce(key[:], out, AX.X, ALU.max))
                    tt(out, out, key[:].unsqueeze(2).broadcast_to(every), ALU.is_equal)

                dve.wait_ge(aff_ready, 1)
                tt(biased[:], aff[:], misc_bank[:, 0:N_EXP].unsqueeze(1).broadcast_to((P, TT, N_EXP)), ALU.add)
                a, b, c, d = (biased[:].rearrange("p t (g n) -> p t g n", n=PER_GRP)[:, :, :, j] for j in range(PER_GRP))
                tt(hi1[:], a, b, ALU.max)
                tt(lo1[:], a, b, ALU.min)
                tt(hi2[:], c, d, ALU.max)
                tt(lo2[:], c, d, ALU.min)
                tt(gs[:], hi1[:], hi2[:], ALU.max)
                tt(hi1[:], hi1[:], hi2[:], ALU.min)
                tt(lo1[:], lo1[:], lo2[:], ALU.max)
                tt(hi1[:], hi1[:], lo1[:], ALU.max)
                tt(gs[:], gs[:], hi1[:], ALU.add)
                last_max(gs[:], rank_g[:], in_grp[:], N_GRP)
                link(dve.tensor_scalar(pen[:], in_grp[:], -1.0, -NEG, ALU.add, ALU.mult))
                four = lambda v: v.rearrange("p t g -> p (t g)").unsqueeze(2).broadcast_to((P, TT * N_GRP, PER_GRP))
                by_four = lambda v: v.rearrange("p t (g n) -> p (t g) n", n=PER_GRP)
                tt(by_four(masked[:]), by_four(biased[:]), four(in_grp[:]), ALU.mult)
                tt(by_four(masked[:]), by_four(masked[:]), four(pen[:]), ALU.add)
                for n in range(2):
                    last_max(masked[:], rank_e[:], hot[n][:], N_EXP)
                    if n == 0:
                        link(dve.scalar_tensor_tensor(out=masked[:], in0=hot[0][:], scalar=2 * NEG, in1=masked[:],
                                                      op0=ALU.mult, op1=ALU.add))
                    tt(eq[:], aff[:], hot[n][:], ALU.mult)
                    link(dve.tensor_reduce(keep.gate[:, n, :], eq[:], AX.X, ALU.add))
                dve.tensor_tensor(sel[:], hot[0][:], hot[1][:], ALU.add).then_inc(sel_ready, 1)
                tt(gate_sum[:], keep.gate[:, 0, :], keep.gate[:, 1, :], ALU.add)
                link(dve.reciprocal(gate_sum[:], gate_sum[:]))
                tt(keep.gate[:], keep.gate[:], gate_sum[:].unsqueeze(1).broadcast_to((P, 2, TT)), ALU.mult)
                dve.wait_ge(counts_ready, 1)
                link(dve.tensor_copy(cnt[:], count_bank[0:N_EXP, 0:1]))
                link(dve.tensor_scalar(blocks[:], cnt[:], float(CAP), None, ALU.is_gt))
                for j in range(2, SEQ // CAP):
                    link(dve.scalar_tensor_tensor(out=blocks[:], in0=cnt[:], scalar=float(j * CAP), in1=blocks[:],
                                                  op0=ALU.is_gt, op1=ALU.add))
                dve.sem_inc(blocks_ready, 1)
                dve.wait_ge(starts_ready, 1)
                link(dve.tensor_scalar(start[:], misc_bank[:, 0:N_EXP], float(CAP), float(CAP * (N_EXP - 1)), ALU.mult, ALU.add))
                tt(jump[:], start[:], base[:], ALU.subtract)
                link(dve.tensor_copy(ends[:], misc_bank[0:1, N_EXP:2 * N_EXP]))
                rank = rank_bank[:, 0:TT * N_EXP].rearrange("p (t n) -> p t n", t=TT)
                every = (P, TT, N_EXP)
                link(dve.tensor_scalar(over[:], rank, float(CAP), None, ALU.is_ge))
                tt(over[:], over[:], jump[:].unsqueeze(1).broadcast_to(every), ALU.mult)
                tt(over[:], over[:], base[:].unsqueeze(1).broadcast_to(every), ALU.add)
                tt(dest[:], rank, over[:], ALU.add)
                for n in range(2):
                    tt(eq[:], dest[:], hot[n][:], ALU.mult)
                    link(dve.tensor_reduce(slot_f[:, n, :], eq[:], AX.X, ALU.add))
                slots = slot_f[:].rearrange("p n t -> p (n t)")
                by_block, by_place = (P, 2 * TT, BLOCKS + 1), (P, 2 * TT, CAP)
                tt(reached[:], slots.unsqueeze(2).broadcast_to(by_block), edges[:].unsqueeze(1).broadcast_to(by_block), ALU.is_ge)
                link(dve.tensor_reduce(n_reached[:], reached[:], AX.X, ALU.add))
                link(dve.scalar_tensor_tensor(out=place[:], in0=n_reached[:], scalar=-float(CAP), in1=slots, op0=ALU.mult, op1=ALU.add))
                tt(in_block[:], reached[:, :, 0:BLOCKS], reached[:, :, 1:BLOCKS + 1], ALU.subtract)
                tt(in_place[:], place[:].unsqueeze(2).broadcast_to(by_place), places[:].unsqueeze(1).broadcast_to(by_place), ALU.is_equal)
                tokens = token_f[:].rearrange("p n t -> p (n t)")
                dve.tensor_tensor(in_place[:], in_place[:], tokens.unsqueeze(2).broadcast_to(by_place), ALU.mult).then_inc(placed, 1)
                link(dve.tensor_copy(slot_i[:], slot_f[:]))
                tt(below[:], ends[:].unsqueeze(1).broadcast_to((1, MAX_OVER, N_EXP)),
                   numbers[:].unsqueeze(2).broadcast_to((1, MAX_OVER, N_EXP)), ALU.is_le)
                link(dve.tensor_reduce(owner[:], below[:], AX.X, ALU.add))
                link(dve.tensor_scalar(owner[:], owner[:], float(N_EXP - 1), None, ALU.min))
                link(dve.tensor_copy(keep.over_info[:, 1:1 + MAX_OVER], owner[:]))
                link(dve.tensor_copy(keep.over_info[:, 0:1], ends[:, N_EXP - 1:N_EXP]))
                dve.wait_ge(table_ready, 1)
                dve.tensor_copy(keep.slot_token[:], turn[0][0:CAP, 0:BLOCKS]).then_inc(tokens_ready, 1)

            @block.gpsimd
            def _(pool):
                iota = lambda out, pattern, base, mult: pool.iota(out, pattern, base=base, channel_multiplier=mult,
                                                                 allow_small_or_imprecise_dtypes=True).then_inc(filled, 1)
                iota(rank_g[:], [[-1, N_GRP]], N_GRP, 0)
                iota(rank_e[:], [[-1, N_EXP]], N_EXP, 0)
                iota(base[:], [[CAP, N_EXP]], 0, 0)
                iota(token_f[:], [[0, 2], [P, TT]], 0, 1)
                iota(edges[:], [[CAP, BLOCKS + 1]], 0, 0)
                iota(places[:], [[1, CAP]], -CAP, 0)
                iota(numbers[:], [[1, MAX_OVER]], 0, 0)
                pool.memset(keep.over_info[:], 0).then_inc(filled, 1)
                for t in range(TT):
                    pool.wait_ge(h_turned, (t + 1) * (DK // 4))
                    pool.tensor_tensor(h[:, t, :], h[:, t, :], gain[:, 0, :], ALU.mult).then_inc(gained, 1)
                    pool.wait_ge(gained, t + 1)
                    pool.tensor_tensor(h[:, t, :], h[:, t, :], gain[:, 1, :], ALU.add).then_inc(h_ready[t], 1)


def run_moe(nc, k, w_gate, w_up, w_down, ple_w, ple_gate_w, scr, keep):
    wg, wu, wd = w_gate[0], w_up[0], w_down[0]
    with ExitStack() as ctx:
        def sb(name, shape, dt=FP32):
            return ctx.enter_context(nc.sbuf_tensor(name, shape, dt))

        def sem(name):
            return k.semaphore(name)

        banks = [ctx.enter_context(nc.psum_tensor(f"mbank{i}", [P, PW], FP32)) for i in range(8)]
        turn, hid, turned_hid, down, gate_bank, emb_bank = banks[0:2], banks[2], banks[3], banks[4:6], banks[6], banks[7]
        gu, dn, pT = keep.gu, keep.dn, keep.pT
        pg = keep.gain[:, 1, :].rearrange("p (k n) -> p k n", n=UW)
        pw = sb("pw", [P, KP, UW])
        sig_emb = sb("sig_emb", [P, TT, UW])
        xg, xT = sb("xg", [CAP, D]), sb("xT", [P, DK, CAP])
        act_sig, hid_sb = sb("act_sig", [P, FT, CAP]), sb("hid_sb", [P, FT, CAP])
        both_sb = sb("both_sb", [P, D_FF])
        y_out = [keep.gain[:, 0, i * 2 * PW:(i + 1) * 2 * PW].rearrange("p (b n) -> p b n", n=PW) for i in range(2)]
        token = sb("token", [CAP, 1], I32)

        gu_here, dn_here = keep.gu_here, keep.dn_here
        gu_used = sem("gu_used")
        emb_here, emb_used, gate_ready = sem("emb_here"), sem("emb_used"), sem("gate_ready")
        emb_sig, emb_step, emb_done = sem("emb_sig"), sem("emb_step"), sem("emb_done")
        token_ready = sem("token_ready")
        x_here = sem("mx_here")
        x_turned, x_out = sem("mx_turned"), sem("mx_out")
        hid_ready, sig_ready, half_ready, act_ready = sem("hid_ready"), sem("sig_ready"), sem("half_ready"), sem("act_ready")
        down_ready, y_out_ready = sem("down_ready"), sem("y_out_ready")
        y_stored = [sem(f"my_stored{i}") for i in range(2)]

        def gu_source(e, j):
            rows = slice(j * KG * P, (j + 1) * KG * P)
            return [v[e, rows, :].rearrange("(k p) n -> p k n", p=P) for v in (wg, wu)]

        def dn_source(e, j):
            return wd[e, :, j * DN_W:(j + 1) * DN_W].rearrange("(f p) n -> p f n", p=P)

        def turn_x(pe, done, free=None):
            for half in range(2):
                if free is not None:
                    pe.wait_ge(x_out, free + half)
                pe.sem_inc(mpassed_pe, 1)
                for j in range(HALF_X):
                    kt = half * HALF_X + j
                    last = pe.transpose(turn[half][:, j * CAP:(j + 1) * CAP], xg[:, kt * P:(kt + 1) * P], k.ident[0:CAP, 0:CAP])
                last.then_inc(done, 1)

        def hidden(pe, j):
            for kk in range(KG):
                kt = j * KG + kk
                for side in range(2):
                    last = pe.matmul(hid[side * CAP:(side + 1) * CAP, :], xT[:, kt, :], gu[j][:, side, kk, :],
                                     start=(kt == 0), stop=(kt == DK - 1))
            return last

        def turn_hidden(pe):
            for f in range(FT):
                last = pe.transpose(turned_hid[:, f * P:(f + 1) * P], both_sb[:, f * P:(f + 1) * P], k.ident[:])
            return last

        def down_product(pe, b):
            for f in range(FT):
                for half in range(2):
                    last = pe.matmul(down[b][half * CAP:(half + 1) * CAP, :], hid_sb[:, f, :],
                                     dn[b][:, f, half * PW:(half + 1) * PW], start=(f == 0), stop=(f == FT - 1))
            return last

        def token_copy(dve, block, done):
            dve.tensor_copy(token[:], keep.slot_token[:, bass.ds(block, 1)] if not isinstance(block, int)
                            else keep.slot_token[:, block:block + 1]).then_inc(done, 1)

        def x_from_psum(act, half, done):
            act.activation(xT[:, half * HALF_X:(half + 1) * HALF_X, :],
                           turn[half][:, :].rearrange("p (k n) -> p k n", n=CAP), ACT.Copy).then_inc(done, 1)

        def store(eng, i, block, done):
            rows = scr.yb[bass.ds(block * CAP, CAP), :].rearrange("r (b h n) -> h r b n", h=2, n=PW)
            for half in range(2):
                eng.dma_start(rows[half], y_out[i][half * CAP:(half + 1) * CAP]).then_inc(done, 16)

        turned = turned_hid[:, :].rearrange("p (f n) -> p f n", n=P)
        gate_turned, up_turned = turned[:, :, 0:CAP], turned[:, :, CAP:2 * CAP]
        hid_out, hid_turned, ov_hid_out, ov_hid_turned = (sem(n) for n in ("hid_out", "hid_turned", "ov_hid_out", "ov_hid_turned"))
        ov_here, ov_token, ov_x, ov_turned, ov_x_out = (sem(n) for n in ("ov_here", "ov_token", "ov_x", "ov_turned", "ov_x_out"))
        ov_hidden, ov_sig, ov_half, ov_act = (sem(n) for n in ("ov_hidden", "ov_sig", "ov_half", "ov_act"))
        ov_down, ov_y_out, ov_stored = (sem(n) for n in ("ov_down", "ov_y_out", "ov_stored"))
        mpassed_pe, mpassed_pool, mpassed_act = sem("mpassed_pe"), sem("mpassed_pool"), sem("mpassed_act")
        OV_DMAS = 2 * GU_CHUNKS + DN_CHUNKS
        STORED = 32

        def blocks_beyond(eng):
            return eng.value_load(keep.over_info[0:1, 0:1], min_val=0, max_val=MAX_OVER)

        with nc.Block() as block:
            @block.sync
            def _(sp):
                def gate_and_up(e):
                    for j in range(GU_CHUNKS):
                        sp.wait_ge(gu_used, GU_CHUNKS * (e - 1) + j + 1)
                        for side, v in enumerate((wg, wu)):
                            rows = v[e, j * KG * P:(j + 1) * KG * P, :].rearrange("(k p) n -> p k n", p=P)
                            sp.dma_start(gu[j][:, side], rows).then_inc(gu_here[j], 16)

                def down_weights(e):
                    for j in range(DN_CHUNKS):
                        sp.wait_ge(down_ready, DN_CHUNKS * (e - 1) + j + 1)
                        rows = wd[e, :, j * DN_W:(j + 1) * DN_W].rearrange("(f p) n -> p f n", p=P)
                        sp.dma_start(dn[j][:], rows).then_inc(dn_here[j], 16)

                def embedding(n):
                    cols = bass.ds(n * UW, UW) if not isinstance(n, int) else slice(n * UW, (n + 1) * UW)
                    sp.dma_start(pg, ple_gate_w[0].rearrange("(k p) n -> p k n", p=P)[:, :, cols]).then_inc(emb_here, 16)
                    sp.dma_start(pw[:], ple_w[0].rearrange("(k p) n -> p k n", p=P)[:, :, cols]).then_inc(emb_here, 16)

                embedding(0)
                with sp.Fori(0, PAIRS - 1) as n:
                    gate_and_up(2 * n + 1)
                    down_weights(2 * n + 1)
                    gate_and_up(2 * n + 2)
                    sp.wait_ge(emb_used, n + 1)
                    embedding(n + 1)
                    down_weights(2 * n + 2)
                gate_and_up(N_EXP - 1)
                down_weights(N_EXP - 1)

                over = blocks_beyond(sp)
                with sp.If(over > 0):
                    with sp.Fori(0, over) as b:
                        sp.wait_ge(ov_down, DN_CHUNKS * b + 1)
                        e = sp.value_load(keep.over_info[0:1, bass.ds(b + 1, 1)], min_val=0, max_val=N_EXP - 1)
                        for j in range(GU_CHUNKS):
                            for side, v in enumerate((w_gate, w_up)):
                                sp.dma_start(gu[j][:, side], v[0, bass.ds(e, 1), j * KG * P:(j + 1) * KG * P, :]
                                             .rearrange("a (k p) n -> p (a k) n", p=P)).then_inc(ov_here, 16)
                        for j in range(DN_CHUNKS):
                            sp.dma_start(dn[j][:], w_down[0, bass.ds(e, 1), :, j * DN_W:(j + 1) * DN_W]
                                         .rearrange("a (f p) n -> p (a f) n", p=P)).then_inc(ov_here, 16)

            @block.tensor
            def _(pe):
                pe.wait_ge(x_here, 16)
                turn_x(pe, x_turned)

                def embedding(n, half):
                    if half == 0:
                        pe.wait_ge(emb_here, 32 * (n + 1))
                        pe.wait_ge(emb_done, n + 1)
                    for t in range(half * TT // 2, (half + 1) * TT // 2):
                        for kt in range(DK):
                            last = pe.matmul(gate_bank[:, t * UW:(t + 1) * UW], keep.hT[:, kt, t * P:(t + 1) * P], pg[:, kt, :],
                                             start=(kt == 0), stop=(kt == DK - 1))
                    if half:
                        last.then_inc(gate_ready, 1)
                        for t in range(TT):
                            for kt in range(KP):
                                last = pe.matmul(emb_bank[:, t * UW:(t + 1) * UW], pT[:, kt, t * P:(t + 1) * P], pw[:, kt, :],
                                                 start=(kt == 0), stop=(kt == KP - 1))
                        last.then_inc(emb_used, 1)

                with pe.Fori(0, PAIRS) as n:
                    for i in range(2):
                        e = 2 * n + i
                        for j in range(GU_CHUNKS):
                            pe.wait_ge(gu_here[j], 32 * (e + 1))
                            if j == 0:
                                pe.wait_ge(x_out, 2 * (e + 1))
                                pe.wait_ge(hid_out, e + 1)
                            hidden(pe, j).then_inc(gu_used, 1)
                        pe.wait_ge(hid_out, 1 + e + 1)
                        pe.wait_ge(act_ready, e + 1)
                        turn_hidden(pe).then_inc(hid_turned, 1)
                        embedding(n, i)
                        pe.wait_ge(x_here, 16 * (e + 2))
                        turn_x(pe, x_turned, free=2 * e + 1)
                        pe.wait_ge(act_ready, 1 + e + 1)
                        for b in range(DN_CHUNKS):
                            pe.wait_ge(dn_here[b], 16 * (e + 1))
                            pe.wait_ge(y_out_ready, 2 * e + b + 1)
                            down_product(pe, b).then_inc(down_ready, 1)

                pe.wait_ge(down_ready, DN_CHUNKS * N_EXP)
                pe.wait_ge(y_out_ready, DN_CHUNKS * (N_EXP + 1))
                pe.wait_ge(x_out, 2 * (N_EXP + 1))
                pe.sem_inc(ov_down, 1)
                over = blocks_beyond(pe)
                with pe.If(over > 0):
                    with pe.Fori(0, over) as b:
                        pe.wait_ge(ov_x, 16 * (b + 1))
                        turn_x(pe, ov_turned)
                        pe.wait_ge(ov_here, 16 * OV_DMAS * (b + 1))
                        pe.wait_ge(ov_x_out, 2 * (b + 1))
                        for j in range(GU_CHUNKS):
                            last = hidden(pe, j)
                        last.then_inc(ov_hidden, 1)
                        pe.wait_ge(ov_hid_out, b + 1)
                        turn_hidden(pe).then_inc(ov_hid_turned, 1)
                        pe.wait_ge(ov_act, b + 1)
                        for c in range(DN_CHUNKS):
                            pe.wait_ge(ov_y_out, DN_CHUNKS * b + c + 1)
                            down_product(pe, c).then_inc(ov_down, 1)

            @block.scalar
            def _(act):
                act.sem_inc(y_out_ready, DN_CHUNKS)
                act.sem_inc(hid_out, 1)
                act.sem_inc(ov_y_out, DN_CHUNKS)
                for i in range(2):
                    act.sem_inc(y_stored[i], STORED)
                for half in range(2):
                    act.wait_ge(x_turned, half + 1)
                    x_from_psum(act, half, x_out)
                with act.Fori(0, PAIRS) as n:
                    for i in range(2):
                        e = 2 * n + i
                        act.wait_ge(gu_used, GU_CHUNKS * (e + 1))
                        act.activation(both_sb[:], hid[:], ACT.Copy).then_inc(hid_out, 1)
                        act.wait_ge(hid_turned, e + 1)
                        act.activation(act_sig[:], gate_turned, ACT.Sigmoid).then_inc(sig_ready, 1)
                        if i:
                            act.wait_ge(gate_ready, n + 1)
                            act.activation(sig_emb[:], gate_bank[:, :].rearrange("p (t n) -> p t n", n=UW), ACT.Sigmoid).then_inc(emb_sig, 1)
                        for half in range(2):
                            act.wait_ge(x_turned, 2 * (e + 1) + half + 1)
                            x_from_psum(act, half, x_out)
                        act.wait_ge(y_stored[i], STORED * (n + 1))
                        for b in range(DN_CHUNKS):
                            act.wait_ge(down_ready, DN_CHUNKS * e + b + 1)
                            act.activation(y_out[i][:, b, :], down[b][:], ACT.Copy).then_inc(y_out_ready, 1)
                        act.wait_ge(y_out_ready, DN_CHUNKS * (e + 2))
                        act.sem_inc(mpassed_act, 1)
                        store(act, i, e, y_stored[i])
                for i in range(2):
                    act.wait_ge(y_stored[i], STORED * (PAIRS + 1))
                over = blocks_beyond(act)
                with act.If(over > 0):
                    with act.Fori(0, over) as b:
                        for half in range(2):
                            act.wait_ge(ov_turned, 2 * b + half + 1)
                            x_from_psum(act, half, ov_x_out)
                        act.wait_ge(ov_hidden, b + 1)
                        act.activation(both_sb[:], hid[:], ACT.Copy).then_inc(ov_hid_out, 1)
                        act.wait_ge(ov_hid_turned, b + 1)
                        act.activation(act_sig[:], gate_turned, ACT.Sigmoid).then_inc(ov_sig, 1)
                        for c in range(DN_CHUNKS):
                            act.wait_ge(ov_down, 1 + DN_CHUNKS * b + c + 1)
                            act.activation(y_out[0][:, c, :], down[c][:], ACT.Copy).then_inc(ov_y_out, 1)
                        act.wait_ge(ov_y_out, DN_CHUNKS * (b + 2))
                        act.sem_inc(mpassed_act, 1)
                        store(act, 0, b + N_EXP, ov_stored)
                        act.wait_ge(ov_stored, STORED * (b + 1))

            @block.vector
            def _(dve):
                dve.sem_inc(act_ready, 1)
                dve.sem_inc(emb_done, 1)
                token_copy(dve, 0, token_ready)
                with dve.Fori(0, PAIRS) as n:
                    for i in range(2):
                        e = 2 * n + i
                        dve.wait_ge(x_turned, 2 * (e + 1))
                        token_copy(dve, e + 1, token_ready)
                        dve.wait_ge(sig_ready, e + 1)
                        dve.tensor_tensor(act_sig[:], gate_turned, act_sig[:], ALU.mult).then_inc(half_ready, 1)
                        dve.wait_ge(half_ready, e + 1)
                        dve.tensor_tensor(hid_sb[:], up_turned, act_sig[:], ALU.mult).then_inc(act_ready, 1)
                        if i:
                            dve.wait_ge(emb_sig, n + 1)
                            dve.wait_ge(emb_used, n + 1)
                            emb = emb_bank[:, :].rearrange("p (t n) -> p t n", n=UW)
                            dve.tensor_tensor(sig_emb[:], emb, sig_emb[:], ALU.mult).then_inc(emb_step, 1)
                            dve.wait_ge(emb_step, n + 1)
                            here = keep.h[:, :, bass.ds(n * UW, UW)]
                            dve.scalar_tensor_tensor(out=here, in0=here, scalar=ALPHA, in1=sig_emb[:],
                                                     op0=ALU.mult, op1=ALU.add).then_inc(emb_done, 1)
                over = blocks_beyond(dve)
                with dve.If(over > 0):
                    with dve.Fori(0, over) as b:
                        dve.wait_ge(ov_down, DN_CHUNKS * b + 1)
                        token_copy(dve, b + N_EXP, ov_token)
                        dve.wait_ge(ov_sig, b + 1)
                        dve.tensor_tensor(act_sig[:], gate_turned, act_sig[:], ALU.mult).then_inc(ov_half, 1)
                        dve.wait_ge(ov_half, b + 1)
                        dve.tensor_tensor(hid_sb[:], up_turned, act_sig[:], ALU.mult).then_inc(ov_act, 1)

            @block.gpsimd
            def _(pool):
                def gather(done):
                    pool.sem_inc(mpassed_pool, 1)
                    pool.indirect_dma_start(out=xg[:], out_offset=None, in_=scr.h1,
                                            in_offset=bass.IndirectOffsetOnAxis(ap=token[:, 0:1], axis=0)).then_inc(done, 16)

                pool.wait_ge(token_ready, 1)
                gather(x_here)
                with pool.Fori(0, N_EXP) as e:
                    pool.wait_ge(token_ready, 1 + e + 1)
                    gather(x_here)
                over = blocks_beyond(pool)
                with pool.If(over > 0):
                    with pool.Fori(0, over) as b:
                        pool.wait_ge(ov_token, b + 1)
                        gather(ov_x)


def run_result(nc, k, ln_g, ln_b, scr, keep, out):
    with ExitStack() as ctx:
        def sb(name, shape, dt=FP32):
            return ctx.enter_context(nc.sbuf_tensor(name, shape, dt))

        def sem(name):
            return k.semaphore(name)

        banks = [ctx.enter_context(nc.psum_tensor(f"fbank{i}", [P, PW], FP32)) for i in range(8)]
        gain = keep.gain
        res = keep.h
        y = [sb(f"fy{n}", [P, TT, D]) for n in range(2)]
        stats = sb("fstats", [P, TT, D // PW, 6])
        mv, rstd, shift = sb("fmv", [P, TT, 2]), sb("frstd", [P, TT]), sb("fshift", [P, TT])
        rows_here, gain_ready, gain_out = sem("frows_here"), sem("fgain_ready"), sem("fgain_out")
        y_here = [[sem(f"fy_here{n}{t}") for t in range(TT)] for n in range(2)]
        first_added, summed, stat_ready, mv_ready, var_ready = (sem(n) for n in ("first_added", "summed", "fstat_ready", "fmv_ready", "fvar_ready"))
        root_ready, rstd_ready, shift_ready, normed, gained, out_stored = \
            (sem(n) for n in ("froot_ready", "frstd_ready", "fshift_ready", "fnormed", "fgained", "out_stored"))
        finished = [sem(f"finished{t}") for t in range(TT)]
        gained_pool = sem("fgained_pool")
        POOLED = TT - 1
        with nc.Block() as block:
            @block.sync
            def _(sp):
                sp.dma_start(gain[0:1, 0, :], ln_g).then_inc(rows_here, 16)
                sp.dma_start(gain[0:1, 1, :], ln_b).then_inc(rows_here, 16)
                for t in range(TT):
                    sp.wait_ge(finished[t], 1)
                    sp.dma_start(out[0, t * P:(t + 1) * P, :], res[:, t, :]).then_inc(out_stored, 16)
                sp.wait_ge(out_stored, 16 * TT)

            @block.tensor
            def _(pe):
                pe.wait_ge(rows_here, 32)
                for j in range(8):
                    last = pe.matmul(banks[j][:], k.ones[0:1, :], gain[0:1, j // 4, (j % 4) * PW:(j % 4 + 1) * PW], start=True, stop=True)
                last.then_inc(gain_ready, 1)

            @block.gpsimd
            def _(pool):
                for t in range(TT):
                    for n in range(2):
                        pool.indirect_dma_start(out=y[n][:, t, :], out_offset=None, in_=scr.yb,
                                                in_offset=bass.IndirectOffsetOnAxis(ap=keep.slot_i[:, n, t:t + 1], axis=0)).then_inc(y_here[n][t], 16)
                pool.wait_ge(gain_out, 8)
                for t in range(POOLED):
                    pool.wait_ge(normed, t + 1)
                    pool.tensor_tensor(res[:, t, :], res[:, t, :], gain[:, 0, :], ALU.mult).then_inc(gained_pool, 1)
                    pool.wait_ge(gained_pool, t + 1)
                    pool.tensor_tensor(res[:, t, :], res[:, t, :], gain[:, 1, :], ALU.add).then_inc(finished[t], 1)

            @block.scalar
            def _(act):
                for t in range(TT):
                    if t == 1:
                        act.wait_ge(gain_ready, 1)
                        for j in range(8):
                            act.activation(gain[:, j // 4, (j % 4) * PW:(j % 4 + 1) * PW], banks[j][:], ACT.Copy).then_inc(gain_out, 1)
                    act.wait_ge(var_ready, t + 1)
                    act.activation(rstd[:, t:t + 1], rstd[:, t:t + 1], ACT.Sqrt).then_inc(root_ready, 1)
                    act.wait_ge(shift_ready, t + 1)
                    act.activation(res[:, t, :], res[:, t, :], ACT.Identity, bias=shift[:, t:t + 1], scale=rstd[:, t:t + 1]).then_inc(normed, 1)

            @block.vector
            def _(dve):
                for t in range(TT):
                    dve.wait_ge(y_here[0][t], 16)
                    dve.scalar_tensor_tensor(out=res[:, t, :], in0=y[0][:, t, :], scalar=keep.gate[:, 0, t:t + 1], in1=res[:, t, :],
                                             op0=ALU.mult, op1=ALU.add).then_inc(first_added, 1)
                    dve.wait_ge(first_added, t + 1)
                    dve.wait_ge(y_here[1][t], 16)
                    dve.scalar_tensor_tensor(out=res[:, t, :], in0=y[1][:, t, :], scalar=keep.gate[:, 1, t:t + 1], in1=res[:, t, :],
                                             op0=ALU.mult, op1=ALU.add).then_inc(summed, 1)
                    dve.wait_ge(summed, t + 1)
                    for j in range(D // PW):
                        dve.bn_stats(stats[:, t, j, :], res[:, t, j * PW:(j + 1) * PW]).then_inc(stat_ready, 1)
                    dve.wait_ge(stat_ready, (D // PW) * (t + 1))
                    dve.bn_aggr(mv[:, t, :], stats[:, t, :, :].rearrange("p a b -> p (a b)")).then_inc(mv_ready, 1)
                    dve.wait_ge(mv_ready, t + 1)
                    dve.tensor_scalar(rstd[:, t:t + 1], mv[:, t, 1:2], EPS, None, ALU.add).then_inc(var_ready, 1)
                    dve.wait_ge(root_ready, t + 1)
                    dve.reciprocal(rstd[:, t:t + 1], rstd[:, t:t + 1]).then_inc(rstd_ready, 1)
                    dve.wait_ge(rstd_ready, t + 1)
                    dve.scalar_tensor_tensor(out=shift[:, t:t + 1], in0=mv[:, t, 0:1], scalar=-1.0, in1=rstd[:, t:t + 1],
                                             op0=ALU.mult, op1=ALU.mult).then_inc(shift_ready, 1)
                dve.wait_ge(gain_out, 8)
                dve.wait_ge(normed, TT)
                dve.tensor_tensor(res[:, TT - 1, :], res[:, TT - 1, :], gain[:, 0, :], ALU.mult).then_inc(gained, 1)
                dve.wait_ge(gained, 1)
                last = res[:, TT - 1, :]
                dve.tensor_tensor(last, last, gain[:, 1, :], ALU.add).then_inc(finished[TT - 1], 1)


def decoder_layer(nc, x, p, w_in, conv_w, conv_b, dt_bias, a_log, d_skip, ssm_norm_w, idx_k_norm_g, idx_k_norm_b, w_out,
                  ln1_g, ln1_b, router_w, router_b, w_gate, w_up, w_down, ple_w, ple_gate_w, ln2_g, ln2_b, out):
    scr, k, keep = Shared(), Shared(), Shared()

    def scratch(name, shape):
        return nc.dram_tensor(f"scratch_{name}", shape, FP32).ap()

    scr.qkT, scr.iqT, scr.v = scratch("qkT", [2 * AH * AD, SEQ]), scratch("iqT", [IH * ID, SEQ]), scratch("v", [SEQ, AH * AD])
    scr.zT, scr.xbcT = scratch("zT", [SSD_W, SEQ]), scratch("xbcT", [CONV_DIM, SEQ])
    scr.dt, scr.attT = scratch("dt", [SEQ, HEADS]), scratch("attT", [AH * AD, SEQ])
    scr.h1 = scratch("h1", [SEQ, D])
    scr.yb = scratch("yb", [BLOCKS * CAP, D])
    with ExitStack() as ctx:
        def sb(name, shape, dt=FP32):
            return ctx.enter_context(nc.sbuf_tensor(name, shape, dt))

        def allocate(stack, name, shape, dt=FP32):
            return stack.enter_context(nc.sbuf_tensor(name, shape, dt))

        taken = []

        def semaphore(name):
            taken.append(nc.alloc_semaphore(name=name))
            return taken[-1]

        def clear_semaphores():
            nc.clear_and_free_semaphores(taken)
            nc.all_engine_barrier()
            taken.clear()

        k.semaphore = semaphore
        k.ones, k.ident, k.strict, k.upto = sb("ones", [P, P]), sb("ident", [P, P]), sb("strict", [P, P]), sb("upto", [P, P])
        keep.gate, keep.slot_i = sb("gate", [P, 2, TT]), sb("slot_i", [P, 2, TT], I32)
        keep.over_info, keep.slot_token = sb("over_info", [1, 1 + MAX_OVER], I32), sb("slot_token", [CAP, BLOCKS], I32)
        k.par, k.head = sb("par", [P, N_PAR]), sb("head", [P, 2 * HEADS])
        with ExitStack() as own:
            k.causal_bias = own.enter_context(nc.sbuf_tensor("causal_bias", [P, SEQ], FP32))
            run_constants(nc, k)
            run_projection(nc, k, x, w_in, idx_k_norm_g, idx_k_norm_b, conv_w, conv_b, dt_bias, a_log, d_skip, ssm_norm_w, scr)
        keep.gain, keep.turned_gain = sb("gain", [P, 2, D]), sb("turned_gain", [P, 2 * DK])
        keep.h, keep.pT = sb("h", [P, TT, D]), sb("pT", [P, KP, SEQ])

        with ExitStack() as early:
            keep.raw = allocate(early, "oraw", [P, CH, KC, PW])
            run_ssd(nc, k, p, w_out, ln1_g, ln1_b, scr, keep)
            keep.yhi, keep.ylo = (allocate(early, n, [P, DK, SEQ], FP32R) for n in ("yhi", "ylo"))
            keep.whi, keep.wlo = ([allocate(early, f"{n}{i}", [P, KC, PW], FP32R) for i in range(SPLIT_SLOTS)] for n in ("owhi", "owlo"))
        clear_semaphores()
        with ExitStack() as own:
            keep.dn = [allocate(own, f"dn{j}", [P, FT, DN_W]) for j in range(DN_CHUNKS)]
            keep.hT = allocate(own, "hT", [P, DK, SEQ])
            keep.gu = [allocate(own, f"gu{j}", [P, 2, KG, D_FF]) for j in range(GU_CHUNKS)]
            keep.gu_here = [semaphore(f"gu_here{j}") for j in range(GU_CHUNKS)]
            keep.dn_here = [semaphore(f"dn_here{j}") for j in range(DN_CHUNKS)]
            run_output(nc, k, x, w_out, router_w, router_b, w_gate, w_up, w_down, scr, keep)
            run_moe(nc, k, w_gate, w_up, w_down, ple_w, ple_gate_w, scr, keep)
        clear_semaphores()
        run_result(nc, k, ln2_g, ln2_b, scr, keep, out)


INPUTS = ["x", "p", "w_in", "conv_w", "conv_b", "dt_bias", "a_log", "d_skip", "ssm_norm_w", "idx_k_norm_g", "idx_k_norm_b",
          "w_out", "ln1_g", "ln1_b", "router_w", "router_b", "w_gate", "w_up", "w_down", "ple_w", "ple_gate_w", "ln2_g", "ln2_b"]


def kernel(**inputs):
    import numpy as np
    import concourse.bacc as bacc
    from concourse.bass_utils import run_bass_kernel_spmd

    nc = bacc.Bacc("TRN2", target_bir_lowering=False, num_devices=1)
    arrays, args = {}, []
    for name in INPUTS:
        a = np.ascontiguousarray(inputs[name])
        arrays[f"in_{name}"] = a
        args.append(nc.dram_tensor(f"in_{name}", a.shape, mybir.dt.from_np(a.dtype), kind="ExternalInput").ap())
    args.append(nc.dram_tensor("result", (1, SEQ, D), FP32, kind="ExternalOutput").ap())
    decoder_layer(nc, *args)
    r = run_bass_kernel_spmd(nc, [arrays], core_ids=[0])
    return r.results[0]["result"]
```
